# Optimizing a Trainium2 kernel written in Bass

```python
import math
import jax, jax.numpy as jnp
from jax import lax
import numpy as np

D_MODEL = 1024
BATCH = 1
SEQ = 1024
DEPTH = 1

HEAD_DIM = 64
N_HEADS_A = 8
N_HEADS_B = 8
N_HEADS = N_HEADS_A + N_HEADS_B
D_MIX = N_HEADS * HEAD_DIM
D_A = N_HEADS_A * HEAD_DIM
D_B = N_HEADS_B * HEAD_DIM
KV_RANK_A = 128
N_KV_A = 2
R_A = N_HEADS_A // N_KV_A
N_IDX_HEADS = 8
IDX_DIM = 64
TOPK_A = 256
N_KV_B = 2
R_B = N_HEADS_B // N_KV_B
D_KV_B = N_KV_B * HEAD_DIM
CMP_BLOCK = 32
CMP_STRIDE = 16
SLC_BLOCK = 64
N_SLC = 16
WINDOW = 512
N_BUCKETS = 32
MAX_DISTANCE = 1024
Q_BLOCK_A = 128
Q_BLOCK_B = 64
EPS = 1e-6
NEG_INF = -1e30
FORCE_BONUS = 1e4
ATTN_SCALE = HEAD_DIM ** -0.5
IDX_SCALE = IDX_DIM ** -0.5
IDX_W_SCALE = N_IDX_HEADS ** -0.5

PROJ_SIZES = (
    D_A, KV_RANK_A, N_IDX_HEADS * IDX_DIM, IDX_DIM, N_IDX_HEADS, D_A,
    D_B, D_KV_B, D_KV_B, D_KV_B, D_KV_B, D_KV_B, D_KV_B, N_HEADS_B * 3, D_B,
)
D_IN = sum(PROJ_SIZES)
PROJ_SPLITS = tuple(int(v) for v in np.cumsum(PROJ_SIZES)[:-1])

kernel_name = 'hybrid_dsa_nsa_parallel_heads'

def rms_norm(x, g):
    xf = x.astype(jnp.float32)
    y = xf * lax.rsqrt(jnp.mean(xf * xf, axis=-1, keepdims=True) + EPS)
    return (y * g.astype(jnp.float32)).astype(x.dtype)

def masked_softmax(logits, mask):
    p = jax.nn.softmax(jnp.where(mask, logits, NEG_INF), axis=-1)
    return jnp.where(mask, p, 0.0)

def t5_bucket(dist):
    n = jnp.maximum(dist, 0)
    max_exact = N_BUCKETS // 2
    nf = jnp.maximum(n, 1).astype(jnp.float32)
    log_b = max_exact + (jnp.log(nf / max_exact) / math.log(MAX_DISTANCE / max_exact)
                         * (N_BUCKETS - max_exact)).astype(jnp.int32)
    return jnp.where(n < max_exact, n, jnp.minimum(log_b, N_BUCKETS - 1))

def band_bias(bias_b, dist):
    return bias_b[t5_bucket(dist)].transpose(0, 2, 3, 1)[None].astype(jnp.float32)

def overlap_map(n_c, n_sb):
    c_start = np.arange(n_c)[:, None] * CMP_STRIDE
    b_start = np.arange(n_sb)[None, :] * SLC_BLOCK
    ov = np.minimum(c_start + CMP_BLOCK, b_start + SLC_BLOCK) - np.maximum(c_start, b_start)
    return (np.maximum(ov, 0) / CMP_BLOCK).astype(np.float32)

def compress(k, pos_emb, w1, w2):
    B, L = k.shape[:2]
    n_c = (L - CMP_BLOCK) // CMP_STRIDE + 1
    idx = np.arange(n_c)[:, None] * CMP_STRIDE + np.arange(CMP_BLOCK)[None, :]
    blocks = k[:, idx] + pos_emb[None, None, :, None, :]
    blocks = blocks.transpose(0, 1, 3, 2, 4).reshape(B, n_c, N_KV_B, CMP_BLOCK * HEAD_DIM)
    return jax.nn.gelu(blocks @ w1) @ w2

def dsa_attention(q, k, v, q_idx, k_idx, w_idx, bias_a):
    B, L = q.shape[:2]
    k_top = min(TOPK_A, L // 4)
    n_qb = L // Q_BLOCK_A
    s_pos = jnp.arange(L)
    b_idx = jnp.arange(B)[:, None, None]

    def block(i):
        q0 = i * Q_BLOCK_A
        t = q0 + jnp.arange(Q_BLOCK_A)
        qa = lax.dynamic_slice_in_dim(q, q0, Q_BLOCK_A, axis=1).reshape(B, Q_BLOCK_A, N_KV_A, R_A, HEAD_DIM)
        qi = lax.dynamic_slice_in_dim(q_idx, q0, Q_BLOCK_A, axis=1)
        wi = lax.dynamic_slice_in_dim(w_idx, q0, Q_BLOCK_A, axis=1).astype(jnp.float32) * IDX_W_SCALE
        dots = jnp.einsum('bqhd,bsd->bqhs', qi, k_idx).astype(jnp.float32) * IDX_SCALE
        score = jnp.einsum('bqh,bqhs->bqs', wi, jax.nn.relu(dots))
        score = jnp.where((s_pos[None, :] <= t[:, None])[None], score, NEG_INF)
        _, sel = lax.top_k(score, k_top)
        k_sel = k[b_idx, sel]
        v_sel = v[b_idx, sel]
        dist = t[None, :, None] - sel
        logits = jnp.einsum('bqgrd,bqkgd->bqgrk', qa, k_sel).astype(jnp.float32) * ATTN_SCALE
        bias = bias_a[t5_bucket(dist)].reshape(B, Q_BLOCK_A, k_top, N_KV_A, R_A).transpose(0, 1, 3, 4, 2)
        p = masked_softmax(logits + bias.astype(jnp.float32), (dist >= 0)[:, :, None, None, :])
        o = jnp.einsum('bqgrk,bqkgd->bqgrd', p.astype(v_sel.dtype), v_sel)
        return o.reshape(B, Q_BLOCK_A, D_A)

    out = lax.map(block, jnp.arange(n_qb))
    return out.transpose(1, 0, 2, 3).reshape(B, L, D_A)

def nsa_attention(q, k_c, v_c, k_s, v_s, k_w, v_w, gates, bias_b):
    B, L = q.shape[:2]
    n_c = k_c.shape[1]
    n_sb = L // SLC_BLOCK
    n_sel = min(N_SLC, n_sb)
    n_qb = L // Q_BLOCK_B
    end_c = jnp.asarray(np.arange(n_c) * CMP_STRIDE + CMP_BLOCK - 1)
    slc_map = jnp.asarray(overlap_map(n_c, n_sb))
    blk = jnp.arange(n_sb)
    ks_blk = k_s.reshape(B, n_sb, SLC_BLOCK, N_KV_B, HEAD_DIM).transpose(0, 3, 1, 2, 4)
    vs_blk = v_s.reshape(B, n_sb, SLC_BLOCK, N_KV_B, HEAD_DIM).transpose(0, 3, 1, 2, 4)
    pad = ((0, 0), (WINDOW, 0), (0, 0), (0, 0))
    kw_pad = jnp.pad(k_w, pad)
    vw_pad = jnp.pad(v_w, pad)
    b_i = jnp.arange(B)[:, None, None, None]
    g_i = jnp.arange(N_KV_B)[None, None, :, None]
    in_blk = jnp.arange(SLC_BLOCK)
    n_tok = n_sel * SLC_BLOCK

    def block(i):
        q0 = i * Q_BLOCK_B
        t = q0 + jnp.arange(Q_BLOCK_B)
        qb = lax.dynamic_slice_in_dim(q, q0, Q_BLOCK_B, axis=1).reshape(B, Q_BLOCK_B, N_KV_B, R_B, HEAD_DIM)
        gb = lax.dynamic_slice_in_dim(gates, q0, Q_BLOCK_B, axis=1).reshape(B, Q_BLOCK_B, N_KV_B, R_B, 3)
        dist_c = t[:, None] - end_c[None, :]
        logits_c = jnp.einsum('bqgrd,bcgd->bqgrc', qb, k_c).astype(jnp.float32) * ATTN_SCALE
        p_c = masked_softmax(logits_c + band_bias(bias_b, dist_c), (dist_c >= 0)[None, :, None, None, :])
        o_c = jnp.einsum('bqgrc,bcgd->bqgrd', p_c.astype(v_c.dtype), v_c)
        imp = jnp.einsum('bqgrc,cn->bqgn', p_c, slc_map)
        jt = t // SLC_BLOCK
        forced = (blk[None, :] == 0) | (blk[None, :] == jt[:, None]) | (blk[None, :] == jt[:, None] - 1)
        imp = imp + jnp.where(forced, FORCE_BONUS, 0.0)[None, :, None, :]
        imp = jnp.where((blk[None, :] * SLC_BLOCK <= t[:, None])[None, :, None, :], imp, NEG_INF)
        _, sel = lax.top_k(imp, n_sel)
        k_sel = ks_blk[b_i, g_i, sel].reshape(B, Q_BLOCK_B, N_KV_B, n_tok, HEAD_DIM)
        v_sel = vs_blk[b_i, g_i, sel].reshape(B, Q_BLOCK_B, N_KV_B, n_tok, HEAD_DIM)
        pos = (sel[..., None] * SLC_BLOCK + in_blk).reshape(B, Q_BLOCK_B, N_KV_B, n_tok)
        dist_s = t[None, :, None, None] - pos
        logits_s = jnp.einsum('bqgrd,bqgnd->bqgrn', qb, k_sel).astype(jnp.float32) * ATTN_SCALE
        bias_s = bias_b[t5_bucket(dist_s), g_i].transpose(0, 1, 2, 4, 3)
        p_s = masked_softmax(logits_s + bias_s.astype(jnp.float32), (dist_s >= 0)[:, :, :, None, :])
        o_s = jnp.einsum('bqgrn,bqgnd->bqgrd', p_s.astype(v_sel.dtype), v_sel)
        s = q0 - WINDOW + jnp.arange(WINDOW + Q_BLOCK_B)
        kw = lax.dynamic_slice_in_dim(kw_pad, q0, WINDOW + Q_BLOCK_B, axis=1)
        vw = lax.dynamic_slice_in_dim(vw_pad, q0, WINDOW + Q_BLOCK_B, axis=1)
        dist_w = t[:, None] - s[None, :]
        mask_w = (dist_w >= 0) & (dist_w < WINDOW) & (s[None, :] >= 0)
        logits_w = jnp.einsum('bqgrd,bsgd->bqgrs', qb, kw).astype(jnp.float32) * ATTN_SCALE
        p_w = masked_softmax(logits_w + band_bias(bias_b, dist_w), mask_w[None, :, None, None, :])
        o_w = jnp.einsum('bqgrs,bsgd->bqgrd', p_w.astype(vw.dtype), vw)
        o = gb[..., 0:1] * o_c + gb[..., 1:2] * o_s + gb[..., 2:3] * o_w
        return o.reshape(B, Q_BLOCK_B, D_B)

    out = lax.map(block, jnp.arange(n_qb))
    return out.transpose(1, 0, 2, 3).reshape(B, L, D_B)

def setup_inputs(seed: int = 0) -> dict:
    key = jax.random.key(seed)
    ks = jax.random.split(key, 24)
    f32 = jnp.float32

    def nrm(k, shape, scale):
        return jax.random.normal(k, shape, f32) * scale

    def gain(k, shape):
        return 1.0 + 0.01 * jax.random.normal(k, shape, f32)

    return {
        'x': nrm(ks[0], (BATCH, SEQ, D_MODEL), 1.0),
        'rel_bias': nrm(ks[1], (N_BUCKETS, N_HEADS), 0.5),
        'norm_g': gain(ks[2], (DEPTH, D_MODEL)),
        'w_in': nrm(ks[3], (DEPTH, D_MODEL, D_IN), D_MODEL ** -0.5),
        'b_gate_b': nrm(ks[4], (DEPTH, N_HEADS_B * 3), 0.1),
        'kv_norm_a': gain(ks[5], (DEPTH, KV_RANK_A)),
        'w_kv_up_a': nrm(ks[6], (DEPTH, KV_RANK_A, 2 * N_KV_A * HEAD_DIM), KV_RANK_A ** -0.5),
        'q_norm_a': gain(ks[7], (DEPTH, HEAD_DIM)),
        'k_norm_a': gain(ks[8], (DEPTH, HEAD_DIM)),
        'q_norm_b': gain(ks[9], (DEPTH, HEAD_DIM)),
        'k_norm_cmp': gain(ks[10], (DEPTH, HEAD_DIM)),
        'k_norm_slc': gain(ks[11], (DEPTH, HEAD_DIM)),
        'k_norm_win': gain(ks[12], (DEPTH, HEAD_DIM)),
        'cmp_pos_k': nrm(ks[13], (DEPTH, CMP_BLOCK, HEAD_DIM), 0.2),
        'cmp_pos_v': nrm(ks[14], (DEPTH, CMP_BLOCK, HEAD_DIM), 0.2),
        'w_cmp_k1': nrm(ks[15], (DEPTH, CMP_BLOCK * HEAD_DIM, HEAD_DIM), (CMP_BLOCK * HEAD_DIM) ** -0.5),
        'w_cmp_k2': nrm(ks[16], (DEPTH, HEAD_DIM, HEAD_DIM), HEAD_DIM ** -0.5),
        'w_cmp_v1': nrm(ks[17], (DEPTH, CMP_BLOCK * HEAD_DIM, HEAD_DIM), (CMP_BLOCK * HEAD_DIM) ** -0.5),
        'w_cmp_v2': nrm(ks[18], (DEPTH, HEAD_DIM, HEAD_DIM), HEAD_DIM ** -0.5),
        'w_out': nrm(ks[19], (DEPTH, D_MIX, D_MODEL), D_MIX ** -0.5),
    }

def reference(x, rel_bias, norm_g, w_in, b_gate_b, kv_norm_a, w_kv_up_a, q_norm_a, k_norm_a,
              q_norm_b, k_norm_cmp, k_norm_slc, k_norm_win, cmp_pos_k, cmp_pos_v,
              w_cmp_k1, w_cmp_k2, w_cmp_v1, w_cmp_v2, w_out):
    B, L, _ = x.shape
    bias_a = rel_bias[:, :N_HEADS_A]
    bias_b = rel_bias[:, N_HEADS_A:].reshape(N_BUCKETS, N_KV_B, R_B)
    kv_shape = (B, L, N_KV_B, HEAD_DIM)
    for l in range(DEPTH):
        h = rms_norm(x, norm_g[l])
        proj = h @ w_in[l]
        (q_a, c_kv, q_idx, k_idx, w_idx, z_a,
         q_b, k_cmp, v_cmp, k_slc, v_slc, k_win, v_win, g_b, z_b) = jnp.split(proj, PROJ_SPLITS, axis=-1)
        q_a = rms_norm(q_a.reshape(B, L, N_HEADS_A, HEAD_DIM), q_norm_a[l])
        kv_a = (rms_norm(c_kv, kv_norm_a[l]) @ w_kv_up_a[l]).reshape(B, L, 2 * N_KV_A, HEAD_DIM)
        k_a, v_a = jnp.split(kv_a, 2, axis=2)
        k_a = rms_norm(k_a, k_norm_a[l])
        o_a = dsa_attention(q_a, k_a, v_a, q_idx.reshape(B, L, N_IDX_HEADS, IDX_DIM), k_idx, w_idx, bias_a)
        q_b = rms_norm(q_b.reshape(B, L, N_HEADS_B, HEAD_DIM), q_norm_b[l])
        k_c = rms_norm(compress(k_cmp.reshape(kv_shape), cmp_pos_k[l], w_cmp_k1[l], w_cmp_k2[l]), k_norm_cmp[l])
        v_c = compress(v_cmp.reshape(kv_shape), cmp_pos_v[l], w_cmp_v1[l], w_cmp_v2[l])
        k_s = rms_norm(k_slc.reshape(kv_shape), k_norm_slc[l])
        k_w = rms_norm(k_win.reshape(kv_shape), k_norm_win[l])
        gates = jax.nn.sigmoid((g_b + b_gate_b[l]).astype(jnp.float32)).astype(x.dtype).reshape(B, L, N_HEADS_B, 3)
        o_b = nsa_attention(q_b, k_c, v_c, k_s, v_slc.reshape(kv_shape), k_w, v_win.reshape(kv_shape), gates, bias_b)
        y = jnp.concatenate([o_a * jax.nn.silu(z_a), o_b * jax.nn.silu(z_b)], axis=-1)
        x = x + y @ w_out[l]
    return x


_drawn_inputs = setup_inputs


def setup_inputs(seed=0):
    import zlib

    import numpy as np

    out = dict(_drawn_inputs(seed))
    spreads = {}
    factors = {'norm_g': 8.0,
     'b_gate_b': 8.0,
     'kv_norm_a': 8.0,
     'q_norm_a': 8.0,
     'k_norm_a': 8.0,
     'q_norm_b': 8.0,
     'k_norm_cmp': 28.185,
     'k_norm_slc': 8.0,
     'k_norm_win': 8.0,
     'cmp_pos_k': 8.0,
     'cmp_pos_v': 6.607}
    for name, (base, spread) in spreads.items():
        noise = np.random.default_rng([zlib.crc32(name.encode()), seed]).standard_normal(out[name].shape)
        drawn = base * np.exp(spread * noise) if base else spread * noise
        out[name] = __import__('jax').numpy.asarray(drawn.astype(out[name].dtype))
    for name, factor in factors.items():
        out[name] = (out[name] * factor).astype(out[name].dtype)
    return out
```

```python
import math
from contextlib import ExitStack

import numpy as np
import concourse.bass as bass
from concourse import mybir

F32 = mybir.dt.float32
BF16 = mybir.dt.bfloat16
I32 = mybir.dt.int32
ALU = mybir.AluOpType
ACT = mybir.ActivationFunctionType
AX = mybir.AxisListType

P = 128
D = 1024
L = 1024
NT = L // P
KT = D // P
HD = 64
NH = 8
NG = 2
TOPK = 256
T_SEL = TOPK // P
SEL_TILES = range(T_SEL, NT)
N_SEL = NT - T_SEL
WIN = 512
WB = WIN // P
CMP_BLOCK, CMP_STRIDE = 32, 16
N_C = (L - CMP_BLOCK) // CMP_STRIDE + 1
N_BUCKETS, MAX_DISTANCE = 32, 1024
EPS = 1e-6
NEG = -1e30
BANK = 512

C_QA, C_CKV, C_QI, C_KI, C_WI, C_ZA = 0, 512, 640, 1152, 1216, 1224
C_QB, C_KC, C_KS, C_GB, C_ZB, C_END = 1736, 2248, 2504, 3016, 3040, 3552

LINE = L + P - 1
REP = 32
CM = 2 * 63
CLINE = CMP_STRIDE * CM
CY = N_C + (NT - 1) * (P // CMP_STRIDE)

SEL_W = [P * (i + 1) for i in SEL_TILES]
SEL_OFF = [sum(SEL_W[:n]) for n in range(N_SEL + 1)]
SEL_TOT = SEL_OFF[-1]
N_BITS = 31


def t5_bucket(dist):
    n = np.maximum(dist, 0)
    exact = N_BUCKETS // 2
    nf = np.maximum(n, 1).astype(np.float32)
    log_b = exact + (np.log(nf / np.float32(exact)) / np.float32(math.log(MAX_DISTANCE / exact))
                     * np.float32(N_BUCKETS - exact)).astype(np.int32)
    return np.where(n < exact, n, np.minimum(log_b, N_BUCKETS - 1))


def one_hot(dist):
    out = np.zeros((N_BUCKETS + 1, dist.size), np.float32)
    row = np.where(dist < 0, N_BUCKETS, t5_bucket(dist))
    out[row, np.arange(dist.size)] = 1.0
    return out


def shape_constants():
    v = np.arange(LINE)
    q, m = np.meshgrid(np.arange(CMP_STRIDE), np.arange(CM), indexing="ij")
    p = np.arange(P)
    eye = np.eye(P, dtype=np.float32)
    return {
        "c_line": one_hot(L - 1 - v),
        "c_cline": one_hot((q - (CMP_BLOCK - 1) + CMP_STRIDE * (63 - m)).ravel()),
        "c_eye": eye,
        "c_bits": np.tile((2.0 ** np.arange(N_BITS - 1, -1, -1, dtype=np.float32))[None], (P, 1)),
        "c_bitsi": np.tile((1 << np.arange(N_BITS - 1, -1, -1)).astype(np.int32)[None], (P, 1)),
        "c_rows": (p[:, None] + P * np.array(SEL_TILES)[None] + 2 - 2 * TOPK).astype(np.float32),
        "c_seen": (p >= CMP_BLOCK - 1).astype(np.float32)[:, None],
    }


def hybrid_layer(nc, x, rel_bias, norm_g, w_in, b_gate_b, kv_norm_a, w_kv_up_a, q_norm_a, k_norm_a, q_norm_b,
                 k_norm_cmp, k_norm_slc, k_norm_win, cmp_pos_k, cmp_pos_v, w_cmp_k1, w_cmp_k2, w_cmp_v1,
                 w_cmp_v2, w_out, c_line, c_cline, c_eye, c_bits, c_bitsi, c_rows, c_seen, out):
    ctx = ExitStack()
    with ctx:
        def sb(name, shape, dt=F32):
            return ctx.enter_context(nc.sbuf_tensor(name, shape, dt))

        def sem(name):
            return ctx.enter_context(nc.semaphore(name))

        line_dram = nc.dram_tensor("line_dram", (2 * NH, REP, LINE), F32, kind="Internal").ap()
        cline_dram = nc.dram_tensor("cline_dram", (NH, CLINE), F32, kind="Internal").ap()

        r_big = sb("r_big", [P, 16384])
        hT = r_big[:, 0:8192].rearrange("p (k t) -> p k t", k=KT)
        wbuf = r_big[:, 8192:16384].rearrange("p (b k c) -> p b k c", b=2, k=KT)
        strip_a = r_big[:, 0:8192].rearrange("p (h x) -> p h x", h=NH)
        strip_b = r_big[:, 8192:16384].rearrange("p (h x) -> p h x", h=NH)
        x_res = strip_b

        r_z = sb("r_z", [P, 8192])
        x_in = r_z[:, :].rearrange("p (t c) -> p t c", t=NT)
        z = x_in
        qiT = r_z[:, 0:4096].rearrange("p (m t) -> p m t", m=NH // 2)
        kiT = r_z[:, 4096:5120]
        relu = r_z[:, 5120:7168].rearrange("p (b c) -> p b c", b=2)
        kcT_raw = r_z[:, 5120:7168].rearrange("p (b t) -> p b t", b=2)

        r_qk = sb("r_qk", [P, 14336])
        qaT = r_qk[:, 0:4096].rearrange("p (m t) -> p m t", m=NH // 2)
        kaT = r_qk[:, 4096:6144].rearrange("p (g t) -> p g t", g=NG)
        qbT = r_qk[:, 6144:10240].rearrange("p (m t) -> p m t", m=NH // 2)
        ksT = r_qk[:, 10240:12288].rearrange("p (g t) -> p g t", g=NG)
        kwT = r_qk[:, 12288:14336].rearrange("p (g t) -> p g t", g=NG)
        wout = r_qk[:, 6144:14336].rearrange("p (k c) -> p k c", k=KT)
        ckv = r_qk[:, 0:1024].rearrange("p (t c) -> p t c", t=NT)
        ckvT = r_qk[:, 1024:2048]
        square = [r_qk[:, 6144 + 1024 * n:7168 + 1024 * n] for n in range(2)]

        va = sb("va", [P, NT, NG * HD])
        vs = sb("vs", [P, NT, NG * HD])
        vw = sb("vw", [P, NT, NG * HD])

        selmask = sb("selmask", [P, SEL_TOT], BF16)
        r_y = sb("r_y", [P, 2 * (LINE + CLINE)])
        oh = r_y[0:N_BUCKETS + 1, 0:LINE + CLINE]
        lines = r_y[0:2 * NH, LINE + CLINE:2 * (LINE + CLINE)]
        score = r_y[:, 0:SEL_TOT]
        tie = r_y[:, SEL_TOT:SEL_TOT + 512].bitcast(BF16)
        unsel = r_y[:, SEL_TOT + 512:SEL_TOT + 1024].bitcast(BF16)
        ties_to = r_y[:, SEL_TOT + 1024:SEL_TOT + 2048]
        mark = [tie, unsel]
        soft = r_y[:, 0:4096].rearrange("p (b c) -> p b c", b=4)
        probT = r_y[:, 4096:5632].rearrange("p (b c) -> p b c", b=3)
        head_o = r_y[:, 5632:6144]
        yT = r_y[:, 0:2048].rearrange("p (b k t) -> p b k t", b=2, k=KT)

        nat = sb("nat", [P, 3, BANK])
        strip_c = nat[:, 0:2, :].rearrange("p b c -> p (b c)")[:, 0:NH * CY].rearrange("p (h y) -> p h y", h=NH)
        o_acc = nat[:, 2, :]
        eye = sb("eye", [P, P])
        eyeb = r_y[:, 6144:6208].bitcast(BF16)
        winb = r_y[:, 6208:6272].bitcast(BF16)
        bits = sb("bits", [P, N_BITS])
        bitsi = sb("bitsi", [P, N_BITS], I32)
        small = sb("small", [P, 12 * N_SEL])
        rows = small[:, 0 * N_SEL:1 * N_SEL]
        seen = sb("seen", [P, 1])
        rel = sb("rel", [N_BUCKETS + 1, 2 * NH])
        gx = sb("gx", [P, KT])
        gain = sb("gain", [P, 7])
        G_QA, G_KA, G_QB, G_KC, G_KS, G_KW, G_CKV = range(7)
        wup = r_qk[:, 2048:2304]
        w2 = r_qk[0:HD, 2304:2432].rearrange("p (v c) -> p v c", v=2)
        posT = r_qk[:, 2432:2496].rearrange("p (v j) -> p v j", v=2)
        hid = r_qk[0:HD, 2496:2752].rearrange("p (v c) -> p v c", v=2 * NG)
        kc = r_qk[0:N_C, 2752:3008].rearrange("p (g two d) -> p g two d", g=NG, two=2)
        bgate = sb("bgate", [P, 3 * NH])
        gates = sb("gates", [P, NT, 3 * NH])
        widx = sb("widx", [P, NT, NH])
        minus_half = sb("minus_half", [P, 12])
        ssx = sb("ssx", [P, NT])
        ssq = sb("ssq", [P, 3, NH])
        junk = sb("junk", [P, 2, P], BF16)
        hid_c = sb("hid_c", [HD, 2])
        vc = sb("vc", [P, NG, 2, HD])
        kcT = sb("kcT", [P, NG, HD])
        cur = small[:, 1 * N_SEL:2 * N_SEL].bitcast(I32)
        cand = small[:, 2 * N_SEL:3 * N_SEL].bitcast(I32)
        cnt = small[:, 3 * N_SEL:4 * N_SEL]
        cnt2 = small[:, 4 * N_SEL:5 * N_SEL]
        keep = small[:, 5 * N_SEL:6 * N_SEL].bitcast(I32)
        ispos = small[:, 6 * N_SEL:7 * N_SEL]
        sgn = small[:, 7 * N_SEL:8 * N_SEL]
        kth = small[:, 8 * N_SEL:9 * N_SEL]
        nkth = small[:, 9 * N_SEL:10 * N_SEL]
        need = small[:, 10 * N_SEL:11 * N_SEL]
        thr = small[:, 11 * N_SEL:12 * N_SEL]
        nmax = sb("nmax", [P, 4, NH])
        rsum = sb("rsum", [P, 4, NH])
        rinv = sb("rinv", [P, NH])

        ps = ctx.enter_context(nc.psum_tensor("ps", [P, 8, BANK], F32))

        s_first = sem("s_first")
        s_const = sem("s_const")
        s_x = [sem(f"s_x{t}") for t in range(NT)]
        s_w = [sem(f"s_w{b}") for b in range(2)]
        s_line = sem("s_line")
        s_linesb = sem("s_linesb")
        s_lined = sem("s_lined")
        s_gp = sem("s_gp")
        s_sqx = sem("s_sqx")
        s_rx = sem("s_rx")
        s_h = sem("s_h")
        s_ht = sem("s_ht")
        s_hact = sem("s_hact")
        s_hdve = sem("s_hdve")
        s_pr = sem("s_pr")
        s_pre = sem("s_pre")
        s_sc = sem("s_sc")
        s_relu = sem("s_relu")
        s_acc = sem("s_acc")
        s_dv = sem("s_dv")
        s_mask = sem("s_mask")
        s_flip = sem("s_flip")
        s_sel = sem("s_sel")
        s_soft = sem("s_soft")
        s_nrm = sem("s_nrm")
        s_sqo = sem("s_sqo")
        s_tr = sem("s_tr")
        s_tre = sem("s_tre")
        s_cmp = sem("s_cmp")
        s_cme = sem("s_cme")
        s_masks = sem("s_masks")
        s_zero = sem("s_zero")
        s_gate = sem("s_gate")
        s_ncst = sem("s_ncst")
        B_PIECES = [(L - P, L), (L - 4 * P, L - P), (0, L - 4 * P)]
        A_PIECES = [(0, L)]
        s_bstrip = [sem(f"s_bstrip{n}") for n in range(len(B_PIECES))]
        s_astrip = [sem(f"s_astrip{n}") for n in range(len(A_PIECES))]
        s_cstrip = sem("s_cstrip")
        s_qk = sem("s_qk")
        s_lg = sem("s_lg")
        s_ex = sem("s_ex")
        s_t = sem("s_t")
        s_pta = sem("s_pta")
        s_ptd = sem("s_ptd")
        s_pv = sem("s_pv")
        s_oe = sem("s_oe")
        s_y = sem("s_y")
        s_wo = sem("s_wo")
        s_xr = sem("s_xr")
        s_yt = sem("s_yt")
        s_yta = sem("s_yta")
        s_ytd = sem("s_ytd")
        s_op = sem("s_op")
        s_oadd = sem("s_oadd")
        s_out = sem("s_out")

        CH_IDX, CH_SMALL, CH_KV, CH_KC, CH_W1, CH_QB, CH_QA, CH_ZA, CH_ZB = range(9)
        w_src = w_in[0].rearrange("(k p) c -> p k c", p=P)
        w1_src = [w.rearrange("a (j d) c -> d (a j) c", d=HD) for w in (w_cmp_k1, w_cmp_v1)]
        w1 = wbuf[:, CH_W1 % 2, :, :].rearrange("p k (f c) -> p (k f) c", f=4).rearrange(
            "p j c -> p (j c)").rearrange("p (v j c) -> p v j c", v=2, j=CMP_BLOCK)
        chunk_loads = {
            CH_IDX: [(0, C_QI, 512)],
            CH_SMALL: [(0, C_KI, 64), (64, C_KI, 64), (128, C_CKV, 128), (256, C_WI, 8), (264, C_GB, 24)],
            CH_KV: [(0, C_KS, 512)],
            CH_KC: [(0, C_KC, 256)],
            CH_QB: [(0, C_QB, 512)],
            CH_QA: [(0, C_QA, 512)],
            CH_ZA: [(0, C_ZA, 512)],
            CH_ZB: [(0, C_ZB, 512)],
        }
        chunk_count = {c: len(v) for c, v in chunk_loads.items()} | {CH_W1: 4}

        def chunk_arrived(c):
            return 16 * sum(chunk_count[n] for n in range(c % 2, c + 1, 2))

        units = []
        units += [("qiT", cb, half) for cb in range(4) for half in range(2)]
        units += [("kiT", 0, half) for half in range(2)]
        units += [("small", t, 0) for t in range(NT)]
        N_EARLY = len(units)
        units += [("kv", t, 0) for t in range(NT)]
        units += [("kcT", cb, half) for cb in range(2) for half in range(2)]
        units += [("up", t, 0) for t in range(NT)]
        units += [("qb", t, 0) for t in range(NT)]
        units += [("qa", t, 0) for t in range(NT)]
        units += [("za", t, 0) for t in range(NT)]
        units += [("zb", t, 0) for t in range(NT)]
        unit_no = {u: n for n, u in enumerate(units)}
        CHUNK_OF = {"qiT": CH_IDX, "kiT": CH_SMALL, "small": CH_SMALL, "kv": CH_KV, "kcT": CH_KC, "qb": CH_QB,
                    "qa": CH_QA, "za": CH_ZA, "zb": CH_ZB}

        norms = [("ckv", t) for t in range(NT)] + [("kv", t) for t in range(NT)] + [("kc", 0)]
        norms += [(kind, t) for kind in ("up", "qb", "qa") for t in range(NT)]
        norm_no = {u: n for n, u in enumerate(norms)}

        trs = [("ckvT", n) for n in range(2)] + [("kv", t) for t in range(NT)] + [("kc", 0)]
        trs += [("up", t) for t in range(NT)] + [("qb", t) for t in range(NT)] + [("qa", t) for t in range(NT)]
        tr_no = {u: n for n, u in enumerate(trs)}

        def last_unit(c):
            return max(n for n, u in enumerate(units) if CHUNK_OF.get(u[0]) == c)

        sjobs = [(i, h) for i in SEL_TILES for h in range(NH)]

        LAG = 2
        stage_order = [("unit", u) for u in range(N_EARLY)] + [("score", n) for n in range(len(sjobs))]
        stage_order += [("tr", 0), ("tr", 1)]
        waiting = []
        for u in range(N_EARLY, len(units)):
            stage_order.append(("unit", u))
            if units[u] == ("kcT", 1, 1):
                stage_order += [("tr", m) for _, m in waiting]
                waiting = []
                trs_before_cmp = sum(what == "tr" for what, _ in stage_order)
                stage_order.append(("compress", 0))
                waiting.append((u, tr_no[("kc", 0)]))
            while waiting and waiting[0][0] <= u - LAG:
                stage_order.append(("tr", waiting.pop(0)[1]))
            if units[u][:2] in tr_no:
                waiting.append((u, tr_no[units[u][:2]]))
        stage_order += [("tr", m) for _, m in waiting]
        assert [n for what, n in stage_order if what == "tr"] == list(range(len(trs)))

        jobs, sets = [], []
        for i in range(NT):
            for br in ("c", "s", "w"):
                sets += [(br, i, None)] if br == "c" else [(br, i, g) for g in range(NG)]
                jobs += [(br, i, h) for h in ([None] if br == "c" else range(NH))]
        for i in range(NT):
            sets += [("a", i, g) for g in range(NG)]
            jobs += [("a", i, h) for h in range(NH)]
        HG = NH // NG

        def set_of(job):
            return (job[0], job[1], None if job[0] == "c" else job[2] // HG)

        set_no = {s: n for n, s in enumerate(sets)}
        first_windowed = jobs.index(("w", WB, 0))
        FIRST_A = jobs.index(("a", 0, 0))

        def first_block(job):
            return max(0, job[1] - WB) if job[0] == "w" else 0

        blocks = []
        for n, job in enumerate(jobs):
            if job[0] == "c":
                blocks += [(n, m, 0) for m in range(NH // 2)]
            else:
                blocks += [(n, job[2], j) for j in range(first_block(job), job[1] + 1)]
        chunks = [blocks[n:n + 4] for n in range(0, len(blocks), 4)]
        last_chunk = {}
        for k, c in enumerate(chunks):
            for b in c:
                last_chunk[b[0]] = k
        chunk_dve = [k % 2 == 1 for k in range(len(chunks))]

        def pt_wait(eng, k):
            if chunk_dve[k]:
                eng.wait_ge(s_ptd, sum(chunk_dve[:k + 1]))
            else:
                eng.wait_ge(s_pta, k + 1 - sum(chunk_dve[:k + 1]))

        PV_LAG = 2
        events = []
        issued = 0
        for k, c in enumerate(chunks):
            while issued < len(jobs) and issued <= c[-1][0] + 2:
                events.append(("qk", issued))
                issued += 1
            events.append(("t", k))
            if k >= PV_LAG:
                events.append(("pv", k - PV_LAG))
        events += [("pv", k) for k in range(len(chunks) - PV_LAG, len(chunks))]

        def ends_set(n, pos):
            return pos + 1 == len(blocks) or set_of(jobs[blocks[pos + 1][0]]) != set_of(jobs[n])

        line_parts = [(2 * NH, c, min(BANK, LINE - c)) for c in range(0, LINE, BANK)]
        line_parts += [(NH, LINE + c, min(BANK, CLINE - c)) for c in range(0, CLINE, BANK)]
        N_LINE = len(line_parts)

        first_loads = [(oh[:, 0:LINE], c_line), (oh[:, LINE:LINE + CLINE], c_cline), (rel[0:N_BUCKETS, :], rel_bias),
                       (eye[:, :], c_eye)]
        const_loads = [(bits[:, :], c_bits), (bitsi[:, :], c_bitsi),
                       (rows[:, :], c_rows), (seen[:, :], c_seen), (wup, w_kv_up_a[0]),
                       (w2[:, 0, :], w_cmp_k2[0]), (w2[:, 1, :], w_cmp_v2[0]),
                       (gain[:, G_CKV:G_CKV + 1], kv_norm_a.rearrange("a p -> p a")),
                       (gx[:, :], norm_g.rearrange("a (k p) -> p (a k)", p=P)),
                       (bgate[:, :], bass.AP(tensor=b_gate_b.tensor, offset=0, ap=[[0, P], [1, 3 * NH]]))]
        for half in range(2):
            rows_h = slice(half * HD, (half + 1) * HD)
            const_loads += [(gain[rows_h, col:col + 1], g.rearrange("a p -> p a")) for col, g in (
                (G_QA, q_norm_a), (G_KA, k_norm_a), (G_QB, q_norm_b), (G_KC, k_norm_cmp), (G_KS, k_norm_slc),
                (G_KW, k_norm_win))]
            const_loads += [(posT[rows_h, v, :], pos[0].rearrange("j d -> d j"))
                            for v, pos in enumerate((cmp_pos_k, cmp_pos_v))]
        N_FIRST, N_CONST = len(first_loads), len(const_loads)

        block = ctx.enter_context(nc.Block())

        @block.sync
        def _(sp):
            for dst, src in first_loads:
                sp.dma_start(dst, src).then_inc(s_first, 16)
            for t in range(NT):
                sp.dma_start(x_in[:, t, :], x[0, t * P:(t + 1) * P, :]).then_inc(s_x[t], 16)

            def load_chunk(c):
                if c - 2 == CH_W1:
                    sp.wait_ge(s_cmp, 1)
                elif c >= 2:
                    sp.wait_ge(s_pr, last_unit(c - 2) + 1)
                if c == CH_W1:
                    for v in range(2):
                        for half in range(2):
                            sp.dma_start(w1[half * HD:(half + 1) * HD, v, :, :], w1_src[v]).then_inc(s_w[c % 2], 16)
                else:
                    for at, col, n in chunk_loads[c]:
                        sp.dma_start(wbuf[:, c % 2, :, at:at + n], w_src[:, :, col:col + n]).then_inc(s_w[c % 2], 16)

            for c in range(9):
                load_chunk(c)
                if c == 0:
                    with nc.allow_non_contiguous_dma(reason="small vectors, once"):
                        for dst, src in const_loads:
                            sp.dma_start(dst, src).then_inc(s_const, 16)
                if c == 1:
                    sp.wait_ge(s_linesb, N_LINE)
                    sp.dma_start(line_dram, lines[:, 0:LINE].unsqueeze(1).to_broadcast([2 * NH, REP, LINE]))\
                      .then_inc(s_lined, 16)
                    sp.dma_start(cline_dram, lines[0:NH, LINE:LINE + CLINE]).then_inc(s_lined, 16)
            sp.wait_ge(s_lined, 32)
            sp.wait_ge(s_tre, len(trs))
            for pb in range(P // CMP_STRIDE):
                src = bass.AP(tensor=cline_dram.tensor, offset=7 - pb, ap=[[CM, CMP_STRIDE], [CLINE, NH], [1, CY]])
                sp.dma_start(strip_c[pb * CMP_STRIDE:(pb + 1) * CMP_STRIDE, :, :], src).then_inc(s_cstrip, 16)
            sp.wait_ge(s_pr, len(units))
            for strip, pieces, h0 in ((strip_b, B_PIECES, NH), (strip_a, A_PIECES, 0)):
                for n, (c0, c1) in enumerate(pieces):
                    for b in range(P // REP):
                        src = bass.AP(tensor=line_dram.tensor, offset=h0 * REP * LINE + P - 1 - REP * b + c0,
                                      ap=[[LINE - 1, REP], [REP * LINE, NH], [1, c1 - c0]])
                        sp.dma_start(strip[b * REP:(b + 1) * REP, :, c0:c1], src)\
                          .then_inc((s_bstrip if h0 else s_astrip)[n], 16)
            sp.wait_ge(s_qk, FIRST_A)
            sp.dma_start(wout[:, :, :], w_out[0].rearrange("(k p) c -> p k c", p=P)).then_inc(s_wo, 16)
            sp.wait_ge(s_lg, FIRST_A)
            sp.dma_start(x_res[:, :, :], x[0].rearrange("(t p) c -> p t c", p=P)).then_inc(s_xr, 16)
            for t in range(NT):
                sp.wait_ge(s_oadd, t + 1)
                sp.dma_start(out[0, t * P:(t + 1) * P, :], x_res[:, t, :]).then_inc(s_out, 16)
            sp.wait_ge(s_out, 16 * NT)

        @block.gpsimd
        def _(pool):
            chain = [0]

            def link(ins):
                chain[0] += 1
                ins.then_inc(s_gp, 1)
                pool.wait_ge(s_gp, chain[0])

            nc.gpsimd.memset(rel[N_BUCKETS:N_BUCKETS + 1, :], NEG).then_inc(s_ncst, 1)
            pool.wait_ge(s_ncst, 1)
            link(nc.gpsimd.memset(minus_half[:, :], -0.5))
            nc.gpsimd.memset(vc[:, :, :, :], 0.0).then_inc(s_zero, 1)
            pool.wait_ge(s_zero, 1)
            pool.wait_ge(s_const, 16 * N_CONST)
            for n, col in enumerate((G_QA, G_QB)):
                nc.gpsimd.tensor_scalar(gain[:, col:col + 1], gain[:, col:col + 1], HD ** -0.5, None,
                                        ALU.mult).then_inc(s_ncst, 1)
                pool.wait_ge(s_ncst, n + 2)
            for n in range(2):
                pool.wait_ge(s_sqx, 4 * (n + 1))
                part = ssx[:, 4 * n:4 * n + 4]
                link(nc.gpsimd.tensor_scalar(part, part, 1.0 / D, EPS, ALU.mult, ALU.add))
                nc.gpsimd.tensor_tensor(part, part, minus_half[:, 0:4], ALU.pow).then_inc(s_rx, 1)

            def norm(n):
                kind, t = norms[n]
                if kind == "kc":
                    pool.wait_ge(s_cme, 4)
                else:
                    pool.wait_ge(s_pre, unit_no[("small" if kind == "ckv" else kind, t, 0)] + 1)
                if kind == "ckv":
                    ss, cols, w = ssq[:, n % 3, 0:1], ckv[:, t, :], P
                elif kind == "kc":
                    ss, cols, w = ssq[0:N_C, n % 3, 0:NG], kc, HD
                elif kind == "up":
                    ss, cols, w = ssq[:, n % 3, 0:NG], nat[:, n % 3, 0:2 * P], HD
                elif kind == "kv":
                    ss, cols, w = ssq[:, n % 3, 0:2 * NG], nat[:, n % 3, :], HD
                else:
                    ss, cols, w = ssq[:, n % 3, 0:NH], nat[:, n % 3, :], HD
                link(nc.gpsimd.tensor_scalar(ss, ss, 1.0 / w, EPS, ALU.mult, ALU.add))
                mh = minus_half[0:ss.shape[0], 0:ss.shape[1]]
                link(nc.gpsimd.tensor_tensor(ss, ss, mh, ALU.pow))
                if kind == "ckv":
                    nc.gpsimd.tensor_tensor(cols, cols, ss.to_broadcast([P, P]), ALU.mult).then_inc(s_nrm, 1)
                elif kind == "kc":
                    for two in range(2):
                        r = ss.unsqueeze(2).to_broadcast([N_C, NG, HD])
                        done = nc.gpsimd.tensor_tensor(kc[:, :, two, :], kc[:, :, two, :], r, ALU.mult)
                        if two == 0:
                            link(done)
                        else:
                            done.then_inc(s_nrm, 1)
                elif kind in ("kv", "up"):
                    ng = ss.shape[1]
                    v = cols.rearrange("p (b two d) -> p b two d", b=ng, two=2)
                    for two in range(2):
                        r = ss.unsqueeze(2).to_broadcast([P, ng, HD])
                        done = nc.gpsimd.tensor_tensor(v[:, :, two, :], v[:, :, two, :], r, ALU.mult)
                        if two == 0:
                            link(done)
                        else:
                            done.then_inc(s_nrm, 1)
                else:
                    v = cols.rearrange("p (h d) -> p h d", h=NH)
                    r = ss.unsqueeze(2).to_broadcast([P, NH, HD])
                    nc.gpsimd.tensor_tensor(v, v, r, ALU.mult).then_inc(s_nrm, 1)

            def mask_diagonals(seen_value):
                pool.wait_ge(s_flip, seen_value)
                for n, i in enumerate(SEL_TILES):
                    d = score[:, SEL_OFF[n] + i * P:SEL_OFF[n] + (i + 1) * P]
                    nc.gpsimd.affine_select(out=d, in_=d, compare_op=ALU.is_ge, fill=NEG, base=0,
                                            pattern=[[-1, P]], channel_multiplier=1).then_inc(s_mask, 1)

            for t in range(NT):
                norm(t)
            mask_diagonals(1)
            mask_diagonals(2)
            for n in range(NT, len(norms)):
                norm(n)
            pool.wait_ge(s_sel, 1)
            nc.gpsimd.memset(eyeb[:, :], 0.0).then_inc(s_masks, 1)
            pool.wait_ge(s_masks, 1)
            nc.gpsimd.memset(winb[:, :], 0.0).then_inc(s_masks, 1)
            pool.wait_ge(s_masks, 2)
            nc.gpsimd.affine_select(out=eyeb[:, :], in_=eyeb[:, :], compare_op=ALU.not_equal, fill=1.0, base=0,
                                    pattern=[[-1, P]], channel_multiplier=1).then_inc(s_masks, 1)
            pool.wait_ge(s_masks, 3)
            nc.gpsimd.affine_select(out=winb[:, :], in_=winb[:, :], compare_op=ALU.is_gt, fill=NEG, base=0,
                                    pattern=[[1, P]], channel_multiplier=-1).then_inc(s_masks, 1)

        @block.scalar
        def _(act):
            sqo = [0]

            def squares(src, ss, w):
                if sqo[0] >= 2:
                    act.wait_ge(s_sqo, sqo[0] - 1)
                nc.scalar.activation(junk[0:src.shape[0], sqo[0] % 2, 0:w], src, ACT.Square,
                                     accum_out=ss).then_inc(s_sqo, 1)
                sqo[0] += 1

            for t in range(NT):
                act.wait_ge(s_x[t], 16)
                if t >= 2:
                    act.wait_ge(s_sqx, t - 1)
                nc.scalar.activation(square[t % 2], x_in[:, t, :], ACT.Square,
                                     accum_out=ssx[:, t:t + 1]).then_inc(s_sqx, 1)
            act.wait_ge(s_const, 16 * N_CONST)
            act.wait_ge(s_ncst, 3)
            for c in range(0, 2 * KT, 2):
                act.wait_ge(s_ht, c + 1)
                half, k = divmod(c, KT)
                nc.scalar.activation(hT[:, k, half * BANK:(half + 1) * BANK], ps[:, c % 8, :], ACT.Copy,
                                     scale=gx[:, k:k + 1]).then_inc(s_hact, 1)

            nats = [0]

            def free_nat(n):
                if n >= 3 and norms[n - 3][0] in ("kv", "up", "qb", "qa"):
                    act.wait_ge(s_tr, tr_no[norms[n - 3]] + 1)
                elif n >= 3:
                    act.wait_ge(s_nrm, n - 2)

            def unit(u):
                kind, a, half = units[u]
                act.wait_ge(s_pr, u + 1)
                bank = ps[:, u % 4, :]
                if kind == "qiT":
                    if u == 0:
                        act.wait_ge(s_ht, 2 * KT)
                    nc.scalar.activation(qiT[:, a, half * BANK:(half + 1) * BANK], bank, ACT.Copy).then_inc(s_pre, 1)
                elif kind == "kiT":
                    nc.scalar.activation(kiT[:, half * BANK:(half + 1) * BANK], bank, ACT.Copy).then_inc(s_pre, 1)
                elif kind == "small":
                    n = norm_no[("ckv", a)]
                    free_nat(n)
                    squares(bank[:, 0:P], ssq[:, n % 3, 0:1], P)
                    nc.scalar.activation(ckv[:, a, :], bank[:, 0:P], ACT.Copy)
                    nc.scalar.activation(widx[:, a, :], bank[:, P:P + NH], ACT.Copy, scale=NH ** -0.5)
                    nc.scalar.activation(gates[:, a, :], bank[:, P + NH:P + NH + 3 * NH], ACT.Copy).then_inc(s_pre, 1)
                elif kind in ("kv", "up"):
                    n = norm_no[(kind, a)]
                    free_nat(n)
                    if kind == "kv":
                        kcols, vcols = (0, 2 * P), ((vs, P), (vw, 3 * P))
                    else:
                        kcols, vcols = (0,), ((va, P),)
                    for b, c0 in enumerate(kcols):
                        for g in range(NG):
                            squares(bank[:, c0 + g * HD:c0 + (g + 1) * HD], ssq[:, n % 3, b * NG + g:b * NG + g + 1], HD)
                    for b, c0 in enumerate(kcols):
                        dst = nat[:, n % 3, b * 2 * P:(b + 1) * 2 * P].rearrange("p (g two d) -> p g two d", g=NG, two=2)
                        for two in range(2):
                            nc.scalar.activation(dst[:, :, two, :],
                                                 bank[:, c0:c0 + P].rearrange("p (g d) -> p g d", g=NG), ACT.Copy)
                    for dst, c0 in vcols:
                        last = nc.scalar.activation(dst[:, a, :], bank[:, c0:c0 + P], ACT.Copy)
                    last.then_inc(s_pre, 1)
                elif kind == "kcT":
                    if a == 0 and half == 0:
                        act.wait_ge(s_acc, len(sjobs))
                    nc.scalar.activation(kcT_raw[:, a, half * BANK:(half + 1) * BANK], bank, ACT.Copy).then_inc(s_pre, 1)
                elif kind in ("qb", "qa"):
                    n = norm_no[(kind, a)]
                    free_nat(n)
                    for h in range(NH):
                        squares(bank[:, h * HD:(h + 1) * HD], ssq[:, n % 3, h:h + 1], HD)
                    nc.scalar.activation(nat[:, n % 3, :], bank, ACT.Copy).then_inc(s_pre, 1)
                else:
                    c0 = 0 if kind == "za" else BANK
                    nc.scalar.activation(z[:, a, c0:c0 + BANK], bank, ACT.Silu).then_inc(s_pre, 1)

            def tr_out(m):
                kind, t = trs[m]
                act.wait_ge(s_tr, m + 1)
                bank = ps[:, 4 + m % 4, :]
                if kind == "ckvT":
                    nc.scalar.activation(ckvT[:, t * BANK:(t + 1) * BANK], bank, ACT.Copy,
                                         scale=gain[:, G_CKV:G_CKV + 1]).then_inc(s_tre, 1)
                    return
                b4 = bank.rearrange("p (m t) -> p m t", m=4)
                cols = slice(t * P, (t + 1) * P)
                if kind == "kv":
                    nc.scalar.activation(ksT[:, :, cols], b4[:, 0:2, :], ACT.Copy, scale=gain[:, G_KS:G_KS + 1])
                    nc.scalar.activation(kwT[:, :, cols], b4[:, 2:4, :], ACT.Copy,
                                         scale=gain[:, G_KW:G_KW + 1]).then_inc(s_tre, 1)
                elif kind == "up":
                    nc.scalar.activation(kaT[:, :, cols], b4[:, 0:2, :], ACT.Copy,
                                         scale=gain[:, G_KA:G_KA + 1]).then_inc(s_tre, 1)
                elif kind == "kc":
                    nc.scalar.activation(kcT[:, :, 0:N_C], b4[:, 0:2, 0:N_C], ACT.Copy,
                                         scale=gain[:, G_KC:G_KC + 1]).then_inc(s_tre, 1)
                else:
                    dst, g = (qbT, G_QB) if kind == "qb" else (qaT, G_QA)
                    nc.scalar.activation(dst[:, :, cols], b4[:, :, :], ACT.Copy, scale=gain[:, g:g + 1]).then_inc(s_tre, 1)

            def compress_steps():
                act.wait_ge(s_cmp, 1)
                nc.scalar.activation(hid_c[:, :], ps[0:HD, 6, 256:258], ACT.Copy).then_inc(s_cme, 1)
                act.wait_ge(s_cme, 1)
                for v in range(2):
                    nc.scalar.activation(hid[:, v * NG:(v + 1) * NG, 0:N_C],
                                         ps[0:HD, 6:8, v * HD:v * HD + N_C],
                                         ACT.Gelu_apprx_tanh, bias=hid_c[:, v:v + 1]).then_inc(s_cme, 1)
                act.wait_ge(s_cmp, 2)
                n = norm_no[("kc", 0)]
                free_nat(n)
                src = ps[0:N_C, 6, :]
                for g in range(NG):
                    squares(src[:, g * HD:(g + 1) * HD], ssq[0:N_C, n % 3, g:g + 1], HD)
                for two in range(2):
                    nc.scalar.activation(kc[:, :, two, :], src[:, 0:P].rearrange("p (g d) -> p g d", g=NG), ACT.Copy)
                act.wait_ge(s_zero, 1)
                for two in range(2):
                    r = slice(two * HD, two * HD + N_C)
                    last = nc.scalar.activation(vc[r, :, two, :], ps[r, 6, P:2 * P].rearrange("p (g d) -> p g d", g=NG),
                                                ACT.Copy)
                last.then_inc(s_cme, 1)

            def score_relu(n):
                i, h = sjobs[n]
                act.wait_ge(s_sc, n + 1)
                if n >= 2:
                    act.wait_ge(s_acc, n - 1)
                w = P * (i + 1)
                nc.scalar.activation(relu[:, n % 2, 0:w],
                                     ps[:, 4 + 2 * (n % 2):6 + 2 * (n % 2), :].rearrange("p b c -> p (b c)")[:, 0:w],
                                     ACT.Relu, scale=HD ** -0.5).then_inc(s_relu, 1)

            for step in stage_order:
                what, n = step
                if what == "unit":
                    unit(n)
                elif what == "tr":
                    tr_out(n)
                elif what == "score":
                    score_relu(n)
                elif what == "compress":
                    compress_steps()
            act.wait_ge(s_gate, 1)
            nc.scalar.activation(gates[:, :, :], gates[:, :, :], ACT.Sigmoid).then_inc(s_gate, 1)

            for what, n in events:
                if what == "qk":
                    br, i, h = jobs[n]
                    act.wait_ge(s_lg, n + 1)
                    s = set_no[set_of(jobs[n])]
                    if br == "c":
                        v = soft[:, n % 4, 0:BANK].rearrange("p (h c) -> p h c", h=NH)[:, :, 0:N_C]
                        nc.scalar.activation(v, v, ACT.Exp).then_inc(s_ex, 1)
                    else:
                        w = P * (i + 1 - first_block(jobs[n]))
                        if s >= 4 and h % HG == 0:
                            act.wait_ge(s_oe, s - 3)
                        nc.scalar.activation(soft[:, n % 4, 0:w], soft[:, n % 4, 0:w], ACT.Exp, scale=-1.0,
                                             bias=nmax[:, n % 4, 0:1],
                                             accum_out=rsum[:, s % 4, h % HG:h % HG + 1]).then_inc(s_ex, 1)
                elif what == "t" and not chunk_dve[n]:
                    act.wait_ge(s_t, n + 1)
                    if n >= 3:
                        act.wait_ge(s_pv, n - 2)
                    nc.scalar.activation(probT[:, n % 3, :], ps[:, 4 + n % 2, :], ACT.Copy).then_inc(s_pta, 1)
            for t in range(NT):
                act.wait_ge(s_yt, 2 * t + 1)
                if t >= 2:
                    act.wait_ge(s_op, t - 1)
                nc.scalar.activation(yT[:, t % 2, 0:4, :], ps[:, 4 + 2 * (t % 2), :].rearrange("p (k t) -> p k t", k=4),
                                     ACT.Copy).then_inc(s_yta, 1)

        @block.vector
        def _(dve):
            chain = [0]

            def link(ins):
                chain[0] += 1
                ins.then_inc(s_dv, 1)
                dve.wait_ge(s_dv, chain[0])

            for n, (m, at, cn) in enumerate(line_parts):
                dve.wait_ge(s_line, n + 1)
                nc.vector.tensor_copy(lines[0:m, at:at + cn], ps[0:m, n, 0:cn]).then_inc(s_linesb, 1)
            for t in range(NT):
                dve.wait_ge(s_rx, t // 4 + 1)
                nc.vector.tensor_scalar(x_in[:, t, :], x_in[:, t, :], ssx[:, t:t + 1], None, ALU.mult).then_inc(s_h, 1)
            for c in range(1, 2 * KT, 2):
                dve.wait_ge(s_ht, c + 1)
                half, k = divmod(c, KT)
                nc.vector.tensor_scalar(hT[:, k, half * BANK:(half + 1) * BANK], ps[:, c % 8, :], gx[:, k:k + 1], None,
                                        ALU.mult).then_inc(s_hdve, 1)
            dve.wait_ge(s_pre, N_EARLY)
            nc.vector.tensor_tensor(gates[:, :, :], gates[:, :, :],
                                    bgate[:, :].unsqueeze(1).to_broadcast([P, NT, 3 * NH]), ALU.add).then_inc(s_gate, 1)
            dve.wait_ge(s_lined, 32)
            for n, (i, h) in enumerate(sjobs):
                o = SEL_OFF[i - T_SEL]
                w = P * (i + 1)
                y = score[:, o:o + w]
                dve.wait_ge(s_relu, n + 1)
                if h == 0:
                    nc.vector.tensor_scalar(y, relu[:, n % 2, 0:w], widx[:, i, h:h + 1], None, ALU.mult).then_inc(s_acc, 1)
                else:
                    dve.wait_ge(s_acc, n)
                    nc.vector.scalar_tensor_tensor(out=y, in0=relu[:, n % 2, 0:w], scalar=widx[:, i, h:h + 1], in1=y,
                                                   op0=ALU.mult, op1=ALU.add).then_inc(s_acc, 1)
            dve.wait_ge(s_acc, len(sjobs))
            nc.vector.memset(cur[:, :], 0).then_inc(s_flip, 1)
            dve.wait_ge(s_mask, N_SEL)

            def count(op, at, out, start=None):
                for n in range(N_SEL):
                    w = SEL_W[n]
                    if n >= 2:
                        dve.wait_ge(s_dv, chain[0] - 1)
                    chain[0] += 1
                    nc.vector.tensor_scalar(mark[n % 2][:, 0:w], score[:, SEL_OFF[n]:SEL_OFF[n] + w],
                                            0.0 if at is None else at[:, n:n + 1],
                                            None if start is None else start[:, n:n + 1],
                                            op, ALU.add, accum_out=out[:, n:n + 1]).then_inc(s_dv, 1)
                dve.wait_ge(s_dv, chain[0])

            count(ALU.is_ge, None, cnt)
            link(nc.vector.tensor_scalar(ispos[:, :], cnt[:, :], float(TOPK), None, ALU.is_ge))
            link(nc.vector.tensor_scalar(sgn[:, :], ispos[:, :], 2.0, -1.0, ALU.mult, ALU.add))
            link(nc.vector.tensor_scalar(kth[:, :], ispos[:, :], -1.0, 1.0, ALU.mult, ALU.add))
            link(nc.vector.tensor_tensor(kth[:, :], kth[:, :], rows[:, :], ALU.mult))
            link(nc.vector.tensor_scalar(kth[:, :], kth[:, :], float(TOPK), None, ALU.add))
            link(nc.vector.tensor_scalar(nkth[:, :], kth[:, :], -1.0, None, ALU.mult))
            for n in range(N_SEL):
                y = score[:, SEL_OFF[n]:SEL_OFF[n + 1]]
                last = nc.vector.tensor_scalar(y, y, sgn[:, n:n + 1], None, ALU.mult)
                if n < N_SEL - 1:
                    link(last)
            last.then_inc(s_flip, 1)
            dve.wait_ge(s_mask, 2 * N_SEL)

            base = chain[0]
            steps = N_SEL + 3
            with dve.Fori(0, N_BITS) as bit:
                dve.wait_ge(s_dv, steps * bit + base)
                nc.vector.tensor_tensor(cand[:, :], cur[:, :],
                                        bitsi[:, bass.ds(bit, 1)].to_broadcast([P, N_SEL]),
                                        ALU.bitwise_or).then_inc(s_dv, 1)
                dve.wait_ge(s_dv, steps * bit + base + 1)
                for n in range(N_SEL):
                    w = SEL_W[n]
                    if n >= 2:
                        dve.wait_ge(s_dv, steps * bit + base + n)
                    nc.vector.tensor_scalar(mark[n % 2][:, 0:w], score[:, SEL_OFF[n]:SEL_OFF[n] + w],
                                            cand[:, n:n + 1].bitcast(F32), nkth[:, n:n + 1], ALU.is_ge, ALU.add,
                                            accum_out=cnt[:, n:n + 1]).then_inc(s_dv, 1)
                dve.wait_ge(s_dv, steps * bit + base + N_SEL + 1)
                nc.vector.tensor_scalar(keep[:, :], cnt[:, :], 0.0, bits[:, bass.ds(bit, 1)], ALU.is_ge,
                                        ALU.mult).then_inc(s_dv, 1)
                dve.wait_ge(s_dv, steps * bit + base + N_SEL + 2)
                nc.vector.tensor_tensor(cur[:, :], cur[:, :], keep[:, :], ALU.bitwise_or).then_inc(s_dv, 1)
            chain[0] += steps * N_BITS
            dve.wait_ge(s_dv, chain[0])

            mag = cur[:, :].bitcast(F32)
            count(ALU.is_ge, mag, cnt)
            count(ALU.is_gt, mag, cnt2)
            link(nc.vector.tensor_tensor(cnt2[:, :], kth[:, :], cnt2[:, :], ALU.subtract))
            link(nc.vector.tensor_tensor(cnt[:, :], cnt[:, :], kth[:, :], ALU.subtract))
            link(nc.vector.tensor_scalar(cnt[:, :], cnt[:, :], 1.0, None, ALU.add))
            link(nc.vector.tensor_tensor(cnt2[:, :], cnt2[:, :], cnt[:, :], ALU.subtract))
            link(nc.vector.tensor_tensor(cnt2[:, :], cnt2[:, :], ispos[:, :], ALU.mult))
            link(nc.vector.tensor_tensor(need[:, :], cnt2[:, :], cnt[:, :], ALU.add))
            link(nc.vector.tensor_tensor(thr[:, :], mag, sgn[:, :], ALU.mult))
            for n in range(N_SEL):
                w = SEL_W[n]
                y = score[:, SEL_OFF[n]:SEL_OFF[n] + w]
                link(nc.vector.tensor_scalar(tie[:, 0:w], y, mag[:, n:n + 1], None, ALU.is_equal))
                link(nc.vector.tensor_tensor_scan(ties_to[:, 0:w], tie[:, 0:w], tie[:, 0:w], 0.0, ALU.add, ALU.max))
                link(nc.vector.scalar_tensor_tensor(out=tie[:, 0:w], in0=ties_to[:, 0:w], scalar=need[:, n:n + 1],
                                                    in1=tie[:, 0:w], op0=ALU.is_gt, op1=ALU.is_ge))
                link(nc.vector.tensor_scalar(unsel[:, 0:w], y, sgn[:, n:n + 1], thr[:, n:n + 1], ALU.mult, ALU.is_le))
                link(nc.vector.scalar_tensor_tensor(out=selmask[:, SEL_OFF[n]:SEL_OFF[n] + w], in0=unsel[:, 0:w],
                                                    scalar=NEG, in1=tie[:, 0:w], op0=ALU.mult, op1=ALU.mult))
            nc.vector.tensor_copy(need[:, :], cnt[:, :]).then_inc(s_sel, 1)

            for b in range(4):
                link(nc.vector.memset(soft[:, b, 0:BANK], 0.0))
            dve.wait_ge(s_gate, 2)
            link(nc.vector.tensor_scalar(gates[:, 0, :].rearrange("p (h b) -> p h b", b=3)[:, :, 0],
                                         gates[:, 0, :].rearrange("p (h b) -> p h b", b=3)[:, :, 0],
                                         seen[:, 0:1], None, ALU.mult))

            def finish(s, k):
                br, i, g = sets[s]
                heads = slice(0, NH) if br == "c" else slice(g * HG, (g + 1) * HG)
                cols = slice(heads.start * HD, heads.stop * HD)
                nh = heads.stop - heads.start
                r = rinv[:, 0:nh]
                link(nc.vector.reciprocal(r, rsum[:, s % 4, 0:nh]))
                if br != "a":
                    gate = gates[:, i, :].rearrange("p (h b) -> p h b", b=3)[:, heads, "csw".index(br)]
                    link(nc.vector.tensor_tensor(r, r, gate, ALU.mult))
                dst = o_acc[:, cols] if br == "c" else head_o[:, cols]
                if br == "c":
                    o_ps = ps[:, 6 + s % 2, :].rearrange("p (h d) -> p h d", h=NH)
                else:
                    o_ps = ps[:, 6 + s % 2, :].rearrange("p (h g d) -> p h g d", h=HG, g=NG)[:, :, g, :]
                dve.wait_ge(s_pv, k + 1)
                nc.vector.tensor_tensor(dst.rearrange("p (h d) -> p h d", h=nh), o_ps,
                                        r.unsqueeze(2).to_broadcast([P, nh, HD]), ALU.mult).then_inc(s_oe, 1)
                dve.wait_ge(s_oe, s + 1)
                c0 = cols.start + (0 if br == "a" else BANK)
                zy = z[:, i, c0:c0 + nh * HD]
                if br in "sw":
                    link(nc.vector.tensor_tensor(o_acc[:, cols], o_acc[:, cols], dst, ALU.add))
                if br == "w":
                    link(nc.vector.tensor_tensor(zy, zy, o_acc[:, cols], ALU.mult))
                if br == "a":
                    y_done[0] += 1
                    nc.vector.tensor_tensor(zy, zy, dst, ALU.mult).then_inc(s_y, 1)
                    dve.wait_ge(s_y, y_done[0])

            y_done = [0]
            pos = 0
            for what, n in events:
                if what == "qk":
                    br, i, h = jobs[n]
                    dve.wait_ge(s_qk, n + 1)
                    if n >= 4:
                        dve.wait_ge(s_t, last_chunk[n - 4] + 1)
                    if n == 0:
                        dve.wait_ge(s_cstrip, 16 * (P // CMP_STRIDE))
                    if h == 0 and br == "s":
                        for m, (c0, c1) in enumerate(B_PIECES):
                            if c1 == L - i * P:
                                dve.wait_ge(s_bstrip[m], 16 * (P // REP))
                    if n == FIRST_A:
                        dve.wait_ge(s_astrip[0], 16 * (P // REP))
                    slot = ps[:, 2 * (n % 2):2 * (n % 2) + 2, :].rearrange("p b c -> p (b c)")
                    if br == "c":
                        c0 = (P // CMP_STRIDE) * (NT - 1 - i)
                        lg = soft[:, n % 4, 0:BANK].rearrange("p (h c) -> p h c", h=NH)[:, :, 0:N_C]
                        for two in range(2):
                            link(nc.vector.tensor_tensor(
                                lg[:, two::2, :], ps[:, 2 * (n % 2) + two, 0:4 * HD].rearrange("p (m c) -> p m c", m=4)[:, :, 0:N_C],
                                strip_c[:, two::2, c0:c0 + N_C], ALU.add))
                        link(nc.vector.tensor_reduce(nmax[:, n % 4, :], lg, AX.X, ALU.max, negate=True))
                        nc.vector.tensor_tensor(lg, lg, nmax[:, n % 4, :].unsqueeze(2).to_broadcast([P, NH, N_C]),
                                                ALU.add).then_inc(s_lg, 1)
                    else:
                        strip = strip_a if br == "a" else strip_b
                        w = P * (i + 1 - first_block(jobs[n]))
                        nc.vector.tensor_tensor_reduce(out=soft[:, n % 4, 0:w], in0=slot[:, 0:w],
                                                       in1=strip[:, h, L - w:L], scale=-1.0, scalar=3e38, op0=ALU.add,
                                                       op1=ALU.min, accum_out=nmax[:, n % 4, 0:1]).then_inc(s_lg, 1)
                elif what == "t":
                    k = n
                    job = jobs[chunks[k][0][0]]
                    if job[0] == "c" and chunks[k][0][1] == 0:
                        m = chunks[k][0][0]
                        dve.wait_ge(s_ex, m + 1)
                        lg = soft[:, m % 4, 0:BANK].rearrange("p (h c) -> p h c", h=NH)[:, :, 0:N_C]
                        link(nc.vector.tensor_reduce(rsum[:, set_no[set_of(job)] % 4, :], lg, AX.X, ALU.add))
                    if chunk_dve[k]:
                        dve.wait_ge(s_t, k + 1)
                        if k >= 3:
                            dve.wait_ge(s_pv, k - 2)
                        nc.vector.tensor_copy(probT[:, k % 3, :], ps[:, 4 + k % 2, :]).then_inc(s_ptd, 1)
                else:
                    for b in chunks[n]:
                        if ends_set(b[0], pos):
                            finish(set_no[set_of(jobs[b[0]])], n)
                        pos += 1
            def add_x(t):
                dve.wait_ge(s_op, t + 1)
                nc.vector.tensor_tensor(x_res[:, t, :],
                                        ps[:, 2 * (t % 2):2 * (t % 2) + 2, :].rearrange("p b c -> p (b c)"),
                                        x_res[:, t, :], ALU.add).then_inc(s_oadd, 1)

            dve.wait_ge(s_xr, 16)
            for t in range(NT):
                dve.wait_ge(s_yt, 2 * t + 2)
                if t >= 2:
                    dve.wait_ge(s_op, t - 1)
                nc.vector.tensor_copy(yT[:, t % 2, 4:8, :],
                                      ps[:, 5 + 2 * (t % 2), :].rearrange("p (k t) -> p k t", k=4)).then_inc(s_ytd, 1)
                if t:
                    add_x(t - 1)
            add_x(NT - 1)

        @block.tensor
        def _(pe):
            mm = nc.tensor.matmul
            pe.wait_ge(s_first, 16 * N_FIRST)
            pe.wait_ge(s_ncst, 1)
            for n, (m, at, cn) in enumerate(line_parts):
                lhs = rel[:, :] if m == 2 * NH else rel[:, NH:2 * NH]
                mm(ps[0:m, n, 0:cn], lhs, oh[:, at:at + cn], start=True, stop=True).then_inc(s_line, 1)
            pe.wait_ge(s_linesb, N_LINE)
            for c in range(2 * KT):
                half, k = divmod(c, KT)
                if k == 0:
                    pe.wait_ge(s_h, 4 * (half + 1))
                if c >= 8:
                    pe.wait_ge(*((s_hact, (c - 8) // 2 + 1) if c % 2 == 0 else (s_hdve, (c - 8) // 2 + 1)))
                for t in range(4):
                    last = nc.tensor.transpose(ps[:, c % 8, t * P:(t + 1) * P],
                                               x_in[:, half * 4 + t, k * P:(k + 1) * P], eye[:, :])
                last.then_inc(s_ht, 1)
            pe.wait_ge(s_hact, KT)
            pe.wait_ge(s_hdve, KT)

            def unit(u):
                kind, a, half = units[u]
                if u >= 4:
                    pe.wait_ge(s_pre, u - 3)
                if kind == "up":
                    if a == 0:
                        pe.wait_ge(s_tre, 2)
                    mm(ps[:, u % 4, 0:2 * P], ckvT[:, a * P:(a + 1) * P], wup[:, :], start=True, stop=True).then_inc(s_pr, 1)
                    return
                ch = CHUNK_OF[kind]
                if unit_no.get((kind, a, half)) == min(n for n, v in enumerate(units) if CHUNK_OF.get(v[0]) == ch):
                    pe.wait_ge(s_w[ch % 2], chunk_arrived(ch))
                w = wbuf[:, ch % 2, :, :]
                for k in range(KT):
                    if kind in ("qiT", "kiT", "kcT"):
                        last = mm(ps[:, u % 4, :], w[:, k, a * P:(a + 1) * P], hT[:, k, half * BANK:(half + 1) * BANK],
                                  start=(k == 0), stop=(k == KT - 1))
                    else:
                        c0, cn = (P, P + NH + 3 * NH) if kind == "small" else (0, BANK)
                        last = mm(ps[:, u % 4, 0:cn], hT[:, k, a * P:(a + 1) * P], w[:, k, c0:c0 + cn],
                                  start=(k == 0), stop=(k == KT - 1))
                last.then_inc(s_pr, 1)

            def score_dots(n):
                i, h = sjobs[n]
                if n == 0:
                    pe.wait_ge(s_pre, unit_no[("small", 0, 0)])
                if n >= 2:
                    pe.wait_ge(s_relu, n - 1)
                r = slice(HD * (h % 2), HD * (h % 2) + HD)
                w = P * (i + 1)
                for b in range(0, w, BANK):
                    cn = min(BANK, w - b)
                    last = mm(ps[:, 4 + 2 * (n % 2) + b // BANK, 0:cn], qiT[r, h // 2, i * P:(i + 1) * P], kiT[r, b:b + cn],
                              start=True, stop=True)
                last.then_inc(s_sc, 1)

            def tr(m):
                kind, t = trs[m]
                if m >= 4:
                    pe.wait_ge(s_tre, m - 3)
                if m == 0:
                    pe.wait_ge(s_relu, len(sjobs))
                if m == trs_before_cmp:
                    pe.wait_ge(s_cme, 4)
                if kind == "ckvT":
                    pe.wait_ge(s_nrm, 4 * (t + 1))
                    for n in range(4):
                        last = nc.tensor.transpose(ps[:, 4 + m % 4, n * P:(n + 1) * P], ckv[:, 4 * t + n, :], eye[:, :])
                else:
                    n = norm_no[(kind, t)]
                    pe.wait_ge(s_nrm, n + 1)
                    if kind == "kc":
                        for g in range(NG):
                            last = nc.tensor.transpose(ps[:, 4 + m % 4, g * P:g * P + N_C],
                                                       kc[:, g, :, :].rearrange("p a d -> p (a d)"), eye[0:N_C, 0:N_C])
                    else:
                        for b in range(2 if kind == "up" else 4):
                            last = nc.tensor.transpose(ps[:, 4 + m % 4, b * P:(b + 1) * P], nat[:, n % 3, b * P:(b + 1) * P],
                                                       eye[:, :])
                last.then_inc(s_tr, 1)

            def compress():
                pe.wait_ge(s_w[CH_W1 % 2], chunk_arrived(CH_W1))
                pe.wait_ge(s_pre, unit_no[("kcT", 1, 1)] + 1)
                pe.wait_ge(s_tre, trs_before_cmp)
                for v in range(2):
                    for j in range(CMP_BLOCK):
                        mm(ps[0:HD, 6, 256 + v:257 + v], w1[0:HD, v, j, :], posT[0:HD, v, j:j + 1], start=(j == 0),
                           stop=(j == CMP_BLOCK - 1))
                    for g in range(NG):
                        r = slice(g * HD, (g + 1) * HD)
                        for j in range(CMP_BLOCK):
                            last = mm(ps[0:HD, 6 + g, v * HD:v * HD + N_C], w1[r, v, j, :],
                                      kcT_raw[r, v, j:j + CMP_STRIDE * (N_C - 1) + 1:CMP_STRIDE],
                                      start=(j == 0), stop=(j == CMP_BLOCK - 1))
                last.then_inc(s_cmp, 1)
                pe.wait_ge(s_cme, 3)
                for v in range(2):
                    for g in range(NG):
                        for at in (0, HD)[0:1 + v]:
                            last = mm(ps[at:at + N_C, 6, (v * NG + g) * HD:(v * NG + g + 1) * HD],
                                      hid[:, v * NG + g, 0:N_C], w2[:, v, :], start=True, stop=True)
                last.then_inc(s_cmp, 1)

            for what, n in stage_order:
                if what == "unit":
                    unit(n)
                elif what == "tr":
                    tr(n)
                elif what == "score":
                    score_dots(n)
                elif what == "compress":
                    compress()

            pe.wait_ge(s_pre, len(units))
            pe.wait_ge(s_tre, len(trs))
            v_of = {"s": vs, "w": vw, "a": va}
            for what, n in events:
                if what == "qk":
                    br, i, h = jobs[n]
                    if n >= 2:
                        pe.wait_ge(s_lg, n - 1)
                    if n == FIRST_A:
                        pe.wait_ge(s_sel, 1)
                    if n == first_windowed:
                        pe.wait_ge(s_masks, 4)
                    tok = slice(i * P, (i + 1) * P)
                    b0 = 2 * (n % 2)
                    if br == "c":
                        for hh in range(NH):
                            r = slice(HD * (hh % 2), HD * (hh % 2) + HD)
                            last = mm(ps[:, b0 + hh % 2, (hh // 2) * HD:(hh // 2) * HD + N_C], qbT[r, hh // 2, tok], kcT[r, hh // 4, 0:N_C],
                                      start=True, stop=True)
                        last.then_inc(s_qk, 1)
                        continue
                    r = slice(HD * (h % 2), HD * (h % 2) + HD)
                    qT, kT = (qaT, kaT) if br == "a" else (qbT, ksT if br == "s" else kwT)
                    k0 = first_block(jobs[n]) * P
                    w = (i + 1) * P - k0
                    for b in range(0, w, BANK):
                        cn = min(BANK, w - b)
                        dst = ps[:, b0 + b // BANK, 0:cn]
                        last = mm(dst, qT[r, h // 2, tok], kT[r, h // 4, k0 + b:k0 + b + cn], start=True,
                                  stop=not (br == "a" and i >= T_SEL or br == "w" and i >= WB and b == 0))
                        if br == "a" and i >= T_SEL:
                            o = SEL_OFF[i - T_SEL] + b
                            last = mm(dst, eyeb[:, :], selmask[:, o:o + cn], start=False, stop=True)
                        elif br == "w" and i >= WB and b == 0:
                            last = mm(dst[:, 0:P], eyeb[:, :], winb[:, :], start=False, stop=True)
                    last.then_inc(s_qk, 1)
                elif what == "t":
                    pe.wait_ge(s_ex, chunks[n][-1][0] + 1)
                    if n >= 2:
                        pt_wait(pe, n - 2)
                    for q, (jn, h, j) in enumerate(chunks[n]):
                        dst = ps[:, 4 + n % 2, q * P:(q + 1) * P]
                        c0 = h * P if jobs[jn][0] == "c" else (j - first_block(jobs[jn])) * P
                        last = nc.tensor.transpose(dst, soft[:, jn % 4, c0:c0 + P], eye[:, :])
                    last.then_inc(s_t, 1)
                else:
                    pt_wait(pe, n)
                    for q, (jn, h, j) in enumerate(chunks[n]):
                        br, i, _ = jobs[jn]
                        s = set_no[set_of(jobs[jn])]
                        first = j == first_block(jobs[jn])
                        if first and h % HG == 0 and s >= 2 and not (br == "c" and h):
                            pe.wait_ge(s_oe, s - 1)
                        cols = slice(q * P, (q + 1) * P)
                        if br == "c":
                            last = mm(ps[:, 6 + s % 2, h * P:(h + 1) * P], probT[:, n % 3, cols],
                                      vc[:, h // 2, :, :].rearrange("p two d -> p (two d)"), start=True, stop=True)
                        else:
                            hc = slice((h % HG) * P, (h % HG + 1) * P)
                            last = mm(ps[:, 6 + s % 2, hc], probT[:, n % 3, cols], v_of[br][:, j, :],
                                      start=first, stop=(j == i))
                    last.then_inc(s_pv, 1)

            def y_transpose(t):
                for half in range(2):
                    for k in range(4):
                        c0 = (4 * half + k) * P
                        last = nc.tensor.transpose(ps[:, 4 + 2 * (t % 2) + half, k * P:(k + 1) * P], z[:, t, c0:c0 + P],
                                                   eye[:, :])
                    last.then_inc(s_yt, 1)

            pe.wait_ge(s_y, NG * NT)
            pe.wait_ge(s_wo, 16)
            y_transpose(0)
            for t in range(NT):
                if t + 1 < NT:
                    y_transpose(t + 1)
                pe.wait_ge(s_yta, t + 1)
                pe.wait_ge(s_ytd, t + 1)
                if t >= 2:
                    pe.wait_ge(s_oadd, t - 1)
                for half in range(2):
                    for k in range(KT):
                        last = mm(ps[:, 2 * (t % 2) + half, :], yT[:, t % 2, k, :], wout[:, k, half * BANK:(half + 1) * BANK],
                                  start=(k == 0), stop=(k == KT - 1))
                last.then_inc(s_op, 1)


_INS = ["x", "rel_bias", "norm_g", "w_in", "b_gate_b", "kv_norm_a", "w_kv_up_a", "q_norm_a", "k_norm_a", "q_norm_b",
        "k_norm_cmp", "k_norm_slc", "k_norm_win", "cmp_pos_k", "cmp_pos_v", "w_cmp_k1", "w_cmp_k2", "w_cmp_v1",
        "w_cmp_v2", "w_out"]


def kernel(**inputs):
    import concourse.bacc as bacc
    from concourse.bass_utils import run_bass_kernel_spmd

    nc = bacc.Bacc("TRN2", target_bir_lowering=False, num_devices=1)
    arrays = {name: np.ascontiguousarray(inputs[name]) for name in _INS} | shape_constants()
    aps = {name: nc.dram_tensor(f"in_{name}", a.shape, mybir.dt.from_np(a.dtype), kind="ExternalInput").ap()
           for name, a in arrays.items()}
    out = nc.dram_tensor("out", (1, L, D), F32, kind="ExternalOutput").ap()
    hybrid_layer(nc, out=out, **aps)
    r = run_bass_kernel_spmd(nc, [{f"in_{name}": a for name, a in arrays.items()}], core_ids=[0])
    return r.results[0]["out"]
```

```python
import math
from contextlib import ExitStack

import numpy as np
import concourse.bass as bass
from concourse import mybir

F32 = mybir.dt.float32
F32R = mybir.dt.float32r
BF16 = mybir.dt.bfloat16
I32 = mybir.dt.int32
ALU = mybir.AluOpType
ACT = mybir.ActivationFunctionType
AX = mybir.AxisListType

P = 128
D = 1024
L = 1024
NT = L // P
KT = D // P
HD = 64
NH = 8
NG = 2
TOPK = 256
T_SEL = TOPK // P
SEL_TILES = range(T_SEL, NT)
N_SEL = NT - T_SEL
WIN = 512
WB = WIN // P
CMP_BLOCK, CMP_STRIDE = 32, 16
N_C = (L - CMP_BLOCK) // CMP_STRIDE + 1
N_BUCKETS, MAX_DISTANCE = 32, 1024
EPS = 1e-6
NEG = -1e30
BANK = 512
CW = 256

C_QA, C_CKV, C_QI, C_KI, C_WI, C_ZA = 0, 512, 640, 1152, 1216, 1224
C_QB, C_KC, C_KS, C_GB, C_ZB, C_END = 1736, 2248, 2504, 3016, 3040, 3552

LINE = L + P - 1
REP = 32
CM = 2 * 63
CLINE = CMP_STRIDE * CM
CY = N_C + (NT - 1) * (P // CMP_STRIDE)

SEL_W = [P * (i + 1) for i in SEL_TILES]
SEL_OFF = [sum(SEL_W[:n]) for n in range(N_SEL + 1)]
SEL_TOT = SEL_OFF[-1]
N_BITS = 31


def t5_bucket(dist):
    n = np.maximum(dist, 0)
    exact = N_BUCKETS // 2
    nf = np.maximum(n, 1).astype(np.float32)
    log_b = exact + (np.log(nf / np.float32(exact)) / np.float32(math.log(MAX_DISTANCE / exact))
                     * np.float32(N_BUCKETS - exact)).astype(np.int32)
    return np.where(n < exact, n, np.minimum(log_b, N_BUCKETS - 1))


def one_hot(dist):
    out = np.zeros((N_BUCKETS + 1, dist.size), np.float32)
    row = np.where(dist < 0, N_BUCKETS, t5_bucket(dist))
    out[row, np.arange(dist.size)] = 1.0
    return out


def shape_constants():
    v = np.arange(LINE)
    q, m = np.meshgrid(np.arange(CMP_STRIDE), np.arange(CM), indexing="ij")
    p = np.arange(P)
    eye = np.eye(P, dtype=np.float32)
    return {
        "c_line": one_hot(L - 1 - v),
        "c_cline": one_hot((q - (CMP_BLOCK - 1) + CMP_STRIDE * (63 - m)).ravel()),
        "c_eye": eye,
        "c_bits": np.tile((2.0 ** np.arange(N_BITS - 1, -1, -1, dtype=np.float32))[None], (P, 1)),
        "c_bitsi": np.tile((1 << np.arange(N_BITS - 1, -1, -1)).astype(np.int32)[None], (P, 1)),
        "c_rows": (p[:, None] + P * np.array(SEL_TILES)[None] + 2 - 2 * TOPK).astype(np.float32),
        "c_seen": (p >= CMP_BLOCK - 1).astype(np.float32)[:, None],
    }


def hybrid_layer(nc, x, rel_bias, norm_g, w_in, b_gate_b, kv_norm_a, w_kv_up_a, q_norm_a, k_norm_a, q_norm_b,
                 k_norm_cmp, k_norm_slc, k_norm_win, cmp_pos_k, cmp_pos_v, w_cmp_k1, w_cmp_k2, w_cmp_v1,
                 w_cmp_v2, w_out, c_line, c_cline, c_eye, c_bits, c_bitsi, c_rows, c_seen, out):
    ctx = ExitStack()
    with ctx:
        def sb(name, shape, dt=F32):
            return ctx.enter_context(nc.sbuf_tensor(name, shape, dt))

        def sem(name):
            return ctx.enter_context(nc.semaphore(name))

        line_dram = nc.dram_tensor("line_dram", (2 * NH, REP, LINE), F32, kind="Internal").ap()
        z_dram = nc.dram_tensor("z_dram", (NT, P, D), F32, kind="Internal").ap()
        cline_dram = nc.dram_tensor("cline_dram", (NH, CLINE), F32, kind="Internal").ap()

        def overlay(n, *names):
            views = []
            for name in names[:-1]:
                with nc.sbuf_tensor(name, [P, n], F32) as view:
                    views.append(view)
            return views + [sb(names[-1], [P, n])]

        o_ht, = overlay(8192, "ht_hi")
        hT_hi = o_ht[:, :].rearrange("p (k t) -> p k t", k=KT)
        q_st = o_ht[:, 0:2048].rearrange("p (b part h t) -> p b part h t", b=2, part=2, h=NH // NG)
        o_raw, o_parts, o_strip = overlay(8192, "w_raw", "w_parts", "strip")
        wraw, wbuf = (o[:, :].rearrange("p (b part k c) -> p b part k c", b=2, part=2, k=KT) for o in (o_raw, o_parts))
        strip = o_strip[:, :].rearrange("p (h x) -> p h x", h=NH)
        o_x, o_lo, o_z = overlay(8192, "x_in", "ht_lo", "z")
        x_in, z = (o[:, :].rearrange("p (t c) -> p t c", t=NT) for o in (o_x, o_z))
        hT_lo = o_lo[:, :].rearrange("p (t k c) -> p t k c", t=NT, k=KT)

        o_keys, r_qk = overlay(14336, "keys", "r_qk")
        qa = r_qk[:, 0:4096].rearrange("p (t c) -> p t c", t=NT)
        qb = r_qk[:, 6144:10240].rearrange("p (t c) -> p t c", t=NT)
        kaT, ksT, kwT = (o_keys[:, at:at + 2048].rearrange("p (g t) -> p g t", g=NG) for at in (4096, 10240, 12288))
        wout = r_qk[:, 6144:14336].rearrange("p (k c) -> p k c", k=KT)
        ckv = r_qk[:, 0:1024].rearrange("p (t c) -> p t c", t=NT)
        ckvT = r_qk[:, 1024:2048]
        kcT_raw = r_qk[:, 3072:7168].rearrange("p (v g t) -> p v g t", v=2, g=NG)
        kiT = r_qk[:, 4096:5120]
        qiT = r_qk[:, 6144:10240].rearrange("p (m t) -> p m t", m=NH // 2)
        relu = r_qk[:, 10240:12288].rearrange("p (b c) -> p b c", b=2)
        square = [r_qk[:, 6144 + 1024 * n:7168 + 1024 * n] for n in range(2)]

        va = sb("va", [P, NT, NG * HD])
        vs = sb("vs", [P, NT, NG * HD])
        vw = sb("vw", [P, NT, NG * HD])
        x_res = [v[:, :, :].rearrange("p t c -> p (t c)") for v in (vs, vw)]

        selmask = sb("selmask", [P, SEL_TOT], BF16)
        r_y = sb("r_y", [P, 2 * (LINE + CLINE) + 66])
        oh = r_y[0:N_BUCKETS + 1, 0:LINE + CLINE]
        lines = r_y[0:2 * NH, LINE + CLINE:2 * (LINE + CLINE)]
        score = r_y[:, 0:SEL_TOT]
        tie = r_y[:, SEL_TOT:SEL_TOT + 512].bitcast(BF16)
        unsel = r_y[:, SEL_TOT + 512:SEL_TOT + 1024].bitcast(BF16)
        ties_to = r_y[:, SEL_TOT + 1024:SEL_TOT + 2048]
        mark = [tie, unsel]
        soft = r_y[:, 0:4096].rearrange("p (b c) -> p b c", b=4)
        probT = r_y[:, 4096:5632].rearrange("p (b c) -> p b c", b=3)
        q_dup = r_y[:, 5888:6400].rearrange("p (h two d) -> p h two d", h=NH // NG, two=2)
        yT = r_y[:, 0:2048].rearrange("p (b k t) -> p b k t", b=2, k=KT)

        r_nat = sb("r_nat", [P, 3 * BANK])
        nat = r_nat[:, 0:3 * CW].rearrange("p (b c) -> p b c", b=3)
        z_out = r_nat[:, 2 * BANK:3 * BANK].rearrange("p (b c) -> p b c", b=2)
        strip_c = r_nat[:, 0:NH * CY].rearrange("p (h y) -> p h y", h=NH)
        low = r_nat[:, 2 * BANK:3 * BANK].rearrange("p (b g t) -> p b g t", b=2, g=NG)
        o_acc = r_nat[:, 960:960 + CW]
        head_o = [r_y[:, 5632:5632 + CW], r_nat[:, 1280:1280 + CW]]
        eye = sb("eye", [P, P])
        eyeb = r_nat[:, 1216:1280].bitcast(BF16)
        bits = sb("bits", [P, N_BITS])
        bitsi = sb("bitsi", [P, N_BITS], I32)
        small = sb("small", [P, 12 * N_SEL])
        winb = small[:, 0:P // 2].bitcast(BF16)
        rows = small[:, 0 * N_SEL:1 * N_SEL]
        seen = sb("seen", [P, 1])
        rel = sb("rel", [N_BUCKETS + 1, 2 * NH])
        gx = sb("gx", [P, KT])
        gain = sb("gain", [P, 7])
        G_QA, G_KA, G_QB, G_KC, G_KS, G_KW, G_CKV = range(7)
        wup = r_qk[:, 2048:2304]
        w2 = r_qk[0:HD, 2304:2432].rearrange("p (v c) -> p v c", v=2)
        posT = r_qk[:, 2432:2464].rearrange("p (v j) -> p v j", v=2)
        hid = r_qk[0:HD, 2496:2752].rearrange("p (v c) -> p v c", v=2 * NG)
        kc64 = r_qk[0:HD, 2752:3008]
        kc = r_qk[0:N_C, 2752:3008].rearrange("p (g two d) -> p g two d", g=NG, two=2)
        bgate = sb("bgate", [P, 3 * NH])
        gates = sb("gates", [P, NT, 3 * NH])
        widx = sb("widx", [P, NT, NH])
        minus_half = sb("minus_half", [P, 12])
        ssx = sb("ssx", [P, NT])
        ssq = sb("ssq", [P, 3, NH])
        junk = r_nat[:, 3 * CW:3 * CW + P].bitcast(BF16).rearrange("p (b c) -> p b c", b=2)
        hid_c = sb("hid_c", [HD, 2])
        vc = sb("vc", [P, NG, 2, HD])
        kcT = sb("kcT", [P, NG, HD])
        cur = small[:, 1 * N_SEL:2 * N_SEL].bitcast(I32)
        cand = small[:, 2 * N_SEL:3 * N_SEL].bitcast(I32)
        cnt = small[:, 3 * N_SEL:4 * N_SEL]
        cnt2 = small[:, 4 * N_SEL:5 * N_SEL]
        keep = small[:, 5 * N_SEL:6 * N_SEL].bitcast(I32)
        ispos = small[:, 6 * N_SEL:7 * N_SEL]
        sgn = small[:, 7 * N_SEL:8 * N_SEL]
        kth = small[:, 8 * N_SEL:9 * N_SEL]
        nkth = small[:, 9 * N_SEL:10 * N_SEL]
        need = small[:, 10 * N_SEL:11 * N_SEL]
        thr = small[:, 11 * N_SEL:12 * N_SEL]
        nmax = sb("nmax", [P, 4, NH // NG])
        rsum = sb("rsum", [P, 4, NH // NG])
        rinv = sb("rinv", [P, 2, NH // NG])

        ps = ctx.enter_context(nc.psum_tensor("ps", [P, 8, BANK], F32))

        s_first = sem("s_first")
        s_const = sem("s_const")
        s_x = [sem(f"s_x{t}") for t in range(NT)]
        s_w = [sem(f"s_w{b}") for b in range(2)]
        s_whi = sem("s_whi")
        s_wlo = sem("s_wlo")
        s_low = sem("s_low")
        s_dup = sem("s_dup")
        s_qt = sem("s_qt")
        s_qhi = sem("s_qhi")
        s_qlo = sem("s_qlo")
        s_kdup = sem("s_kdup")
        s_zout = [sem(f"s_zout{b}") for b in range(2)]
        s_zin = [sem(f"s_zin{t}") for t in range(NT)]
        s_line = sem("s_line")
        s_linesb = sem("s_linesb")
        s_lined = sem("s_lined")
        s_gp = sem("s_gp")
        s_sqx = sem("s_sqx")
        s_rx = sem("s_rx")
        s_h = sem("s_h")
        s_ht = sem("s_ht")
        s_hact = sem("s_hact")
        s_hdve = sem("s_hdve")
        s_pr = sem("s_pr")
        s_pre = sem("s_pre")
        s_sc = sem("s_sc")
        s_relu = sem("s_relu")
        s_acc = sem("s_acc")
        s_dv = sem("s_dv")
        s_mask = sem("s_mask")
        s_flip = sem("s_flip")
        s_sel = sem("s_sel")
        s_soft = sem("s_soft")
        s_nrm = sem("s_nrm")
        s_sqo = sem("s_sqo")
        s_tr = sem("s_tr")
        s_tre = sem("s_tre")
        s_cmp = sem("s_cmp")
        s_cme = sem("s_cme")
        s_masks = sem("s_masks")
        s_zero = sem("s_zero")
        s_gate = sem("s_gate")
        s_ncst = sem("s_ncst")
        B_PIECES = [(L - P, L), (L - 4 * P, L - P), (0, L - 4 * P)]
        s_bstrip = [sem(f"s_bstrip{n}") for n in range(len(B_PIECES))]
        s_astrip = [sem(f"s_astrip{g}") for g in range(NG)]
        s_cstrip = sem("s_cstrip")
        s_qk = sem("s_qk")
        s_lg = sem("s_lg")
        s_ex = sem("s_ex")
        s_t = sem("s_t")
        s_pta = sem("s_pta")
        s_ptd = sem("s_ptd")
        s_pv = sem("s_pv")
        s_oe = sem("s_oe")
        s_fin = sem("s_fin")
        s_wo = sem("s_wo")
        s_xr = [sem(f"s_xr{b}") for b in range(2)]
        s_yt = sem("s_yt")
        s_yta = sem("s_yta")
        s_ytd = sem("s_ytd")
        s_op = sem("s_op")
        s_oadd = sem("s_oadd")
        s_out = [sem(f"s_out{b}") for b in range(2)]

        (CH_QI0, CH_QI1, CH_SMALL, CH_KS, CH_KW, CH_KC, CH_W1, CH_QB0, CH_QB1, CH_QA0, CH_QA1, CH_Z0, CH_Z1, CH_Z2,
         CH_Z3) = range(15)
        N_CHUNKS = 15
        w_src = w_in[0].rearrange("(k p) c -> p k c", p=P)
        JJ = CMP_BLOCK // 2
        w1_src = [w.rearrange("a (jj r) c -> r (a jj) c", r=P) for w in (w_cmp_k1, w_cmp_v1)]
        w1 = wraw[:, CH_W1 % 2, 0, :, :].rearrange("p k c -> p (k c)").rearrange("p (v j c) -> p v j c", v=2, j=JJ)
        KI_AT, SMALL_AT, SMALL_W = 0, HD, P + NH + 3 * NH
        first_col = {CH_QI0: C_QI, CH_QI1: C_QI + CW, CH_KS: C_KS, CH_KW: C_KS + CW, CH_KC: C_KC, CH_QB0: C_QB,
                     CH_QB1: C_QB + CW, CH_QA0: C_QA, CH_QA1: C_QA + CW, CH_Z0: C_ZA, CH_Z1: C_ZA + CW, CH_Z2: C_ZB,
                     CH_Z3: C_ZB + CW}
        chunk_loads = {c: [(0, col, CW)] for c, col in first_col.items()}
        chunk_loads[CH_SMALL] = [(KI_AT, C_KI, HD), (SMALL_AT, C_CKV, P), (SMALL_AT + P, C_WI, NH),
                                 (SMALL_AT + P + NH, C_GB, 3 * NH)]
        chunk_width = {c: CW for c in first_col} | {CH_SMALL: HD + SMALL_W}
        chunk_count = {c: len(v) for c, v in chunk_loads.items()} | {CH_W1: 2}
        split_chunks = [c for c in range(N_CHUNKS) if c != CH_W1]
        split_no = {c: n for n, c in enumerate(split_chunks)}

        SPLIT_LEAD = 0

        def chunk_arrived(c):
            return 16 * sum(chunk_count[n] for n in range(c % 2, c + 1, 2))

        units = []
        units += [("qiT", cb, half) for cb in range(4) for half in range(2)]
        units += [("kiT", 0, half) for half in range(2)]
        units += [("small", t, 0) for t in range(NT)]
        N_EARLY = len(units)
        units += [("ks", t, 0) for t in range(NT)]
        units += [("kw", t, 0) for t in range(NT)]
        units += [("kcT", cb, half) for cb in range(2) for half in range(2)]
        for c, kind in enumerate(("qb0", "qb1")):
            for t in range(NT):
                units.append((kind, t, 0))
                if t % 2:
                    units.append(("up", (c * NT + t) // 2, 0))
        for kind in ("qa0", "qa1", "z0", "z1", "z2", "z3"):
            units += [(kind, t, 0) for t in range(NT)]
        unit_no = {u: n for n, u in enumerate(units)}
        CHUNK_OF = {"kiT": CH_SMALL, "small": CH_SMALL, "ks": CH_KS, "kw": CH_KW, "kcT": CH_KC, "qb0": CH_QB0,
                    "qb1": CH_QB1, "qa0": CH_QA0, "qa1": CH_QA1, "z0": CH_Z0, "z1": CH_Z1, "z2": CH_Z2, "z3": CH_Z3}

        def chunk_of(u):
            if u[0] == "qiT":
                return (CH_QI0, CH_QI1)[u[1] // 2]
            return CHUNK_OF.get(u[0])

        first_unit, last_unit = {}, {}
        for n, u in enumerate(units):
            first_unit.setdefault(chunk_of(u), n)
            last_unit[chunk_of(u)] = n

        trs = [("ckvT", n) for n in range(2)] + [(kind, t) for kind in ("ks", "kw") for t in range(NT)] + [("kc", 0)]
        trs += [("up", t) for t in range(NT)]
        tr_no = {u: n for n, u in enumerate(trs)}
        KEY_TRS = len(trs) - 2

        sjobs = [(i, h) for i in SEL_TILES for h in range(NH)]

        LAG = 3
        split_at = {first_unit[c - 1] + (last_unit[c - 1] - first_unit[c - 1]) // 2 - SPLIT_LEAD: c
                    for c in split_chunks[2:] if c != CH_QB0}
        stage_order = []
        for u in range(N_EARLY):
            stage_order.append(("unit", u))
            if u in split_at:
                stage_order.append(("split", split_at[u]))
        stage_order += [("score", n) for n in range(len(sjobs))]
        stage_order += [("tr", 0), ("tr", 1)]
        waiting, between = [], []
        for u in range(N_EARLY, len(units)):
            stage_order.append(("unit", u))
            if u in split_at:
                stage_order.append(("split", split_at[u]))
            if units[u] == ("kcT", 1, 1):
                stage_order += [("tr", m) for _, m in waiting]
                waiting = []
                trs_before_cmp = sum(what == "tr" for what, _ in stage_order)
                stage_order += [("split", CH_QB0), ("compress", 0)]
                between = [u + 1, u + 2]
                continue
            if u in between:
                if u == between[-1]:
                    stage_order.append(("compress_out", 0))
                    waiting.append((u, tr_no[("kc", 0)]))
                continue
            while waiting and waiting[0][0] <= u - LAG:
                stage_order.append(("tr", waiting.pop(0)[1]))
            if units[u][:2] in tr_no:
                waiting.append((u, tr_no[units[u][:2]]))
        stage_order += [("tr", m) for _, m in waiting]
        assert [n for what, n in stage_order if what == "tr"] == list(range(len(trs)))

        norms = []
        for what, n in stage_order:
            if what == "compress_out":
                norms.append(("kc", 0))
            elif what == "unit" and units[n][0] not in ("qiT", "kiT", "kcT", "z0", "z1", "z2", "z3"):
                norms.append(("ckv" if units[n][0] == "small" else units[n][0], units[n][1]))
        norm_no = {u: n for n, u in enumerate(norms)}

        HG = NH // NG
        jobs = []
        for i in range(NT):
            for g in range(NG):
                jobs.append(("c", i, g * HG))
                jobs += [(br, i, h) for br in "sw" for h in range(g * HG, (g + 1) * HG)]
        for g in range(NG):
            jobs += [("a", i, h) for i in range(NT) for h in range(g * HG, (g + 1) * HG)]

        def set_of(job):
            return (job[0], job[1], job[2] // HG)

        sets = list(dict.fromkeys(set_of(job) for job in jobs))
        stages = list(dict.fromkeys((job[0] == "a", job[1], job[2] // HG) for job in jobs))
        stage_of = [stages.index((job[0] == "a", job[1], job[2] // HG)) for job in jobs]
        first_job = [stage_of.index(m) for m in range(len(stages))] + [len(jobs)]
        set_no = {s: n for n, s in enumerate(sets)}
        first_windowed = jobs.index(("w", WB, 0))
        FIRST_A = jobs.index(("a", 0, 0))

        def first_block(job):
            return max(0, job[1] - WB) if job[0] == "w" else 0

        blocks = []
        for n, job in enumerate(jobs):
            if job[0] == "c":
                blocks += [(n, m, 0) for m in range(HG // 2)]
            else:
                blocks += [(n, job[2], j) for j in range(first_block(job), job[1] + 1)]
        chunks = [blocks[n:n + 4] for n in range(0, len(blocks), 4)]
        last_chunk = {}
        for k, c in enumerate(chunks):
            for b in c:
                last_chunk[b[0]] = k
        chunk_dve = [k % 3 == 1 for k in range(len(chunks))]

        def pt_wait(eng, k):
            if chunk_dve[k]:
                eng.wait_ge(s_ptd, sum(chunk_dve[:k + 1]))
            else:
                eng.wait_ge(s_pta, k + 1 - sum(chunk_dve[:k + 1]))

        PV_LAG = 2
        events = [("q", 0)]
        issued = 0
        for k, c in enumerate(chunks):
            while issued < len(jobs) and issued <= c[-1][0] + 2:
                if issued in first_job and stage_of[issued] + 1 < len(stages):
                    events.append(("q", stage_of[issued] + 1))
                events.append(("qk", issued))
                issued += 1
            events.append(("t", k))
            if k >= PV_LAG:
                events.append(("pv", k - PV_LAG))
        events += [("pv", k) for k in range(len(chunks) - PV_LAG, len(chunks))]
        turns = [e for e in events if e[0] in ("t", "q")]
        turn_of = {e: n for n, e in enumerate(turns)}

        def turn_wait(eng, e):
            if turn_of[e] >= 2:
                what, n = turns[turn_of[e] - 2]
                if what == "t":
                    pt_wait(eng, n)
                else:
                    eng.wait_ge(s_qlo, n + 1)

        def ends_set(n, pos):
            return pos + 1 == len(blocks) or set_of(jobs[blocks[pos + 1][0]]) != set_of(jobs[n])

        ended = [[] for _ in chunks]
        for pos, b in enumerate(blocks):
            if ends_set(b[0], pos):
                ended[pos // 4].append(set_no[set_of(jobs[b[0]])])
        added = [sum(st[0] != "c" for st in sets[:n + 1]) for n in range(len(sets))]

        line_parts = [(2 * NH, c, min(BANK, LINE - c)) for c in range(0, LINE, BANK)]
        line_parts += [(NH, LINE + c, min(BANK, CLINE - c)) for c in range(0, CLINE, BANK)]
        N_LINE = len(line_parts)

        first_loads = [(oh[:, 0:LINE], c_line), (oh[:, LINE:LINE + CLINE], c_cline), (rel[0:N_BUCKETS, :], rel_bias),
                       (eye[:, :], c_eye)]
        const_loads = [(bits[:, :], c_bits), (bitsi[:, :], c_bitsi),
                       (rows[:, :], c_rows), (seen[:, :], c_seen), (wup, w_kv_up_a[0]),
                       (w2[:, 0, :], w_cmp_k2[0]), (w2[:, 1, :], w_cmp_v2[0]),
                       (gain[:, G_CKV:G_CKV + 1], kv_norm_a.rearrange("a p -> p a")),
                       (gx[:, :], norm_g.rearrange("a (k p) -> p (a k)", p=P)),
                       (bgate[:, :], bass.AP(tensor=b_gate_b.tensor, offset=0, ap=[[0, P], [1, 3 * NH]]))]
        for half in range(2):
            rows_h = slice(half * HD, (half + 1) * HD)
            const_loads += [(gain[rows_h, col:col + 1], g.rearrange("a p -> p a")) for col, g in (
                (G_QA, q_norm_a), (G_KA, k_norm_a), (G_QB, q_norm_b), (G_KC, k_norm_cmp), (G_KS, k_norm_slc),
                (G_KW, k_norm_win))]
            const_loads += [(posT[rows_h, v, :], pos[0].rearrange("(jj two) d -> two d jj", two=2)[half])
                            for v, pos in enumerate((cmp_pos_k, cmp_pos_v))]
        N_FIRST, N_CONST = len(first_loads), len(const_loads)

        def key_dst(m):
            kind, t = trs[m]
            if kind == "kc":
                return kcT[:, :, :]
            return {"ks": ksT, "kw": kwT, "up": kaT}[kind][:, :, t * P:(t + 1) * P]

        def queries(kind, t):
            at = int(kind[2]) * CW
            return (qb if kind[1] == "b" else qa)[:, t, at:at + CW]

        block = ctx.enter_context(nc.Block())

        @block.sync
        def _(sp):
            for dst, src in first_loads:
                sp.dma_start(dst, src).then_inc(s_first, 16)
            for t in range(NT):
                sp.dma_start(x_in[:, t, :], x[0, t * P:(t + 1) * P, :]).then_inc(s_x[t], 16)

            def load_chunk(c):
                if c - 2 == CH_W1:
                    sp.wait_ge(s_cmp, 1)
                elif c >= 2:
                    sp.wait_ge(s_pr, last_unit[c - 2] + 1)
                if c == CH_W1:
                    for v in range(2):
                        sp.dma_start(w1[:, v, :, :], w1_src[v]).then_inc(s_w[c % 2], 16)
                else:
                    for at, col, n in chunk_loads[c]:
                        sp.dma_start(wraw[:, c % 2, 0, :, at:at + n], w_src[:, :, col:col + n]).then_inc(s_w[c % 2], 16)

            def store_z(q):
                for t in range(NT):
                    sp.wait_ge(s_pre, unit_no[(f"z{q}", t, 0)] + 1)
                    sp.dma_start(z_dram[t, :, q * CW:(q + 1) * CW], z_out[:, t % 2, :])\
                      .then_inc(s_zout[t % 2], 16)

            for c in range(N_CHUNKS):
                if c >= CH_Z2:
                    store_z(c - CH_Z2)
                load_chunk(c)
                if c == 0:
                    with nc.allow_non_contiguous_dma(reason="small vectors, once"):
                        for dst, src in const_loads:
                            sp.dma_start(dst, src).then_inc(s_const, 16)
                if c == 1:
                    sp.wait_ge(s_linesb, N_LINE)
                    sp.dma_start(line_dram, lines[:, 0:LINE].unsqueeze(1).to_broadcast([2 * NH, REP, LINE]))\
                      .then_inc(s_lined, 16)
                    sp.dma_start(cline_dram, lines[0:NH, LINE:LINE + CLINE]).then_inc(s_lined, 16)
                if c == CH_SMALL:
                    sp.wait_ge(s_pre, unit_no[("kiT", 0, 1)] + 1)
                    sp.dma_start(kiT[HD:P, :], kiT[0:HD, :]).then_inc(s_kdup, 16)
            for q in (2, 3):
                store_z(q)
            sp.wait_ge(s_lined, 32)
            sp.wait_ge(s_tre, len(trs))
            for pb in range(P // CMP_STRIDE):
                src = bass.AP(tensor=cline_dram.tensor, offset=7 - pb, ap=[[CM, CMP_STRIDE], [CLINE, NH], [1, CY]])
                sp.dma_start(strip_c[pb * CMP_STRIDE:(pb + 1) * CMP_STRIDE, :, :], src).then_inc(s_cstrip, 16)
            sp.wait_ge(s_pr, len(units))
            for b in range(2):
                sp.wait_ge(s_zout[b], 16 * 4 * NT // 2)

            def load_strip(line, heads, c0, c1, sem):
                h0, h1 = heads
                for b in range(P // REP):
                    src = bass.AP(tensor=line_dram.tensor, offset=line * REP * LINE + P - 1 - REP * b + c0,
                                  ap=[[LINE - 1, REP], [REP * LINE, h1 - h0], [1, c1 - c0]])
                    sp.dma_start(strip[b * REP:(b + 1) * REP, h0:h1, c0:c1], src).then_inc(sem, 16)

            for n, (c0, c1) in enumerate(B_PIECES):
                load_strip(NH, (0, NH), c0, c1, s_bstrip[n])
                if n == 0:
                    for t in range(NT):
                        sp.dma_start(z[:, t, :], z_dram[t]).then_inc(s_zin[t], 16)
            for g in range(NG):
                sp.wait_ge(s_lg, first_job[stages.index((False, NT - 1, g)) + 1])
                load_strip(g * HG, (g * HG, (g + 1) * HG), 0, L, s_astrip[g])
            sp.wait_ge(s_qk, FIRST_A)
            sp.dma_start(wout[:, :, :], w_out[0].rearrange("(k p) c -> p k c", p=P)).then_inc(s_wo, 16)
            sp.wait_ge(s_oe, set_no[("a", 0, 0)])
            for t in range(2):
                sp.dma_start(x_res[t], x[0, t * P:(t + 1) * P, :]).then_inc(s_xr[t], 16)
            for t in range(NT):
                sp.wait_ge(s_oadd, t + 1)
                sp.dma_start(out[0, t * P:(t + 1) * P, :], x_res[t % 2]).then_inc(s_out[t % 2], 16)
                if t + 2 < NT:
                    sp.wait_ge(s_out[t % 2], 16 * (t // 2 + 1))
                    sp.dma_start(x_res[t % 2], x[0, (t + 2) * P:(t + 3) * P, :]).then_inc(s_xr[t % 2], 16)
            for b in range(2):
                sp.wait_ge(s_out[b], 16 * NT // 2)

        @block.gpsimd
        def _(pool):
            chain = [0]

            def link(ins):
                chain[0] += 1
                ins.then_inc(s_gp, 1)
                pool.wait_ge(s_gp, chain[0])

            nc.gpsimd.memset(rel[N_BUCKETS:N_BUCKETS + 1, :], NEG).then_inc(s_ncst, 1)
            pool.wait_ge(s_ncst, 1)
            link(nc.gpsimd.memset(minus_half[:, :], -0.5))
            nc.gpsimd.memset(vc[:, :, :, :], 0.0).then_inc(s_zero, 1)
            pool.wait_ge(s_zero, 1)
            nc.gpsimd.memset(kc64, 0.0).then_inc(s_zero, 1)
            pool.wait_ge(s_zero, 2)
            pool.wait_ge(s_const, 16 * N_CONST)
            for n, col in enumerate((G_QA, G_QB)):
                nc.gpsimd.tensor_scalar(gain[:, col:col + 1], gain[:, col:col + 1], HD ** -0.5, None,
                                        ALU.mult).then_inc(s_ncst, 1)
                pool.wait_ge(s_ncst, n + 2)
            for n in range(2):
                pool.wait_ge(s_sqx, 4 * (n + 1))
                part = ssx[:, 4 * n:4 * n + 4]
                link(nc.gpsimd.tensor_scalar(part, part, 1.0 / D, EPS, ALU.mult, ALU.add))
                nc.gpsimd.tensor_tensor(part, part, minus_half[:, 0:4], ALU.pow).then_inc(s_rx, 1)

            def norm(n):
                kind, t = norms[n]
                if kind == "kc":
                    pool.wait_ge(s_cme, 4)
                else:
                    pool.wait_ge(s_pre, unit_no[("small" if kind == "ckv" else kind, t, 0)] + 1)
                if kind == "ckv":
                    ss, cols, w = ssq[:, n % 3, 0:1], ckv[:, t, :], P
                elif kind == "kc":
                    ss, cols, w = ssq[0:N_C, n % 3, 0:NG], kc, HD
                elif kind in ("ks", "kw", "up"):
                    ss, cols, w = ssq[:, n % 3, 0:NG], nat[:, n % 3, :], HD
                else:
                    ss, cols, w = ssq[:, n % 3, 0:HG], queries(kind, t), HD
                link(nc.gpsimd.tensor_scalar(ss, ss, 1.0 / w, EPS, ALU.mult, ALU.add))
                mh = minus_half[0:ss.shape[0], 0:ss.shape[1]]
                link(nc.gpsimd.tensor_tensor(ss, ss, mh, ALU.pow))
                if kind == "ckv":
                    nc.gpsimd.tensor_tensor(cols, cols, ss.to_broadcast([P, P]), ALU.mult).then_inc(s_nrm, 1)
                elif kind == "kc":
                    for two in range(2):
                        r = ss.unsqueeze(2).to_broadcast([N_C, NG, HD])
                        done = nc.gpsimd.tensor_tensor(kc[:, :, two, :], kc[:, :, two, :], r, ALU.mult)
                        if two == 0:
                            link(done)
                        else:
                            done.then_inc(s_nrm, 1)
                elif kind in ("ks", "kw", "up"):
                    v = cols.rearrange("p (g two d) -> p g two d", g=NG, two=2)
                    r = ss.unsqueeze(2).to_broadcast([P, NG, HD])
                    link(nc.gpsimd.tensor_tensor(v[:, :, 0, :], v[:, :, 0, :], r, ALU.mult))
                    nc.gpsimd.tensor_copy(v[:, :, 1, :], v[:, :, 0, :]).then_inc(s_nrm, 1)
                else:
                    v = cols.rearrange("p (h d) -> p h d", d=HD)
                    r = ss.unsqueeze(2).to_broadcast([P, CW // HD, HD])
                    nc.gpsimd.tensor_tensor(v, v, r, ALU.mult).then_inc(s_nrm, 1)
                pool.wait_ge(s_nrm, n + 1)

            def mask_diagonals(seen_value):
                pool.wait_ge(s_flip, seen_value)
                for n, i in enumerate(SEL_TILES):
                    d = score[:, SEL_OFF[n] + i * P:SEL_OFF[n] + (i + 1) * P]
                    nc.gpsimd.affine_select(out=d, in_=d, compare_op=ALU.is_ge, fill=NEG, base=0,
                                            pattern=[[-1, P]], channel_multiplier=1).then_inc(s_mask, 1)
                pool.wait_ge(s_mask, N_SEL * seen_value)

            def split(c):
                pool.wait_ge(s_whi, split_no[c] + 1)
                w = chunk_width[c]
                raw, lo, hi = wraw[:, c % 2, 0, :, 0:w], wbuf[:, c % 2, 0, :, 0:w], wbuf[:, c % 2, 1, :, 0:w]
                nc.gpsimd.tensor_tensor(lo.bitcast(F32R), raw, hi, ALU.subtract).then_inc(s_wlo, 1)
                pool.wait_ge(s_wlo, split_no[c] + 1)

            split(0)
            split(1)
            mask_after = {("unit", unit_no["ks", 1, 0]): 1, ("unit", unit_no["ks", 4, 0]): 2}
            for what, n in stage_order:
                if what == "tr" and n >= 2:
                    m = n - 2
                    pool.wait_ge(s_tre, n + 1)
                    keys = key_dst(n)[HD:P]
                    w = keys.shape[2]
                    nc.gpsimd.tensor_tensor(keys.bitcast(F32R), low[HD:P, m % 2, :, 0:w], keys,
                                            ALU.subtract).then_inc(s_low, 1)
                    pool.wait_ge(s_low, m + 1)
                elif what == "split":
                    split(n)
                elif what == "unit" and units[n][0] not in ("qiT", "kiT", "kcT", "z0", "z1", "z2", "z3"):
                    norm(norm_no[("ckv" if units[n][0] == "small" else units[n][0], units[n][1])])
                elif what == "compress_out":
                    norm(norm_no[("kc", 0)])
                if (what, n) in mask_after:
                    mask_diagonals(mask_after[what, n])
            def dup(m):
                if m:
                    pool.wait_ge(s_qt, m)
                is_a, i, g = stages[m]
                q = (qa if is_a else qb)[:, i, g * CW:(g + 1) * CW].rearrange("p (h d) -> p h d", h=HG)
                nc.gpsimd.tensor_copy(q_dup[:, :, :, :], q.unsqueeze(2).to_broadcast([P, HG, 2, HD])).then_inc(s_dup, 1)
                pool.wait_ge(s_dup, m + 1)

            def add_up(s):
                br, i, g = sets[s]
                c0 = g * CW + (0 if br == "a" else BANK)
                zy = z[:, i, c0:c0 + CW]
                if br == "c":
                    return
                pool.wait_ge(s_oe, s + 1)
                if br == "s":
                    nc.gpsimd.tensor_tensor(o_acc, o_acc, head_o[s % 2], ALU.add).then_inc(s_fin, 1)
                elif br == "w":
                    link(nc.gpsimd.tensor_tensor(o_acc, o_acc, head_o[s % 2], ALU.add))
                    pool.wait_ge(s_zin[i], 16)
                    nc.gpsimd.tensor_tensor(zy, zy, o_acc, ALU.mult).then_inc(s_fin, 1)
                else:
                    nc.gpsimd.tensor_tensor(zy, zy, head_o[s % 2], ALU.mult).then_inc(s_fin, 1)
                pool.wait_ge(s_fin, added[s])

            def make_masks():
                for b in range(2):
                    pool.wait_ge(s_zout[b], 16 * 4 * NT // 2)
                nc.gpsimd.memset(eyeb[:, :], 0.0).then_inc(s_masks, 1)
                pool.wait_ge(s_masks, 1)
                nc.gpsimd.memset(winb[:, :], 0.0).then_inc(s_masks, 1)
                pool.wait_ge(s_masks, 2)
                nc.gpsimd.affine_select(out=eyeb[:, :], in_=eyeb[:, :], compare_op=ALU.not_equal, fill=1.0, base=0,
                                        pattern=[[-1, P]], channel_multiplier=1).then_inc(s_masks, 1)
                pool.wait_ge(s_masks, 3)
                nc.gpsimd.affine_select(out=winb[:, :], in_=winb[:, :], compare_op=ALU.is_gt, fill=NEG, base=0,
                                        pattern=[[1, P]], channel_multiplier=-1).then_inc(s_masks, 1)
                pool.wait_ge(s_masks, 4)

            pool.wait_ge(s_sel, 1)
            dup(0)
            for what, n in events:
                if what == "q" and n + 1 < len(stages):
                    dup(n + 1)
                    if n == 1:
                        make_masks()
                elif what == "pv":
                    for s in ended[n]:
                        add_up(s)

        @block.scalar
        def _(act):
            sqo = [0]

            def squares(src, ss, w):
                if sqo[0] >= 2:
                    act.wait_ge(s_sqo, sqo[0] - 1)
                nc.scalar.activation(junk[0:src.shape[0], sqo[0] % 2, 0:w], src, ACT.Square,
                                     accum_out=ss).then_inc(s_sqo, 1)
                sqo[0] += 1

            for t in range(NT):
                act.wait_ge(s_x[t], 16)
                if t >= 2:
                    act.wait_ge(s_sqx, t - 1)
                nc.scalar.activation(square[t % 2], x_in[:, t, :], ACT.Square,
                                     accum_out=ssx[:, t:t + 1]).then_inc(s_sqx, 1)
            act.wait_ge(s_const, 16 * N_CONST)
            act.wait_ge(s_ncst, 3)

            def split(c):
                act.wait_ge(s_w[c % 2], chunk_arrived(c))
                w = chunk_width[c]
                nc.scalar.activation(wbuf[:, c % 2, 1, :, 0:w].bitcast(F32R), wraw[:, c % 2, 0, :, 0:w],
                                     ACT.Copy).then_inc(s_whi, 1)

            split(0)
            for c in range(2 * KT):
                act.wait_ge(s_ht, c + 1)
                half, k = divmod(c, KT)
                nc.scalar.activation(hT_hi[:, k, half * BANK:(half + 1) * BANK].bitcast(F32R), ps[:, c % 8, :], ACT.Copy,
                                     scale=gx[:, k:k + 1]).then_inc(s_hact, 1)
            split(1)

            def free_nat(n):
                if n >= 3 and norms[n - 3][0] in ("ks", "kw", "up"):
                    act.wait_ge(s_tr, tr_no[norms[n - 3]] + 1)
                elif n >= 3:
                    act.wait_ge(s_nrm, n - 2)

            def unit(u):
                kind, a, half = units[u]
                act.wait_ge(s_pr, u + 1)
                bank = ps[:, u % 4, :]
                if kind == "qiT":
                    nc.scalar.activation(qiT[:, a, half * BANK:(half + 1) * BANK], bank, ACT.Copy).then_inc(s_pre, 1)
                elif kind == "kiT":
                    nc.scalar.activation(kiT[0:HD, half * BANK:(half + 1) * BANK], bank[0:HD, :],
                                         ACT.Copy).then_inc(s_pre, 1)
                elif kind == "small":
                    n = norm_no[("ckv", a)]
                    free_nat(n)
                    squares(bank[:, 0:P], ssq[:, n % 3, 0:1], P)
                    nc.scalar.activation(ckv[:, a, :], bank[:, 0:P], ACT.Copy)
                    nc.scalar.activation(widx[:, a, :], bank[:, P:P + NH], ACT.Copy, scale=NH ** -0.5)
                    nc.scalar.activation(gates[:, a, :], bank[:, P + NH:P + NH + 3 * NH], ACT.Copy).then_inc(s_pre, 1)
                elif kind in ("ks", "kw", "up"):
                    n = norm_no[(kind, a)]
                    free_nat(n)
                    for g in range(NG):
                        squares(bank[:, g * HD:(g + 1) * HD], ssq[:, n % 3, g:g + 1], HD)
                    nc.scalar.activation(nat[:, n % 3, :].rearrange("p (g two d) -> p g two d", g=NG, two=2)[:, :, 0, :],
                                         bank[:, 0:P].rearrange("p (g d) -> p g d", g=NG), ACT.Copy)
                    nc.scalar.activation({"ks": vs, "kw": vw, "up": va}[kind][:, a, :], bank[:, P:2 * P],
                                         ACT.Copy).then_inc(s_pre, 1)
                elif kind == "kcT":
                    for g in range(NG):
                        rows_g = slice(g * HD, (g + 1) * HD)
                        nc.scalar.activation(kcT_raw[0:HD, a, g, half * BANK:(half + 1) * BANK], bank[rows_g, :], ACT.Copy)
                        ahead = 1 if half == 0 else 0
                        last = nc.scalar.activation(kcT_raw[HD:P, a, g, half * BANK - 1 + ahead:(half + 1) * BANK - 1],
                                                    bank[rows_g, ahead:], ACT.Copy)
                    last.then_inc(s_pre, 1)
                elif kind[0] == "q":
                    n = norm_no[(kind, a)]
                    free_nat(n)
                    for h in range(CW // HD):
                        squares(bank[:, h * HD:(h + 1) * HD], ssq[:, n % 3, h:h + 1], HD)
                    nc.scalar.activation(queries(kind, a), bank[:, 0:CW], ACT.Copy).then_inc(s_pre, 1)
                else:
                    stores = int(kind[1]) * NT + a
                    if stores >= 2:
                        act.wait_ge(s_zout[a % 2], 16 * (stores // 2))
                    nc.scalar.activation(z_out[:, a % 2, :], bank[:, 0:CW], ACT.Silu).then_inc(s_pre, 1)

            def tr_out(m):
                kind, t = trs[m]
                act.wait_ge(s_tr, m + 1)
                bank = ps[:, 4 + m % 4, :]
                if kind == "ckvT":
                    nc.scalar.activation(ckvT[:, t * BANK:(t + 1) * BANK], bank, ACT.Copy,
                                         scale=gain[:, G_CKV:G_CKV + 1]).then_inc(s_tre, 1)
                    return
                if m == 2:
                    act.wait_ge(s_acc, len(sjobs))
                if m >= 4:
                    act.wait_ge(s_low, m - 3)
                dst = key_dst(m)
                w = dst.shape[2]
                src = bank.rearrange("p (m t) -> p m t", m=4)[:, 0:2, 0:w]
                g = {"kc": G_KC, "ks": G_KS, "kw": G_KW, "up": G_KA}[kind]
                nc.scalar.activation(low[HD:P, m % 2, :, 0:w], src[HD:P], ACT.Copy, scale=gain[HD:P, g:g + 1])
                nc.scalar.activation(dst.bitcast(F32R), src, ACT.Copy, scale=gain[:, g:g + 1]).then_inc(s_tre, 1)

            def compress_steps():
                act.wait_ge(s_cmp, 1)
                nc.scalar.activation(hid_c[:, :], ps[0:HD, 6:8, 256], ACT.Copy).then_inc(s_cme, 1)
                act.wait_ge(s_cme, 1)
                for v in range(2):
                    nc.scalar.activation(hid[:, v * NG:(v + 1) * NG, 0:N_C],
                                         ps[0:HD, 6 + v, 0:2 * N_C].rearrange("p (g c) -> p g c", g=NG),
                                         ACT.Gelu_apprx_tanh, bias=hid_c[:, v:v + 1]).then_inc(s_cme, 1)

            def compress_results():
                act.wait_ge(s_cmp, 2)
                n = norm_no[("kc", 0)]
                free_nat(n)
                src = ps[0:N_C, 6, :]
                for g in range(NG):
                    squares(src[:, g * HD:(g + 1) * HD], ssq[0:N_C, n % 3, g:g + 1], HD)
                act.wait_ge(s_zero, 2)
                for two in range(2):
                    nc.scalar.activation(kc[:, :, two, :], src[:, 0:P].rearrange("p (g d) -> p g d", g=NG), ACT.Copy)
                for two in range(2):
                    r = slice(two * HD, two * HD + N_C)
                    last = nc.scalar.activation(vc[r, :, two, :], ps[r, 6, P:2 * P].rearrange("p (g d) -> p g d", g=NG),
                                                ACT.Copy)
                last.then_inc(s_cme, 1)

            def score_relu(n):
                i, h = sjobs[n]
                act.wait_ge(s_sc, n + 1)
                if n >= 2:
                    act.wait_ge(s_acc, n - 1)
                w = P * (i + 1)
                nc.scalar.activation(relu[:, n % 2, 0:w],
                                     ps[:, 4 + 2 * (n % 2):6 + 2 * (n % 2), :].rearrange("p b c -> p (b c)")[:, 0:w],
                                     ACT.Relu, scale=HD ** -0.5).then_inc(s_relu, 1)

            for step in stage_order:
                what, n = step
                if what == "unit":
                    unit(n)
                elif what == "tr":
                    tr_out(n)
                elif what == "score":
                    score_relu(n)
                elif what == "compress":
                    compress_steps()
                elif what == "compress_out":
                    compress_results()
                elif what == "split":
                    split(n)
            act.wait_ge(s_gate, 1)
            nc.scalar.activation(gates[:, :, :], gates[:, :, :], ACT.Sigmoid).then_inc(s_gate, 1)

            for what, n in events:
                if what == "qk":
                    br, i, h = jobs[n]
                    act.wait_ge(s_lg, n + 1)
                    s = set_no[set_of(jobs[n])]
                    if br == "c":
                        v = soft[:, n % 4, 0:CW].rearrange("p (h c) -> p h c", h=HG)[:, :, 0:N_C]
                        nc.scalar.activation(v, v, ACT.Exp).then_inc(s_ex, 1)
                    else:
                        w = P * (i + 1 - first_block(jobs[n]))
                        if s >= 4 and h % HG == 0:
                            act.wait_ge(s_oe, s - 3)
                        nc.scalar.activation(soft[:, n % 4, 0:w], soft[:, n % 4, 0:w], ACT.Exp, scale=-1.0,
                                             bias=nmax[:, n % 4, 0:1],
                                             accum_out=rsum[:, s % 4, h % HG:h % HG + 1]).then_inc(s_ex, 1)
                elif what == "q":
                    act.wait_ge(s_qt, n + 1)
                    if n >= 2:
                        act.wait_ge(s_qk, first_job[n - 1])
                    g = G_QA if stages[n][0] else G_QB
                    nc.scalar.activation(q_st[:, n % 2, 0, :, :].rearrange("p h t -> p (h t)").bitcast(F32R),
                                         ps[:, 4 + turn_of[what, n] % 2, :], ACT.Copy,
                                         scale=gain[:, g:g + 1]).then_inc(s_qhi, 1)
                elif what == "t" and not chunk_dve[n]:
                    act.wait_ge(s_t, n + 1)
                    if n >= 3:
                        act.wait_ge(s_pv, n - 2)
                    nc.scalar.activation(probT[:, n % 3, :], ps[:, 4 + turn_of[what, n] % 2, :], ACT.Copy).then_inc(s_pta, 1)
            for t in range(NT):
                act.wait_ge(s_yt, 2 * t + 1)
                if t >= 2:
                    act.wait_ge(s_op, t - 1)
                nc.scalar.activation(yT[:, t % 2, 0:4, :], ps[:, 4 + 2 * (t % 2), :].rearrange("p (k t) -> p k t", k=4),
                                     ACT.Copy).then_inc(s_yta, 1)

        @block.vector
        def _(dve):
            chain = [0]

            def link(ins):
                chain[0] += 1
                ins.then_inc(s_dv, 1)
                dve.wait_ge(s_dv, chain[0])

            for n, (m, at, cn) in enumerate(line_parts):
                dve.wait_ge(s_line, n + 1)
                nc.vector.tensor_copy(lines[0:m, at:at + cn], ps[0:m, n, 0:cn]).then_inc(s_linesb, 1)
            for t in range(NT):
                dve.wait_ge(s_rx, t // 4 + 1)
                nc.vector.tensor_scalar(x_in[:, t, :], x_in[:, t, :], ssx[:, t:t + 1], None, ALU.mult).then_inc(s_h, 1)
            for c in range(2 * KT):
                dve.wait_ge(s_hact, c + 1)
                half, k = divmod(c, KT)
                nc.vector.scalar_tensor_tensor(
                    out=hT_lo[:, 4 * half:4 * half + 4, k, :].bitcast(F32R),
                    in0=ps[:, c % 8, :].rearrange("p (t c) -> p t c", t=4), scalar=gx[:, k:k + 1],
                    in1=hT_hi[:, k, half * BANK:(half + 1) * BANK].rearrange("p (t c) -> p t c", t=4),
                    op0=ALU.mult, op1=ALU.subtract).then_inc(s_hdve, 1)
            dve.wait_ge(s_pre, N_EARLY)
            nc.vector.tensor_tensor(gates[:, :, :], gates[:, :, :],
                                    bgate[:, :].unsqueeze(1).to_broadcast([P, NT, 3 * NH]), ALU.add).then_inc(s_gate, 1)
            dve.wait_ge(s_lined, 32)
            for n, (i, h) in enumerate(sjobs):
                o = SEL_OFF[i - T_SEL]
                w = P * (i + 1)
                y = score[:, o:o + w]
                dve.wait_ge(s_relu, n + 1)
                if h == 0:
                    nc.vector.tensor_scalar(y, relu[:, n % 2, 0:w], widx[:, i, h:h + 1], None, ALU.mult).then_inc(s_acc, 1)
                else:
                    dve.wait_ge(s_acc, n)
                    nc.vector.scalar_tensor_tensor(out=y, in0=relu[:, n % 2, 0:w], scalar=widx[:, i, h:h + 1], in1=y,
                                                   op0=ALU.mult, op1=ALU.add).then_inc(s_acc, 1)
            dve.wait_ge(s_acc, len(sjobs))
            nc.vector.memset(cur[:, :], 0).then_inc(s_flip, 1)
            dve.wait_ge(s_mask, N_SEL)

            def count(op, at, out, start=None):
                for n in range(N_SEL):
                    w = SEL_W[n]
                    if n >= 2:
                        dve.wait_ge(s_dv, chain[0] - 1)
                    chain[0] += 1
                    nc.vector.tensor_scalar(mark[n % 2][:, 0:w], score[:, SEL_OFF[n]:SEL_OFF[n] + w],
                                            0.0 if at is None else at[:, n:n + 1],
                                            None if start is None else start[:, n:n + 1],
                                            op, ALU.add, accum_out=out[:, n:n + 1]).then_inc(s_dv, 1)
                dve.wait_ge(s_dv, chain[0])

            count(ALU.is_ge, None, cnt)
            link(nc.vector.tensor_scalar(ispos[:, :], cnt[:, :], float(TOPK), None, ALU.is_ge))
            link(nc.vector.tensor_scalar(sgn[:, :], ispos[:, :], 2.0, -1.0, ALU.mult, ALU.add))
            link(nc.vector.tensor_scalar(kth[:, :], ispos[:, :], -1.0, 1.0, ALU.mult, ALU.add))
            link(nc.vector.tensor_tensor(kth[:, :], kth[:, :], rows[:, :], ALU.mult))
            link(nc.vector.tensor_scalar(kth[:, :], kth[:, :], float(TOPK), None, ALU.add))
            link(nc.vector.tensor_scalar(nkth[:, :], kth[:, :], -1.0, None, ALU.mult))
            for n in range(N_SEL):
                y = score[:, SEL_OFF[n]:SEL_OFF[n + 1]]
                last = nc.vector.tensor_scalar(y, y, sgn[:, n:n + 1], None, ALU.mult)
                if n < N_SEL - 1:
                    link(last)
            last.then_inc(s_flip, 1)
            dve.wait_ge(s_mask, 2 * N_SEL)

            base = chain[0]
            steps = N_SEL + 3
            with dve.Fori(0, N_BITS) as bit:
                dve.wait_ge(s_dv, steps * bit + base)
                nc.vector.tensor_tensor(cand[:, :], cur[:, :],
                                        bitsi[:, bass.ds(bit, 1)].to_broadcast([P, N_SEL]),
                                        ALU.bitwise_or).then_inc(s_dv, 1)
                dve.wait_ge(s_dv, steps * bit + base + 1)
                for n in range(N_SEL):
                    w = SEL_W[n]
                    if n >= 2:
                        dve.wait_ge(s_dv, steps * bit + base + n)
                    nc.vector.tensor_scalar(mark[n % 2][:, 0:w], score[:, SEL_OFF[n]:SEL_OFF[n] + w],
                                            cand[:, n:n + 1].bitcast(F32), nkth[:, n:n + 1], ALU.is_ge, ALU.add,
                                            accum_out=cnt[:, n:n + 1]).then_inc(s_dv, 1)
                dve.wait_ge(s_dv, steps * bit + base + N_SEL + 1)
                nc.vector.tensor_scalar(keep[:, :], cnt[:, :], 0.0, bits[:, bass.ds(bit, 1)], ALU.is_ge,
                                        ALU.mult).then_inc(s_dv, 1)
                dve.wait_ge(s_dv, steps * bit + base + N_SEL + 2)
                nc.vector.tensor_tensor(cur[:, :], cur[:, :], keep[:, :], ALU.bitwise_or).then_inc(s_dv, 1)
            chain[0] += steps * N_BITS
            dve.wait_ge(s_dv, chain[0])

            mag = cur[:, :].bitcast(F32)
            count(ALU.is_ge, mag, cnt)
            count(ALU.is_gt, mag, cnt2)
            link(nc.vector.tensor_tensor(cnt2[:, :], kth[:, :], cnt2[:, :], ALU.subtract))
            link(nc.vector.tensor_tensor(cnt[:, :], cnt[:, :], kth[:, :], ALU.subtract))
            link(nc.vector.tensor_scalar(cnt[:, :], cnt[:, :], 1.0, None, ALU.add))
            link(nc.vector.tensor_tensor(cnt2[:, :], cnt2[:, :], cnt[:, :], ALU.subtract))
            link(nc.vector.tensor_tensor(cnt2[:, :], cnt2[:, :], ispos[:, :], ALU.mult))
            link(nc.vector.tensor_tensor(need[:, :], cnt2[:, :], cnt[:, :], ALU.add))
            link(nc.vector.tensor_tensor(thr[:, :], mag, sgn[:, :], ALU.mult))
            for n in range(N_SEL):
                w = SEL_W[n]
                y = score[:, SEL_OFF[n]:SEL_OFF[n] + w]
                link(nc.vector.tensor_scalar(tie[:, 0:w], y, mag[:, n:n + 1], None, ALU.is_equal))
                link(nc.vector.tensor_tensor_scan(ties_to[:, 0:w], tie[:, 0:w], tie[:, 0:w], 0.0, ALU.add, ALU.max))
                link(nc.vector.scalar_tensor_tensor(out=tie[:, 0:w], in0=ties_to[:, 0:w], scalar=need[:, n:n + 1],
                                                    in1=tie[:, 0:w], op0=ALU.is_gt, op1=ALU.is_ge))
                link(nc.vector.tensor_scalar(unsel[:, 0:w], y, sgn[:, n:n + 1], thr[:, n:n + 1], ALU.mult, ALU.is_le))
                link(nc.vector.scalar_tensor_tensor(out=selmask[:, SEL_OFF[n]:SEL_OFF[n] + w], in0=unsel[:, 0:w],
                                                    scalar=NEG, in1=tie[:, 0:w], op0=ALU.mult, op1=ALU.mult))
            nc.vector.tensor_copy(need[:, :], cnt[:, :]).then_inc(s_sel, 1)

            for b in range(4):
                link(nc.vector.memset(soft[:, b, 0:CW], 0.0))
            dve.wait_ge(s_gate, 2)
            link(nc.vector.tensor_scalar(gates[:, 0, :].rearrange("p (h b) -> p h b", b=3)[:, :, 0],
                                         gates[:, 0, :].rearrange("p (h b) -> p h b", b=3)[:, :, 0],
                                         seen[:, 0:1], None, ALU.mult))

            def finish(s, k):
                br, i, g = sets[s]
                r = rinv[:, s % 2, :]
                if br == "a":
                    link(nc.vector.reciprocal(r, rsum[:, s % 4, :]))
                else:
                    gate = gates[:, i, :].rearrange("p (h b) -> p h b", b=3)[:, g * HG:(g + 1) * HG, "csw".index(br)]
                    link(nc.vector.reciprocal(r, rsum[:, s % 4, :]))
                    link(nc.vector.tensor_tensor(r, r, gate, ALU.mult))
                if br == "c":
                    dst, o_ps = o_acc, ps[:, 6 + s % 2, 0:CW].rearrange("p (h d) -> p h d", h=HG)
                    if s:
                        dve.wait_ge(s_fin, added[s - 1])
                else:
                    dst = head_o[s % 2]
                    o_ps = ps[:, 6 + s % 2, :].rearrange("p (h g d) -> p h g d", h=HG, g=NG)[:, :, g, :]
                    if s >= 2 and added[s - 2]:
                        dve.wait_ge(s_fin, added[s - 2])
                dve.wait_ge(s_pv, k + 1)
                nc.vector.tensor_tensor(dst.rearrange("p (h d) -> p h d", h=HG), o_ps,
                                        r.unsqueeze(2).to_broadcast([P, HG, HD]), ALU.mult).then_inc(s_oe, 1)

            for what, n in events:
                if what == "qk":
                    br, i, h = jobs[n]
                    if n >= 3 and jobs[n - 3][0] == "c":
                        m = n - 3
                        dve.wait_ge(s_ex, m + 1)
                        lg = soft[:, m % 4, 0:CW].rearrange("p (h c) -> p h c", h=HG)[:, :, 0:N_C]
                        link(nc.vector.tensor_reduce(rsum[:, set_no[set_of(jobs[m])] % 4, 0:HG], lg, AX.X, ALU.add))
                    dve.wait_ge(s_qk, n + 1)
                    if n >= 4:
                        dve.wait_ge(s_t, last_chunk[n - 4] + 1)
                    if n == 0:
                        dve.wait_ge(s_cstrip, 16 * (P // CMP_STRIDE))
                    if h == 0 and br == "s":
                        for m, (c0, c1) in enumerate(B_PIECES):
                            if c1 == L - i * P:
                                dve.wait_ge(s_bstrip[m], 16 * (P // REP))
                    if br == "a" and i == 0 and h % HG == 0:
                        dve.wait_ge(s_astrip[h // HG], 16 * (P // REP))
                    slot = ps[:, 2 * (n % 2):2 * (n % 2) + 2, :].rearrange("p b c -> p (b c)")
                    if br == "c":
                        c0 = (P // CMP_STRIDE) * (NT - 1 - i)
                        lg = soft[:, n % 4, 0:CW].rearrange("p (h c) -> p h c", h=HG)[:, :, 0:N_C]
                        link(nc.vector.tensor_tensor(lg, slot[:, 0:CW].rearrange("p (h c) -> p h c", h=HG)[:, :, 0:N_C],
                                                     strip_c[:, h:h + HG, c0:c0 + N_C], ALU.add))
                        link(nc.vector.tensor_reduce(nmax[:, n % 4, 0:HG], lg, AX.X, ALU.max, negate=True))
                        nc.vector.tensor_tensor(lg, lg, nmax[:, n % 4, 0:HG].unsqueeze(2).to_broadcast([P, HG, N_C]),
                                                ALU.add).then_inc(s_lg, 1)
                    else:
                        w = P * (i + 1 - first_block(jobs[n]))
                        nc.vector.tensor_tensor_reduce(out=soft[:, n % 4, 0:w], in0=slot[:, 0:w],
                                                       in1=strip[:, h, L - w:L], scale=-1.0, scalar=3e38, op0=ALU.add,
                                                       op1=ALU.min, accum_out=nmax[:, n % 4, 0:1]).then_inc(s_lg, 1)
                elif what == "t":
                    k = n
                    if chunk_dve[k]:
                        dve.wait_ge(s_t, k + 1)
                        if k >= 3:
                            dve.wait_ge(s_pv, k - 2)
                        nc.vector.tensor_copy(probT[:, k % 3, :], ps[:, 4 + turn_of[what, k] % 2, :]).then_inc(s_ptd, 1)
                elif what == "q":
                    dve.wait_ge(s_qhi, n + 1)
                    g = G_QA if stages[n][0] else G_QB
                    nc.vector.scalar_tensor_tensor(
                        out=q_st[:, n % 2, 1, :, :].rearrange("p h t -> p (h t)").bitcast(F32R),
                        in0=ps[:, 4 + turn_of[what, n] % 2, :], scalar=gain[:, g:g + 1],
                        in1=q_st[:, n % 2, 0, :, :].rearrange("p h t -> p (h t)"), op0=ALU.mult,
                        op1=ALU.subtract).then_inc(s_qlo, 1)
                else:
                    for s in ended[n]:
                        finish(s, n)
            def add_x(t):
                dve.wait_ge(s_op, t + 1)
                dve.wait_ge(s_xr[t % 2], 16 * (t // 2 + 1))
                nc.vector.tensor_tensor(x_res[t % 2], ps[:, 2 * (t % 2):2 * (t % 2) + 2, :].rearrange("p b c -> p (b c)"),
                                        x_res[t % 2], ALU.add).then_inc(s_oadd, 1)

            for t in range(NT):
                dve.wait_ge(s_yt, 2 * t + 2)
                if t >= 2:
                    dve.wait_ge(s_op, t - 1)
                nc.vector.tensor_copy(yT[:, t % 2, 4:8, :],
                                      ps[:, 5 + 2 * (t % 2), :].rearrange("p (k t) -> p k t", k=4)).then_inc(s_ytd, 1)
                if t:
                    add_x(t - 1)
            add_x(NT - 1)

        @block.tensor
        def _(pe):
            mm = nc.tensor.matmul
            pe.wait_ge(s_first, 16 * N_FIRST)
            pe.wait_ge(s_ncst, 1)
            for n, (m, at, cn) in enumerate(line_parts):
                lhs = rel[:, :] if m == 2 * NH else rel[:, NH:2 * NH]
                mm(ps[0:m, n, 0:cn], lhs, oh[:, at:at + cn], start=True, stop=True).then_inc(s_line, 1)
            pe.wait_ge(s_linesb, N_LINE)
            for c in range(2 * KT):
                half, k = divmod(c, KT)
                if k == 0:
                    pe.wait_ge(s_h, 4 * (half + 1))
                if c >= 8:
                    pe.wait_ge(s_hdve, c - 7)
                for t in range(4):
                    last = nc.tensor.transpose(ps[:, c % 8, t * P:(t + 1) * P],
                                               x_in[:, half * 4 + t, k * P:(k + 1) * P], eye[:, :])
                last.then_inc(s_ht, 1)
            pe.wait_ge(s_hdve, 2 * KT)

            def unit(u):
                kind, a, half = units[u]
                if u >= 4:
                    pe.wait_ge(s_pre, u - 3)
                if kind == "up":
                    if a == 0:
                        pe.wait_ge(s_tre, 2)
                    mm(ps[:, u % 4, 0:2 * P], ckvT[:, a * P:(a + 1) * P], wup[:, :], start=True, stop=True).then_inc(s_pr, 1)
                    return
                ch = chunk_of(units[u])
                if u == first_unit[ch]:
                    pe.wait_ge(s_whi, split_no[ch] + 1)
                for n, (wp, hp) in enumerate(((1, 1), (1, 0), (0, 1))):
                    if n == 2 and u == first_unit[ch]:
                        pe.wait_ge(s_wlo, split_no[ch] + 1)
                    for k in range(KT):
                        begin, end = n == 0 and k == 0, n == 2 and k == KT - 1
                        if kind in ("qiT", "kiT", "kcT"):
                            w = wbuf[:, ch % 2, wp, k, (a % 2) * P:(a % 2 + 1) * P]
                            if hp:
                                h = hT_hi[:, k, half * BANK:(half + 1) * BANK]
                            else:
                                h = hT_lo[:, 4 * half:4 * half + 4, k, :]
                            last = mm(ps[:, u % 4, :], w.bitcast(F32R), h.bitcast(F32R), start=begin, stop=end)
                        else:
                            c0, cn = (SMALL_AT, SMALL_W) if kind == "small" else (0, CW)
                            h = hT_hi[:, k, a * P:(a + 1) * P] if hp else hT_lo[:, a, k, :]
                            w = wbuf[:, ch % 2, wp, k, c0:c0 + cn]
                            last = mm(ps[:, u % 4, 0:cn], h.bitcast(F32R), w.bitcast(F32R), start=begin, stop=end)
                last.then_inc(s_pr, 1)

            def score_dots(n):
                i, h = sjobs[n]
                if n == 0:
                    pe.wait_ge(s_pre, unit_no[("small", 0, 0)])
                    pe.wait_ge(s_kdup, 16)
                if n >= 2:
                    pe.wait_ge(s_relu, n - 1)
                r = slice(HD * (h % 2), HD * (h % 2) + HD)
                w = P * (i + 1)
                for b in range(0, w, BANK):
                    cn = min(BANK, w - b)
                    last = mm(ps[:, 4 + 2 * (n % 2) + b // BANK, 0:cn], qiT[r, h // 2, i * P:(i + 1) * P], kiT[r, b:b + cn],
                              start=True, stop=True)
                last.then_inc(s_sc, 1)

            def tr(m):
                kind, t = trs[m]
                if m >= 4:
                    pe.wait_ge(s_tre, m - 3)
                if m == 0:
                    pe.wait_ge(s_relu, len(sjobs))
                if m == trs_before_cmp:
                    pe.wait_ge(s_cme, 4)
                if kind == "ckvT":
                    pe.wait_ge(s_nrm, 4 * (t + 1))
                    for n in range(4):
                        last = nc.tensor.transpose(ps[:, 4 + m % 4, n * P:(n + 1) * P], ckv[:, 4 * t + n, :], eye[:, :])
                else:
                    n = norm_no[(kind, t)]
                    pe.wait_ge(s_nrm, n + 1)
                    if kind == "kc":
                        for g in range(NG):
                            last = nc.tensor.transpose(ps[:, 4 + m % 4, g * P:g * P + HD], kc64[:, g * P:(g + 1) * P],
                                                       eye[0:HD, 0:HD])
                    else:
                        for b in range(2):
                            last = nc.tensor.transpose(ps[:, 4 + m % 4, b * P:(b + 1) * P], nat[:, n % 3, b * P:(b + 1) * P],
                                                       eye[:, :])
                last.then_inc(s_tr, 1)

            def compress():
                pe.wait_ge(s_w[CH_W1 % 2], chunk_arrived(CH_W1))
                pe.wait_ge(s_pre, unit_no[("kcT", 1, 1)] + 1)
                pe.wait_ge(s_tre, trs_before_cmp)
                for v in range(2):
                    for j in range(JJ):
                        mm(ps[0:HD, 6 + v, 256:257], w1[:, v, j, :], posT[:, v, j:j + 1], start=(j == 0),
                           stop=(j == JJ - 1))
                    for j in range(JJ):
                        t0 = 2 * j
                        last = mm(ps[0:HD, 6 + v, 0:2 * N_C], w1[:, v, j, :],
                                  kcT_raw[:, v, :, t0:t0 + CMP_STRIDE * (N_C - 1) + 1:CMP_STRIDE],
                                  start=(j == 0), stop=(j == JJ - 1))
                last.then_inc(s_cmp, 1)

            def compress_out():
                pe.wait_ge(s_cme, 3)
                for v in range(2):
                    for g in range(NG):
                        for at in (0, HD)[0:1 + v]:
                            last = mm(ps[at:at + N_C, 6, (v * NG + g) * HD:(v * NG + g + 1) * HD],
                                      hid[:, v * NG + g, 0:N_C], w2[:, v, :], start=True, stop=True)
                last.then_inc(s_cmp, 1)

            for what, n in stage_order:
                if what == "unit":
                    unit(n)
                elif what == "tr":
                    tr(n)
                elif what == "score":
                    score_dots(n)
                elif what == "compress":
                    compress()
                elif what == "compress_out":
                    compress_out()

            pe.wait_ge(s_pre, len(units))
            pe.wait_ge(s_tre, len(trs))
            pe.wait_ge(s_low, KEY_TRS)
            v_of = {"s": vs, "w": vw, "a": va}
            for what, n in events:
                if what == "qk":
                    br, i, h = jobs[n]
                    if n >= 2:
                        pe.wait_ge(s_lg, n - 1)
                    if n == FIRST_A:
                        pe.wait_ge(s_sel, 1)
                    if n == first_windowed:
                        pe.wait_ge(s_masks, 4)
                    b0 = 2 * (n % 2)
                    m = stage_of[n]
                    if n == first_job[m]:
                        pe.wait_ge(s_qlo, m + 1)
                    if br == "c":
                        for q in range(HG):
                            for part in range(2):
                                last = mm(ps[:, b0, q * HD:(q + 1) * HD], q_st[:, m % 2, part, q, :].bitcast(F32R),
                                          kcT[:, h // HG, :].bitcast(F32R), start=(part == 0), stop=(part == 1))
                        last.then_inc(s_qk, 1)
                        continue
                    kT = {"a": kaT, "s": ksT, "w": kwT}[br]
                    k0 = first_block(jobs[n]) * P
                    w = (i + 1) * P - k0
                    for b in range(0, w, BANK):
                        cn = min(BANK, w - b)
                        dst = ps[:, b0 + b // BANK, 0:cn]
                        masked = br == "a" and i >= T_SEL or br == "w" and i >= WB and b == 0
                        for part in range(2):
                            last = mm(dst, q_st[:, m % 2, part, h % HG, :].bitcast(F32R),
                                      kT[:, h // HG, k0 + b:k0 + b + cn].bitcast(F32R), start=(part == 0),
                                      stop=(part == 1 and not masked))
                        if br == "a" and i >= T_SEL:
                            o = SEL_OFF[i - T_SEL] + b
                            last = mm(dst, eyeb[:, :], selmask[:, o:o + cn], start=False, stop=True)
                        elif br == "w" and i >= WB and b == 0:
                            last = mm(dst[:, 0:P], eyeb[:, :], winb[:, :], start=False, stop=True)
                    last.then_inc(s_qk, 1)
                elif what == "t":
                    pe.wait_ge(s_ex, chunks[n][-1][0] + 1)
                    turn_wait(pe, (what, n))
                    for q, (jn, h, j) in enumerate(chunks[n]):
                        dst = ps[:, 4 + turn_of[what, n] % 2, q * P:(q + 1) * P]
                        c0 = h * P if jobs[jn][0] == "c" else (j - first_block(jobs[jn])) * P
                        last = nc.tensor.transpose(dst, soft[:, jn % 4, c0:c0 + P], eye[:, :])
                    last.then_inc(s_t, 1)
                elif what == "q":
                    pe.wait_ge(s_dup, n + 1)
                    turn_wait(pe, (what, n))
                    for q in range(HG):
                        last = nc.tensor.transpose(ps[:, 4 + turn_of[what, n] % 2, q * P:(q + 1) * P],
                                                   q_dup[:, q, :, :].rearrange("p two d -> p (two d)"), eye[:, :])
                    last.then_inc(s_qt, 1)
                else:
                    pt_wait(pe, n)
                    for q, (jn, h, j) in enumerate(chunks[n]):
                        br, i, _ = jobs[jn]
                        s = set_no[set_of(jobs[jn])]
                        first = j == first_block(jobs[jn])
                        if first and h % HG == 0 and s >= 2:
                            pe.wait_ge(s_oe, s - 1)
                        cols = slice(q * P, (q + 1) * P)
                        if br == "c":
                            last = mm(ps[:, 6 + s % 2, h * P:(h + 1) * P], probT[:, n % 3, cols],
                                      vc[:, jobs[jn][2] // HG, :, :].rearrange("p two d -> p (two d)"), start=True, stop=True)
                        else:
                            hc = slice((h % HG) * P, (h % HG + 1) * P)
                            last = mm(ps[:, 6 + s % 2, hc], probT[:, n % 3, cols], v_of[br][:, j, :],
                                      start=first, stop=(j == i))
                    last.then_inc(s_pv, 1)

            def y_transpose(t):
                for half in range(2):
                    for k in range(4):
                        c0 = (4 * half + k) * P
                        last = nc.tensor.transpose(ps[:, 4 + 2 * (t % 2) + half, k * P:(k + 1) * P], z[:, t, c0:c0 + P],
                                                   eye[:, :])
                    last.then_inc(s_yt, 1)

            pe.wait_ge(s_fin, added[-1])
            pe.wait_ge(s_wo, 16)
            y_transpose(0)
            for t in range(NT):
                if t + 1 < NT:
                    y_transpose(t + 1)
                pe.wait_ge(s_yta, t + 1)
                pe.wait_ge(s_ytd, t + 1)
                if t >= 2:
                    pe.wait_ge(s_oadd, t - 1)
                for half in range(2):
                    for k in range(KT):
                        last = mm(ps[:, 2 * (t % 2) + half, :], yT[:, t % 2, k, :], wout[:, k, half * BANK:(half + 1) * BANK],
                                  start=(k == 0), stop=(k == KT - 1))
                last.then_inc(s_op, 1)


_INS = ["x", "rel_bias", "norm_g", "w_in", "b_gate_b", "kv_norm_a", "w_kv_up_a", "q_norm_a", "k_norm_a", "q_norm_b",
        "k_norm_cmp", "k_norm_slc", "k_norm_win", "cmp_pos_k", "cmp_pos_v", "w_cmp_k1", "w_cmp_k2", "w_cmp_v1",
        "w_cmp_v2", "w_out"]


def kernel(**inputs):
    import concourse.bacc as bacc
    from concourse.bass_utils import run_bass_kernel_spmd

    nc = bacc.Bacc("TRN2", target_bir_lowering=False, num_devices=1)
    arrays = {name: np.ascontiguousarray(inputs[name]) for name in _INS} | shape_constants()
    aps = {name: nc.dram_tensor(f"in_{name}", a.shape, mybir.dt.from_np(a.dtype), kind="ExternalInput").ap()
           for name, a in arrays.items()}
    out = nc.dram_tensor("out", (1, L, D), F32, kind="ExternalOutput").ap()
    hybrid_layer(nc, out=out, **aps)
    r = run_bass_kernel_spmd(nc, [{f"in_{name}": a for name, a in arrays.items()}], core_ids=[0])
    return r.results[0]["out"]
```

```python
import math
from contextlib import ExitStack

import numpy as np
import concourse.bass as bass
from concourse import mybir

F32 = mybir.dt.float32
F32R = mybir.dt.float32r
BF16 = mybir.dt.bfloat16
I32 = mybir.dt.int32
ALU = mybir.AluOpType
ACT = mybir.ActivationFunctionType
AX = mybir.AxisListType

P = 128
D = 1024
L = 1024
NT = L // P
KT = D // P
HD = 64
NH = 8
NG = 2
TOPK = 256
T_SEL = TOPK // P
SEL_TILES = range(T_SEL, NT)
N_SEL = NT - T_SEL
WIN = 512
WB = WIN // P
CMP_BLOCK, CMP_STRIDE = 32, 16
N_C = (L - CMP_BLOCK) // CMP_STRIDE + 1
N_BUCKETS, MAX_DISTANCE = 32, 1024
EPS = 1e-6
NEG = -1e30
BANK = 512
CW = 256

C_QA, C_CKV, C_QI, C_KI, C_WI, C_ZA = 0, 512, 640, 1152, 1216, 1224
C_QB, C_KC, C_KS, C_GB, C_ZB, C_END = 1736, 2248, 2504, 3016, 3040, 3552

LINE = L + P - 1
REP = 32
CM = 2 * 63
CLINE = CMP_STRIDE * CM
CY = N_C + (NT - 1) * (P // CMP_STRIDE)

SEL_W = [P * (i + 1) for i in SEL_TILES]
SEL_OFF = [sum(SEL_W[:n]) for n in range(N_SEL + 1)]
SEL_TOT = SEL_OFF[-1]
N_BITS = 31


def t5_bucket(dist):
    n = np.maximum(dist, 0)
    exact = N_BUCKETS // 2
    nf = np.maximum(n, 1).astype(np.float32)
    log_b = exact + (np.log(nf / np.float32(exact)) / np.float32(math.log(MAX_DISTANCE / exact))
                     * np.float32(N_BUCKETS - exact)).astype(np.int32)
    return np.where(n < exact, n, np.minimum(log_b, N_BUCKETS - 1))


def one_hot(dist):
    out = np.zeros((N_BUCKETS + 1, dist.size), np.float32)
    row = np.where(dist < 0, N_BUCKETS, t5_bucket(dist))
    out[row, np.arange(dist.size)] = 1.0
    return out


def shape_constants():
    v = np.arange(LINE)
    q, m = np.meshgrid(np.arange(CMP_STRIDE), np.arange(CM), indexing="ij")
    p = np.arange(P)
    eye = np.eye(P, dtype=np.float32)
    return {
        "c_line": one_hot(L - 1 - v),
        "c_cline": one_hot((q - (CMP_BLOCK - 1) + CMP_STRIDE * (63 - m)).ravel()),
        "c_eye": eye,
        "c_bits": np.tile((2.0 ** np.arange(N_BITS - 1, -1, -1, dtype=np.float32))[None], (P, 1)),
        "c_bitsi": np.tile((1 << np.arange(N_BITS - 1, -1, -1)).astype(np.int32)[None], (P, 1)),
        "c_rows": (p[:, None] + P * np.array(SEL_TILES)[None] + 2 - 2 * TOPK).astype(np.float32),
        "c_seen": (p >= CMP_BLOCK - 1).astype(np.float32)[:, None],
    }


def hybrid_layer(nc, x, rel_bias, norm_g, w_in, b_gate_b, kv_norm_a, w_kv_up_a, q_norm_a, k_norm_a, q_norm_b,
                 k_norm_cmp, k_norm_slc, k_norm_win, cmp_pos_k, cmp_pos_v, w_cmp_k1, w_cmp_k2, w_cmp_v1,
                 w_cmp_v2, w_out, c_line, c_cline, c_eye, c_bits, c_bitsi, c_rows, c_seen, out):
    ctx = ExitStack()
    with ctx:
        def sb(name, shape, dt=F32):
            return ctx.enter_context(nc.sbuf_tensor(name, shape, dt))

        def sem(name):
            return ctx.enter_context(nc.semaphore(name))

        line_dram = nc.dram_tensor("line_dram", (2 * NH, REP, LINE), F32, kind="Internal").ap()
        z_dram = nc.dram_tensor("z_dram", (NT, P, D), F32, kind="Internal").ap()
        cline_dram = nc.dram_tensor("cline_dram", (NH, CLINE), F32, kind="Internal").ap()

        def overlay(n, *names):
            views = []
            for name in names[:-1]:
                with nc.sbuf_tensor(name, [P, n], F32) as view:
                    views.append(view)
            return views + [sb(names[-1], [P, n])]

        o_ht, o_wo1 = overlay(8192, "ht_hi", "wout_1")
        hT_hi = o_ht[:, :].rearrange("p (k t) -> p k t", k=KT)
        q_st = o_ht[:, 0:2048].rearrange("p (b part h t) -> p b part h t", b=2, part=2, h=NH // NG)
        o_raw, o_parts, o_strip = overlay(8192, "w_raw", "w_parts", "strip")
        wraw, wbuf = (o[:, :].rearrange("p (b part k c) -> p b part k c", b=2, part=2, k=KT) for o in (o_raw, o_parts))
        strip = o_strip[:, :].rearrange("p (place h x) -> p place h x", place=NG, h=NH // NG)
        GROUP_AT = (1, 0)
        o_x, o_lo, o_z = overlay(8192, "x_in", "ht_lo", "z")
        x_in, z = (o[:, :].rearrange("p (t c) -> p t c", t=NT) for o in (o_x, o_z))
        hT_lo = o_lo[:, :].rearrange("p (t k c) -> p t k c", t=NT, k=KT)

        o_keys, r_qk = overlay(14336, "keys", "r_qk")
        qa = r_qk[:, 0:4096].rearrange("p (t c) -> p t c", t=NT)
        qb = r_qk[:, 6144:10240].rearrange("p (t c) -> p t c", t=NT)
        kaT, ksT, kwT = (o_keys[:, at:at + 2048].rearrange("p (g t) -> p g t", g=NG) for at in (4096, 10240, 12288))
        wout_raw = [o[:, at:at + 4096].rearrange("p (k c) -> p k c", k=KT) for o, at in ((r_qk, 6144), (o_wo1, 2048))]
        wout_lo = [o[:, at:at + 4096].rearrange("p (k c) -> p k c", k=KT) for o, at in ((o_keys, 6144), (o_ht, 2048))]
        wout_hi = [[o[:, at + 1024 * n:at + 1024 * (n + 1)].rearrange("p (k c) -> p k c", k=2) for n in range(2)]
                   for o, at in ((o_keys, 10240), (o_keys, 12288), (o_ht, 6144), (o_ht, 0))]
        wout_hi = [wout_hi[0] + wout_hi[1], wout_hi[2] + wout_hi[3]]
        ckv = r_qk[:, 0:1024].rearrange("p (t c) -> p t c", t=NT)
        ckvT = r_qk[:, 1024:2048]
        kcT_raw = r_qk[:, 6144:10240].rearrange("p (v g t) -> p v g t", v=2, g=NG)
        kiT = r_qk[:, 4096:5120]
        Q_SEL = N_SEL * P
        qiT = r_qk[:, 6144:6144 + 4 * Q_SEL].rearrange("p (m t) -> p m t", m=NH // 2)
        relu = r_qk[:, 12288:14336].rearrange("p (b c) -> p b c", b=2)
        square = [r_qk[:, 6144 + 1024 * n:7168 + 1024 * n] for n in range(2)]

        va = sb("va", [P, NT, NG * HD])
        vs = sb("vs", [P, NT, NG * HD])
        vw = sb("vw", [P, NT, NG * HD])
        x_res = [v[:, :, :].rearrange("p t c -> p (t c)") for v in (vs, vw)]

        selmask = sb("selmask", [P, SEL_TOT], BF16)
        o_yt, r_y = overlay(2 * (LINE + CLINE) + 66, "y_parts", "r_y")
        yT = o_yt[:, 0:4096].rearrange("p (b part k t) -> p b part k t", b=2, part=2, k=KT)
        oh = r_y[0:N_BUCKETS + 1, 0:LINE + CLINE]
        lines = r_y[0:2 * NH, LINE + CLINE:2 * (LINE + CLINE)]
        score = r_y[:, 0:SEL_TOT]
        tie = r_y[:, SEL_TOT:SEL_TOT + 512].bitcast(BF16)
        unsel = r_y[:, SEL_TOT + 512:SEL_TOT + 1024].bitcast(BF16)
        ties_to = r_y[:, SEL_TOT + 1024:SEL_TOT + 2048]
        mark = [tie, unsel]
        soft = r_y[:, 0:4096].rearrange("p (b c) -> p b c", b=4)
        probT = r_y[:, 4096:5632].rearrange("p (b c) -> p b c", b=3)
        q_dup = r_y[:, 5888:6400].rearrange("p (h two d) -> p h two d", h=NH // NG, two=2)

        r_nat = sb("r_nat", [P, 3 * BANK])
        nat = r_nat[:, 0:3 * CW].rearrange("p (b c) -> p b c", b=3)
        z_out = r_nat[:, 2 * BANK:3 * BANK].rearrange("p (b c) -> p b c", b=2)
        strip_c = r_nat[:, 0:NH * CY].rearrange("p (h y) -> p h y", h=NH)
        low = r_nat[:, 2 * BANK:3 * BANK].rearrange("p (b g t) -> p b g t", b=2, g=NG)
        o_acc = r_nat[:, 960:960 + CW]
        head_o = [r_y[:, 5632:5632 + CW], r_nat[:, 1280:1280 + CW]]
        eye = sb("eye", [P, P])
        eyeb = r_nat[:, 1216:1280].bitcast(BF16)
        bits = sb("bits", [P, N_BITS])
        bitsi = sb("bitsi", [P, N_BITS], I32)
        small = sb("small", [P, 12 * N_SEL])
        winb = small[:, 0:P // 2].bitcast(BF16)
        rows = small[:, 0 * N_SEL:1 * N_SEL]
        seen = sb("seen", [P, 1])
        rel = sb("rel", [N_BUCKETS + 1, 2 * NH])
        gx = sb("gx", [P, KT])
        gain = sb("gain", [P, 7])
        G_QA, G_KA, G_QB, G_KC, G_KS, G_KW, G_CKV = range(7)
        wup = r_qk[:, 2048:2304]
        w2 = r_qk[0:HD, 2304:2432].rearrange("p (v c) -> p v c", v=2)
        posT = r_qk[:, 2432:2464].rearrange("p (v j) -> p v j", v=2)
        hid = r_qk[0:HD, 2496:2752].rearrange("p (v c) -> p v c", v=2 * NG)
        kc64 = r_qk[0:HD, 2752:3008]
        kc = r_qk[0:N_C, 2752:3008].rearrange("p (g two d) -> p g two d", g=NG, two=2)
        bgate = sb("bgate", [P, 3 * NH])
        gates = sb("gates", [P, NT, 3 * NH])
        widx = sb("widx", [P, NT, NH])
        minus_half = sb("minus_half", [P, 12])
        ssx = sb("ssx", [P, NT])
        ssq = sb("ssq", [P, 3, NH])
        junk = r_nat[:, 3 * CW:3 * CW + P].bitcast(BF16).rearrange("p (b c) -> p b c", b=2)
        hid_c = sb("hid_c", [HD, 2])
        vc = sb("vc", [P, NG, 2, HD])
        kcT = sb("kcT", [P, NG, HD])
        cur = small[:, 1 * N_SEL:2 * N_SEL].bitcast(I32)
        cand = small[:, 2 * N_SEL:3 * N_SEL].bitcast(I32)
        cnt = small[:, 3 * N_SEL:4 * N_SEL]
        cnt2 = small[:, 4 * N_SEL:5 * N_SEL]
        keep = small[:, 5 * N_SEL:6 * N_SEL].bitcast(I32)
        ispos = small[:, 6 * N_SEL:7 * N_SEL]
        sgn = small[:, 7 * N_SEL:8 * N_SEL]
        kth = small[:, 8 * N_SEL:9 * N_SEL]
        nkth = small[:, 9 * N_SEL:10 * N_SEL]
        need = small[:, 10 * N_SEL:11 * N_SEL]
        thr = small[:, 11 * N_SEL:12 * N_SEL]
        nmax = sb("nmax", [P, 4, NH // NG])
        rsum = sb("rsum", [P, 4, NH // NG])
        rinv = sb("rinv", [P, 2, NH // NG])

        ps = ctx.enter_context(nc.psum_tensor("ps", [P, 8, BANK], F32))

        s_first = sem("s_first")
        s_const = sem("s_const")
        s_x = [sem(f"s_x{t}") for t in range(NT)]
        s_w = [sem(f"s_w{b}") for b in range(2)]
        s_whi = sem("s_whi")
        s_wlo = sem("s_wlo")
        s_low = sem("s_low")
        s_dup = sem("s_dup")
        s_qt = sem("s_qt")
        s_qhi = sem("s_qhi")
        s_qlo = sem("s_qlo")
        s_zout = [sem(f"s_zout{b}") for b in range(2)]
        s_zin = [sem(f"s_zin{t}") for t in range(NT)]
        s_line = sem("s_line")
        s_linesb = sem("s_linesb")
        s_lined = sem("s_lined")
        s_gp = sem("s_gp")
        s_sqx = sem("s_sqx")
        s_rx = sem("s_rx")
        s_h = sem("s_h")
        s_ht = sem("s_ht")
        s_hact = sem("s_hact")
        s_hdve = sem("s_hdve")
        s_pr = sem("s_pr")
        s_pre = sem("s_pre")
        s_sc = sem("s_sc")
        s_relu = sem("s_relu")
        s_acc = sem("s_acc")
        s_dv = sem("s_dv")
        s_mask = sem("s_mask")
        s_flip = sem("s_flip")
        s_sel = sem("s_sel")
        s_nrm = sem("s_nrm")
        s_sqo = sem("s_sqo")
        s_tr = sem("s_tr")
        s_tre = sem("s_tre")
        s_cmp = sem("s_cmp")
        s_cme = sem("s_cme")
        s_masks = sem("s_masks")
        s_zero = sem("s_zero")
        s_gate = sem("s_gate")
        s_ncst = sem("s_ncst")
        B_PIECES = [(L - P, L), (L - 4 * P, L - P), (0, L - 4 * P)]
        s_bstrip0 = sem("s_bstrip0_all")
        s_bstrip = [sem(f"s_bstrip{n}") for n in range(len(B_PIECES))]
        s_astrip = [sem(f"s_astrip{g}") for g in range(NG)]
        s_cstrip = sem("s_cstrip")
        s_qk = sem("s_qk")
        s_lg = sem("s_lg")
        s_ex = sem("s_ex")
        s_t = sem("s_t")
        s_pta = sem("s_pta")
        s_ptd = sem("s_ptd")
        s_pv = sem("s_pv")
        s_oe = sem("s_oe")
        s_fin = sem("s_fin")
        s_wo = [sem(f"s_wo{n}") for n in range(2)]
        s_ohi = sem("s_ohi")
        s_olo = sem("s_olo")
        s_xr = [sem(f"s_xr{b}") for b in range(2)]
        s_yt = sem("s_yt")
        s_yta = sem("s_yta")
        s_ytd = sem("s_ytd")
        s_op = sem("s_op")
        s_oadd = sem("s_oadd")
        s_out = [sem(f"s_out{b}") for b in range(2)]

        (CH_QI0, CH_QI1, CH_SMALL, CH_KS, CH_KW, CH_KC, CH_W1, CH_QB0, CH_QB1, CH_QA0, CH_QA1, CH_Z0, CH_Z1, CH_Z2,
         CH_Z3) = range(15)
        N_CHUNKS = 15
        w_src = w_in[0].rearrange("(k p) c -> p k c", p=P)
        JJ = CMP_BLOCK // 2
        w1_src = [w.rearrange("a (jj r) c -> r (a jj) c", r=P) for w in (w_cmp_k1, w_cmp_v1)]
        w1 = wraw[:, CH_W1 % 2, 0, :, :].rearrange("p k c -> p (k c)").rearrange("p (v j c) -> p v j c", v=2, j=JJ)
        KI_AT, SMALL_AT, SMALL_W = 0, HD, P + NH + 3 * NH
        first_col = {CH_QI0: C_QI, CH_QI1: C_QI + CW, CH_KS: C_KS, CH_KW: C_KS + CW, CH_KC: C_KC, CH_QB0: C_QB,
                     CH_QB1: C_QB + CW, CH_QA0: C_QA, CH_QA1: C_QA + CW, CH_Z0: C_ZA, CH_Z1: C_ZA + CW, CH_Z2: C_ZB,
                     CH_Z3: C_ZB + CW}
        chunk_loads = {c: [(0, col, CW)] for c, col in first_col.items()}
        chunk_loads[CH_SMALL] = [(KI_AT, C_KI, HD), (SMALL_AT, C_CKV, P), (SMALL_AT + P, C_WI, NH),
                                 (SMALL_AT + P + NH, C_GB, 3 * NH)]
        chunk_width = {c: CW for c in first_col} | {CH_SMALL: HD + SMALL_W}
        chunk_count = {c: len(v) for c, v in chunk_loads.items()} | {CH_W1: 2}
        split_chunks = [c for c in range(N_CHUNKS) if c != CH_W1]
        split_no = {c: n for n, c in enumerate(split_chunks)}

        SPLIT_PIECES = 4

        def chunk_arrived(c):
            return 16 * sum(chunk_count[n] for n in range(c % 2, c + 1, 2))

        units = []
        units += [("qiT", 2 * c + cb, half) for c in range(2) for half in range(2) for cb in range(2)]
        units += [("kiT", 0, half) for half in range(2)]
        units += [("small", t, 0) for t in range(NT)]
        N_EARLY = len(units)
        units += [("ks", t, 0) for t in range(NT)]
        units += [("kw", t, 0) for t in range(NT)]
        up = 0
        for cb, half, n in ((0, 0, 3), (0, 1, 3), (1, 0, 2), (1, 1, 0)):
            units += [("kcT", cb, half)] + [("up", t, 0) for t in range(up, up + n)]
            up += n
        for kind in ("qb0", "qb1", "qa0", "qa1", "z0", "z1", "z2", "z3"):
            units += [(kind, t, 0) for t in range(NT)]
        unit_no = {u: n for n, u in enumerate(units)}
        CHUNK_OF = {"kiT": CH_SMALL, "small": CH_SMALL, "ks": CH_KS, "kw": CH_KW, "kcT": CH_KC, "qb0": CH_QB0,
                    "qb1": CH_QB1, "qa0": CH_QA0, "qa1": CH_QA1, "z0": CH_Z0, "z1": CH_Z1, "z2": CH_Z2, "z3": CH_Z3}

        def chunk_of(u):
            if u[0] == "qiT":
                return (CH_QI0, CH_QI1)[u[1] // 2]
            return CHUNK_OF.get(u[0])

        first_unit, last_unit = {}, {}
        for n, u in enumerate(units):
            first_unit.setdefault(chunk_of(u), n)
            last_unit[chunk_of(u)] = n

        trs = [("ckvT", n) for n in range(2)] + [(kind, t) for kind in ("ks", "kw", "up") for t in range(NT)] + [("kc", 0)]
        tr_no = {u: n for n, u in enumerate(trs)}
        KEY_TRS = len(trs) - 2

        sjobs = [(i, h) for i in SEL_TILES for h in range(NH)]

        LAG, SPLIT_LEAD = 3, 1
        split_at = {first_unit[c - 1] + (last_unit[c - 1] - first_unit[c - 1]) // 2 - SPLIT_LEAD: c
                    for c in split_chunks[2:] if c != CH_QB0}
        stage_order = []
        for u in range(N_EARLY):
            stage_order.append(("unit", u))
            if u in split_at:
                stage_order.append(("split", split_at[u]))
        stage_order += [("score", n) for n in range(len(sjobs))]
        stage_order += [("tr", 0), ("tr", 1)]
        waiting, between = [], []
        for u in range(N_EARLY, len(units)):
            stage_order.append(("unit", u))
            if u in split_at:
                stage_order.append(("split", split_at[u]))
            if units[u] == ("kcT", 1, 1):
                stage_order += [("tr", m) for _, m in waiting]
                waiting = []
                trs_before_cmp = sum(what == "tr" for what, _ in stage_order)
                stage_order += [("split", CH_QB0), ("compress", 0)]
                between = [u + 1, u + 2]
                continue
            if u in between:
                if u == between[-1]:
                    stage_order.append(("compress_out", 0))
                    waiting.append((u, tr_no[("kc", 0)]))
                continue
            while waiting and waiting[0][0] <= u - LAG:
                stage_order.append(("tr", waiting.pop(0)[1]))
            if units[u][:2] in tr_no:
                waiting.append((u, tr_no[units[u][:2]]))
        stage_order += [("tr", m) for _, m in waiting]
        assert [n for what, n in stage_order if what == "tr"] == list(range(len(trs)))

        norms = []
        for what, n in stage_order:
            if what == "compress_out":
                norms.append(("kc", 0))
            elif what == "unit" and units[n][0] not in ("qiT", "kiT", "kcT", "z0", "z1", "z2", "z3"):
                norms.append(("ckv" if units[n][0] == "small" else units[n][0], units[n][1]))
        norm_no = {u: n for n, u in enumerate(norms)}

        HG = NH // NG
        jobs = []
        for i in range(NT):
            for g in range(NG):
                jobs.append(("c", i, g * HG))
                jobs += [(br, i, h) for br in "sw" for h in range(g * HG, (g + 1) * HG)]
        for g in range(NG):
            jobs += [("a", i, h) for i in range(NT) for h in range(g * HG, (g + 1) * HG)]

        def set_of(job):
            return (job[0], job[1], job[2] // HG)

        sets = list(dict.fromkeys(set_of(job) for job in jobs))
        stages = list(dict.fromkeys((job[0] == "a", job[1], job[2] // HG) for job in jobs))
        stage_of = [stages.index((job[0] == "a", job[1], job[2] // HG)) for job in jobs]
        first_job = [stage_of.index(m) for m in range(len(stages))] + [len(jobs)]
        set_no = {s: n for n, s in enumerate(sets)}
        first_windowed = jobs.index(("w", WB, 0))
        FIRST_A = jobs.index(("a", 0, 0))

        def first_block(job):
            return max(0, job[1] - WB) if job[0] == "w" else 0

        blocks = []
        for n, job in enumerate(jobs):
            if job[0] == "c":
                blocks += [(n, m, 0) for m in range(HG // 2)]
            else:
                blocks += [(n, job[2], j) for j in range(first_block(job), job[1] + 1)]
        chunks = [blocks[n:n + 4] for n in range(0, len(blocks), 4)]
        last_chunk = {}
        for k, c in enumerate(chunks):
            for b in c:
                last_chunk[b[0]] = k
        chunk_dve = [k % 5 in (1, 3) for k in range(len(chunks))]

        def pt_wait(eng, k):
            if chunk_dve[k]:
                eng.wait_ge(s_ptd, sum(chunk_dve[:k + 1]))
            else:
                eng.wait_ge(s_pta, k + 1 - sum(chunk_dve[:k + 1]))

        PV_LAG = 2
        events = [("q", 0)]
        issued = 0
        for k, c in enumerate(chunks):
            while issued < len(jobs) and issued <= c[-1][0] + 2:
                if issued and issued in first_job and stage_of[issued] + 1 < len(stages):
                    events.append(("q", stage_of[issued] + 1))
                events.append(("qk", issued))
                if issued == 1:
                    events.append(("q", 1))
                issued += 1
            events.append(("t", k))
            if k >= PV_LAG:
                events.append(("pv", k - PV_LAG))
        events += [("pv", k) for k in range(len(chunks) - PV_LAG, len(chunks))]
        N_PIECES = KT
        for p in range(N_PIECES):
            at = ("qk", FIRST_A + 24 + 4 * p) if p < N_PIECES - 2 else ("t", len(chunks) - 1)
            events.insert(events.index(at) + 1 + max(0, p - (N_PIECES - 2)), ("wout", p))
        turns = [e for e in events if e[0] in ("t", "q")]
        turn_of = {e: n for n, e in enumerate(turns)}

        def turn_wait(eng, e):
            if turn_of[e] >= 2:
                what, n = turns[turn_of[e] - 2]
                if what == "t":
                    pt_wait(eng, n)
                else:
                    eng.wait_ge(s_qlo, n + 1)

        def ends_set(n, pos):
            return pos + 1 == len(blocks) or set_of(jobs[blocks[pos + 1][0]]) != set_of(jobs[n])

        ended = [[] for _ in chunks]
        for pos, b in enumerate(blocks):
            if ends_set(b[0], pos):
                ended[pos // 4].append(set_no[set_of(jobs[b[0]])])
        added = [sum(st[0] != "c" for st in sets[:n + 1]) for n in range(len(sets))]

        line_parts = [(2 * NH, c, min(BANK, LINE - c)) for c in range(0, LINE, BANK)]
        line_parts += [(NH, LINE + c, min(BANK, CLINE - c)) for c in range(0, CLINE, BANK)]
        N_LINE = len(line_parts)

        first_loads = [(oh[:, 0:LINE], c_line), (oh[:, LINE:LINE + CLINE], c_cline), (rel[0:N_BUCKETS, :], rel_bias),
                       (eye[:, :], c_eye), (gx[:, :], norm_g.rearrange("a (k p) -> p (a k)", p=P))]
        const_loads = [(bits[:, :], c_bits), (bitsi[:, :], c_bitsi),
                       (rows[:, :], c_rows), (seen[:, :], c_seen), (wup, w_kv_up_a[0]),
                       (w2[:, 0, :], w_cmp_k2[0]), (w2[:, 1, :], w_cmp_v2[0]),
                       (gain[:, G_CKV:G_CKV + 1], kv_norm_a.rearrange("a p -> p a")),
                       (bgate[:, :], bass.AP(tensor=b_gate_b.tensor, offset=0, ap=[[0, P], [1, 3 * NH]]))]
        for half in range(2):
            rows_h = slice(half * HD, (half + 1) * HD)
            const_loads += [(gain[rows_h, col:col + 1], g.rearrange("a p -> p a")) for col, g in (
                (G_QA, q_norm_a), (G_KA, k_norm_a), (G_QB, q_norm_b), (G_KC, k_norm_cmp), (G_KS, k_norm_slc),
                (G_KW, k_norm_win))]
            const_loads += [(posT[rows_h, v, :], pos[0].rearrange("(jj two) d -> two d jj", two=2)[half])
                            for v, pos in enumerate((cmp_pos_k, cmp_pos_v))]
        N_FIRST, N_CONST = len(first_loads), len(const_loads)

        def idx_cols(half):
            t0 = T_SEL * P
            return (slice(0, BANK - t0), slice(t0, BANK)) if half == 0 else (slice(BANK - t0, Q_SEL), slice(0, BANK))

        def key_dst(m):
            kind, t = trs[m]
            if kind == "kc":
                return kcT[:, :, :]
            return {"ks": ksT, "kw": kwT, "up": kaT}[kind][:, :, t * P:(t + 1) * P]

        def queries(kind, t):
            at = int(kind[2]) * CW
            return (qb if kind[1] == "b" else qa)[:, t, at:at + CW]

        block = ctx.enter_context(nc.Block())

        @block.sync
        def _(sp):
            with nc.allow_non_contiguous_dma(reason="small vectors, once"):
                for dst, src in first_loads:
                    sp.dma_start(dst, src).then_inc(s_first, 16)

            def load_x(half):
                for t in range(4 * half, 4 * half + 4):
                    sp.dma_start(x_in[:, t, :], x[0, t * P:(t + 1) * P, :]).then_inc(s_x[t], 16)

            load_x(0)

            def load_chunk(c):
                if c - 2 == CH_W1:
                    sp.wait_ge(s_cmp, 1)
                elif c >= 2:
                    sp.wait_ge(s_pr, last_unit[c - 2] + 1)
                if c == CH_W1:
                    for v in range(2):
                        sp.dma_start(w1[:, v, :, :], w1_src[v]).then_inc(s_w[c % 2], 16)
                else:
                    for at, col, n in chunk_loads[c]:
                        sp.dma_start(wraw[:, c % 2, 0, :, at:at + n], w_src[:, :, col:col + n]).then_inc(s_w[c % 2], 16)

            def store_z(q):
                for t in range(NT):
                    sp.wait_ge(s_pre, unit_no[(f"z{q}", t, 0)] + 1)
                    sp.dma_start(z_dram[t, :, q * CW:(q + 1) * CW], z_out[:, t % 2, :])\
                      .then_inc(s_zout[t % 2], 16)

            for c in range(N_CHUNKS):
                if c >= CH_Z2:
                    store_z(c - CH_Z2)
                load_chunk(c)
                if c == 0:
                    load_x(1)
                if c == 1:
                    with nc.allow_non_contiguous_dma(reason="small vectors, once"):
                        for dst, src in const_loads:
                            sp.dma_start(dst, src).then_inc(s_const, 16)
                    sp.wait_ge(s_linesb, N_LINE)
                    sp.dma_start(line_dram, lines[:, 0:LINE].unsqueeze(1).to_broadcast([2 * NH, REP, LINE]))\
                      .then_inc(s_lined, 16)
                    sp.dma_start(cline_dram, lines[0:NH, LINE:LINE + CLINE]).then_inc(s_lined, 16)
            def load_strip(line, g, c0, c1, sem):
                for b in range(P // REP):
                    src = bass.AP(tensor=line_dram.tensor, offset=(line + g * HG) * REP * LINE + P - 1 - REP * b + c0,
                                  ap=[[LINE - 1, REP], [REP * LINE, HG], [1, c1 - c0]])
                    sp.dma_start(strip[b * REP:(b + 1) * REP, GROUP_AT[g], :, c0:c1], src).then_inc(sem, 16)

            sp.wait_ge(s_lined, 32)
            sp.wait_ge(s_tre, len(trs))
            for pb in range(P // CMP_STRIDE):
                src = bass.AP(tensor=cline_dram.tensor, offset=7 - pb, ap=[[CM, CMP_STRIDE], [CLINE, NH], [1, CY]])
                sp.dma_start(strip_c[pb * CMP_STRIDE:(pb + 1) * CMP_STRIDE, :, :], src).then_inc(s_cstrip, 16)
            store_z(2)
            sp.wait_ge(s_pr, last_unit[CH_Z2] + 1)
            load_strip(NH, 0, 0, L, s_bstrip0)
            store_z(3)
            sp.wait_ge(s_pr, len(units))
            for n, (c0, c1) in enumerate(B_PIECES):
                load_strip(NH, 1, c0, c1, s_bstrip[n])
                if n == 0:
                    for b in range(2):
                        sp.wait_ge(s_zout[b], 16 * 4 * NT // 2)
                for t in ((0,), (1, 2), range(3, NT))[n]:
                    sp.dma_start(z[:, t, :], z_dram[t]).then_inc(s_zin[t], 16)
            for g in range(NG):
                sp.wait_ge(s_lg, first_job[stages.index((False, NT - 1, g)) + 1])
                load_strip(0, g, 0, L, s_astrip[g])
            sp.wait_ge(s_qk, FIRST_A)
            for n in range(2):
                sp.dma_start(wout_raw[n], w_out[0, :, n * BANK:(n + 1) * BANK].rearrange("(k p) c -> p k c", p=P))\
                  .then_inc(s_wo[n], 16)
            sp.wait_ge(s_oe, set_no[("a", 0, 0)])
            for t in range(2):
                sp.dma_start(x_res[t], x[0, t * P:(t + 1) * P, :]).then_inc(s_xr[t], 16)
            for t in range(NT):
                sp.wait_ge(s_oadd, t + 1)
                sp.dma_start(out[0, t * P:(t + 1) * P, :], x_res[t % 2]).then_inc(s_out[t % 2], 16)
                if t + 2 < NT:
                    sp.wait_ge(s_out[t % 2], 16 * (t // 2 + 1))
                    sp.dma_start(x_res[t % 2], x[0, (t + 2) * P:(t + 3) * P, :]).then_inc(s_xr[t % 2], 16)
            for b in range(2):
                sp.wait_ge(s_out[b], 16 * NT // 2)

        @block.gpsimd
        def _(pool):
            chain = [0]

            def link(ins):
                chain[0] += 1
                ins.then_inc(s_gp, 1)
                pool.wait_ge(s_gp, chain[0])

            nc.gpsimd.memset(rel[N_BUCKETS:N_BUCKETS + 1, :], NEG).then_inc(s_ncst, 1)
            pool.wait_ge(s_ncst, 1)
            link(nc.gpsimd.memset(minus_half[:, :], -0.5))
            nc.gpsimd.memset(vc[:, :, :, :], 0.0).then_inc(s_zero, 1)
            pool.wait_ge(s_zero, 1)
            nc.gpsimd.memset(kc64, 0.0).then_inc(s_zero, 1)
            pool.wait_ge(s_zero, 2)
            for n in range(NT // 2):
                pool.wait_ge(s_sqx, 2 * (n + 1))
                part = ssx[:, 2 * n:2 * n + 2]
                link(nc.gpsimd.tensor_scalar(part, part, 1.0 / D, EPS, ALU.mult, ALU.add))
                nc.gpsimd.tensor_tensor(part, part, minus_half[:, 0:2], ALU.pow).then_inc(s_rx, 1)
                pool.wait_ge(s_rx, n + 1)

            def norm(n):
                kind, t = norms[n]
                if kind == "kc":
                    pool.wait_ge(s_cme, 4)
                else:
                    pool.wait_ge(s_pre, unit_no[("small" if kind == "ckv" else kind, t, 0)] + 1)
                if kind == "ckv":
                    ss, cols, w = ssq[:, n % 3, 0:1], ckv[:, t, :], P
                elif kind == "kc":
                    ss, cols, w = ssq[0:N_C, n % 3, 0:NG], kc, HD
                elif kind in ("ks", "kw", "up"):
                    ss, cols, w = ssq[:, n % 3, 0:NG], nat[:, n % 3, :], HD
                else:
                    ss, cols, w = ssq[:, n % 3, 0:HG], queries(kind, t), HD
                link(nc.gpsimd.tensor_scalar(ss, ss, 1.0 / w, EPS, ALU.mult, ALU.add))
                mh = minus_half[0:ss.shape[0], 0:ss.shape[1]]
                link(nc.gpsimd.tensor_tensor(ss, ss, mh, ALU.pow))
                if kind == "ckv":
                    nc.gpsimd.tensor_tensor(cols, cols, ss.to_broadcast([P, P]), ALU.mult).then_inc(s_nrm, 1)
                elif kind == "kc":
                    for two in range(2):
                        r = ss.unsqueeze(2).to_broadcast([N_C, NG, HD])
                        done = nc.gpsimd.tensor_tensor(kc[:, :, two, :], kc[:, :, two, :], r, ALU.mult)
                        if two == 0:
                            link(done)
                        else:
                            done.then_inc(s_nrm, 1)
                elif kind in ("ks", "kw", "up"):
                    v = cols.rearrange("p (g c) -> p g c", g=NG)
                    r = ss.unsqueeze(2).to_broadcast([P, NG, 2 * HD])
                    nc.gpsimd.tensor_tensor(v, v, r, ALU.mult).then_inc(s_nrm, 1)
                else:
                    v = cols.rearrange("p (h d) -> p h d", d=HD)
                    r = ss.unsqueeze(2).to_broadcast([P, CW // HD, HD])
                    nc.gpsimd.tensor_tensor(v, v, r, ALU.mult).then_inc(s_nrm, 1)
                pool.wait_ge(s_nrm, n + 1)

            def mask_diagonals(seen_value):
                pool.wait_ge(s_flip, seen_value)
                for n, i in enumerate(SEL_TILES):
                    d = score[:, SEL_OFF[n] + i * P:SEL_OFF[n] + (i + 1) * P]
                    nc.gpsimd.affine_select(out=d, in_=d, compare_op=ALU.is_ge, fill=NEG, base=0,
                                            pattern=[[-1, P]], channel_multiplier=1).then_inc(s_mask, 1)
                pool.wait_ge(s_mask, N_SEL * seen_value)

            def split(c, piece):
                if piece == 0:
                    pool.wait_ge(s_whi, split_no[c] + 1)
                w = chunk_width[c]
                k = slice(piece * KT // SPLIT_PIECES, (piece + 1) * KT // SPLIT_PIECES)
                raw, lo, hi = wraw[:, c % 2, 0, k, 0:w], wbuf[:, c % 2, 0, k, 0:w], wbuf[:, c % 2, 1, k, 0:w]
                nc.gpsimd.tensor_tensor(lo.bitcast(F32R), raw, hi, ALU.subtract).then_inc(s_wlo, 1)
                pool.wait_ge(s_wlo, SPLIT_PIECES * split_no[c] + piece + 1)

            for piece in range(SPLIT_PIECES):
                split(0, piece)
            pool.wait_ge(s_const, 16 * N_CONST)
            for n, col in enumerate((G_QA, G_QB)):
                nc.gpsimd.tensor_scalar(gain[:, col:col + 1], gain[:, col:col + 1], HD ** -0.5, None,
                                        ALU.mult).then_inc(s_ncst, 1)
                pool.wait_ge(s_ncst, n + 2)
            for piece in range(SPLIT_PIECES):
                split(1, piece)
            pieces = []
            mask_after = {("unit", unit_no["ks", 1, 0]): 1, ("unit", unit_no["ks", 4, 0]): 2}
            for what, n in stage_order:
                if what == "tr" and n >= 2:
                    m = n - 2
                    pool.wait_ge(s_tre, n + 1)
                    keys = key_dst(n)[HD:P]
                    w = keys.shape[2]
                    nc.gpsimd.tensor_tensor(keys.bitcast(F32R), low[HD:P, m % 2, :, 0:w], keys,
                                            ALU.subtract).then_inc(s_low, 1)
                    pool.wait_ge(s_low, m + 1)
                elif what == "split":
                    pieces = [(n, piece) for piece in range(SPLIT_PIECES)]
                elif what == "unit" and units[n][0] not in ("qiT", "kiT", "kcT", "z0", "z1", "z2", "z3"):
                    norm(norm_no[("ckv" if units[n][0] == "small" else units[n][0], units[n][1])])
                elif what == "compress_out":
                    norm(norm_no[("kc", 0)])
                if pieces and what in ("unit", "compress"):
                    rest = what == "compress" or n + 1 == first_unit[pieces[0][0]]
                    for _ in range(len(pieces) if rest else 2):
                        split(*pieces.pop(0))
                if (what, n) in mask_after:
                    mask_diagonals(mask_after[what, n])

            def dup(m):
                if m:
                    pool.wait_ge(s_qt, m)
                is_a, i, g = stages[m]
                q = (qa if is_a else qb)[:, i, g * CW:(g + 1) * CW].rearrange("p (h d) -> p h d", h=HG)
                nc.gpsimd.tensor_copy(q_dup[:, :, :, :], q.unsqueeze(2).to_broadcast([P, HG, 2, HD])).then_inc(s_dup, 1)
                pool.wait_ge(s_dup, m + 1)

            def add_up(s):
                br, i, g = sets[s]
                c0 = g * CW + (0 if br == "a" else BANK)
                zy = z[:, i, c0:c0 + CW]
                if br == "c":
                    return
                pool.wait_ge(s_oe, s + 1)
                if br == "s":
                    nc.gpsimd.tensor_tensor(o_acc, o_acc, head_o[s % 2], ALU.add).then_inc(s_fin, 1)
                elif br == "w":
                    link(nc.gpsimd.tensor_tensor(o_acc, o_acc, head_o[s % 2], ALU.add))
                    pool.wait_ge(s_zin[i], 16)
                    nc.gpsimd.tensor_tensor(zy, zy, o_acc, ALU.mult).then_inc(s_fin, 1)
                else:
                    nc.gpsimd.tensor_tensor(zy, zy, head_o[s % 2], ALU.mult).then_inc(s_fin, 1)
                pool.wait_ge(s_fin, added[s])

            def make_masks():
                for b in range(2):
                    pool.wait_ge(s_zout[b], 16 * 4 * NT // 2)
                nc.gpsimd.memset(eyeb[:, :], 0.0).then_inc(s_masks, 1)
                pool.wait_ge(s_masks, 1)
                nc.gpsimd.memset(winb[:, :], 0.0).then_inc(s_masks, 1)
                pool.wait_ge(s_masks, 2)
                nc.gpsimd.affine_select(out=eyeb[:, :], in_=eyeb[:, :], compare_op=ALU.not_equal, fill=1.0, base=0,
                                        pattern=[[-1, P]], channel_multiplier=1).then_inc(s_masks, 1)
                pool.wait_ge(s_masks, 3)
                nc.gpsimd.affine_select(out=winb[:, :], in_=winb[:, :], compare_op=ALU.is_gt, fill=NEG, base=0,
                                        pattern=[[1, P]], channel_multiplier=-1).then_inc(s_masks, 1)
                pool.wait_ge(s_masks, 4)

            pool.wait_ge(s_sel, 1)
            dup(0)
            for what, n in events:
                if what == "q" and n + 1 < len(stages):
                    dup(n + 1)
                    if n == 1:
                        make_masks()
                elif what == "pv":
                    for s in ended[n]:
                        add_up(s)
                elif what == "wout":
                    half, pair = divmod(n, KT // 2)
                    pool.wait_ge(s_ohi, n + 1)
                    k = slice(2 * pair, 2 * pair + 2)
                    nc.gpsimd.tensor_tensor(wout_lo[half][:, k, :].bitcast(F32R), wout_raw[half][:, k, :],
                                            wout_hi[half][pair], ALU.subtract).then_inc(s_olo, 1)
                    pool.wait_ge(s_olo, n + 1)

        @block.scalar
        def _(act):
            sqo = [0]

            def squares(src, ss, w):
                if sqo[0] >= 2:
                    act.wait_ge(s_sqo, sqo[0] - 1)
                nc.scalar.activation(junk[0:src.shape[0], sqo[0] % 2, 0:w], src, ACT.Square,
                                     accum_out=ss).then_inc(s_sqo, 1)
                sqo[0] += 1

            for t in range(NT):
                act.wait_ge(s_x[t], 16)
                if t >= 2:
                    act.wait_ge(s_sqx, t - 1)
                nc.scalar.activation(square[t % 2], x_in[:, t, :], ACT.Square,
                                     accum_out=ssx[:, t:t + 1]).then_inc(s_sqx, 1)
            act.wait_ge(s_first, 16 * N_FIRST)

            def split(c):
                act.wait_ge(s_w[c % 2], chunk_arrived(c))
                w = chunk_width[c]
                nc.scalar.activation(wbuf[:, c % 2, 1, :, 0:w].bitcast(F32R), wraw[:, c % 2, 0, :, 0:w],
                                     ACT.Copy).then_inc(s_whi, 1)

            def h_out(half):
                for k in range(KT):
                    act.wait_ge(s_ht, half * KT + k + 1)
                    nc.scalar.activation(hT_hi[:, k, half * BANK:(half + 1) * BANK].bitcast(F32R), ps[:, k, :], ACT.Copy,
                                         scale=gx[:, k:k + 1]).then_inc(s_hact, 1)

            def free_nat(n):
                if n >= 3 and norms[n - 3][0] in ("ks", "kw", "up"):
                    act.wait_ge(s_tr, tr_no[norms[n - 3]] + 1)
                elif n >= 3:
                    act.wait_ge(s_nrm, n - 2)

            def unit(u):
                kind, a, half = units[u]
                act.wait_ge(s_pr, u + 1)
                bank = ps[:, u % 4, :]
                if kind == "qiT":
                    cols, src = idx_cols(half)
                    nc.scalar.activation(qiT[:, a, cols], bank[:, src], ACT.Copy).then_inc(s_pre, 1)
                elif kind == "kiT":
                    for rows_h in (slice(0, HD), slice(HD, P)):
                        last = nc.scalar.activation(kiT[rows_h, half * BANK:(half + 1) * BANK], bank[0:HD, :], ACT.Copy)
                    last.then_inc(s_pre, 1)
                elif kind == "small":
                    n = norm_no[("ckv", a)]
                    free_nat(n)
                    squares(bank[:, 0:P], ssq[:, n % 3, 0:1], P)
                    nc.scalar.activation(ckv[:, a, :], bank[:, 0:P], ACT.Copy)
                    nc.scalar.activation(widx[:, a, :], bank[:, P:P + NH], ACT.Copy, scale=NH ** -0.5)
                    nc.scalar.activation(gates[:, a, :], bank[:, P + NH:P + NH + 3 * NH], ACT.Copy).then_inc(s_pre, 1)
                elif kind in ("ks", "kw", "up"):
                    n = norm_no[(kind, a)]
                    free_nat(n)
                    for g in range(NG):
                        squares(bank[:, g * HD:(g + 1) * HD], ssq[:, n % 3, g:g + 1], HD)
                    nc.scalar.activation(nat[:, n % 3, :].rearrange("p (g two d) -> p g two d", g=NG, two=2),
                                         bank[:, 0:P].rearrange("p (g d) -> p g d", g=NG).unsqueeze(2)
                                         .to_broadcast([P, NG, 2, HD]), ACT.Copy)
                    nc.scalar.activation({"ks": vs, "kw": vw, "up": va}[kind][:, a, :], bank[:, P:2 * P],
                                         ACT.Copy).then_inc(s_pre, 1)
                elif kind == "kcT":
                    for g in range(NG):
                        rows_g = slice(g * HD, (g + 1) * HD)
                        nc.scalar.activation(kcT_raw[0:HD, a, g, half * BANK:(half + 1) * BANK], bank[rows_g, :], ACT.Copy)
                        ahead = 1 if half == 0 else 0
                        last = nc.scalar.activation(kcT_raw[HD:P, a, g, half * BANK - 1 + ahead:(half + 1) * BANK - 1],
                                                    bank[rows_g, ahead:], ACT.Copy)
                    last.then_inc(s_pre, 1)
                elif kind[0] == "q":
                    n = norm_no[(kind, a)]
                    free_nat(n)
                    for h in range(CW // HD):
                        squares(bank[:, h * HD:(h + 1) * HD], ssq[:, n % 3, h:h + 1], HD)
                    nc.scalar.activation(queries(kind, a), bank[:, 0:CW], ACT.Copy).then_inc(s_pre, 1)
                else:
                    stores = int(kind[1]) * NT + a
                    if stores >= 2:
                        act.wait_ge(s_zout[a % 2], 16 * (stores // 2))
                    nc.scalar.activation(z_out[:, a % 2, :], bank[:, 0:CW], ACT.Silu).then_inc(s_pre, 1)

            def tr_out(m):
                kind, t = trs[m]
                act.wait_ge(s_tr, m + 1)
                bank = ps[:, 4 + m % 4, :]
                if kind == "ckvT":
                    nc.scalar.activation(ckvT[:, t * BANK:(t + 1) * BANK], bank, ACT.Copy,
                                         scale=gain[:, G_CKV:G_CKV + 1]).then_inc(s_tre, 1)
                    return
                if m == 2:
                    act.wait_ge(s_acc, len(sjobs))
                if m >= 4:
                    act.wait_ge(s_low, m - 3)
                dst = key_dst(m)
                w = dst.shape[2]
                src = bank.rearrange("p (m t) -> p m t", m=4)[:, 0:2, 0:w]
                g = {"kc": G_KC, "ks": G_KS, "kw": G_KW, "up": G_KA}[kind]
                nc.scalar.activation(low[HD:P, m % 2, :, 0:w], src[HD:P], ACT.Copy, scale=gain[HD:P, g:g + 1])
                nc.scalar.activation(dst.bitcast(F32R), src, ACT.Copy, scale=gain[:, g:g + 1]).then_inc(s_tre, 1)

            def compress_steps():
                act.wait_ge(s_cmp, 1)
                nc.scalar.activation(hid_c[:, :], ps[0:HD, 6:8, 256], ACT.Copy).then_inc(s_cme, 1)
                act.wait_ge(s_cme, 1)
                for v in range(2):
                    nc.scalar.activation(hid[:, v * NG:(v + 1) * NG, 0:N_C],
                                         ps[0:HD, 6 + v, 0:2 * N_C].rearrange("p (g c) -> p g c", g=NG),
                                         ACT.Gelu_apprx_tanh, bias=hid_c[:, v:v + 1]).then_inc(s_cme, 1)

            def compress_results():
                act.wait_ge(s_cmp, 2)
                n = norm_no[("kc", 0)]
                free_nat(n)
                src = ps[0:N_C, 6, :]
                for g in range(NG):
                    squares(src[:, g * HD:(g + 1) * HD], ssq[0:N_C, n % 3, g:g + 1], HD)
                act.wait_ge(s_zero, 2)
                for two in range(2):
                    nc.scalar.activation(kc[:, :, two, :], src[:, 0:P].rearrange("p (g d) -> p g d", g=NG), ACT.Copy)
                for two in range(2):
                    r = slice(two * HD, two * HD + N_C)
                    last = nc.scalar.activation(vc[r, :, two, :], ps[r, 6, P:2 * P].rearrange("p (g d) -> p g d", g=NG),
                                                ACT.Copy)
                last.then_inc(s_cme, 1)

            def score_relu(n):
                i, h = sjobs[n]
                act.wait_ge(s_sc, n + 1)
                if n >= 2:
                    act.wait_ge(s_acc, n - 1)
                w = P * (i + 1)
                nc.scalar.activation(relu[:, n % 2, 0:w],
                                     ps[:, 4 + 2 * (n % 2):6 + 2 * (n % 2), :].rearrange("p b c -> p (b c)")[:, 0:w],
                                     ACT.Relu, scale=HD ** -0.5).then_inc(s_relu, 1)

            h_out(0)
            split(0)
            unit(0)
            h_out(1)
            unit(1)
            split(1)
            act.wait_ge(s_const, 16 * N_CONST)
            act.wait_ge(s_ncst, 3)
            for what, n in stage_order[2:]:
                if what == "unit":
                    unit(n)
                elif what == "tr":
                    tr_out(n)
                elif what == "score":
                    score_relu(n)
                elif what == "compress":
                    compress_steps()
                elif what == "compress_out":
                    compress_results()
                elif what == "split":
                    split(n)
            act.wait_ge(s_gate, 1)
            nc.scalar.activation(gates[:, :, :], gates[:, :, :], ACT.Sigmoid).then_inc(s_gate, 1)

            for what, n in events:
                if what == "qk":
                    br, i, h = jobs[n]
                    act.wait_ge(s_lg, n + 1)
                    s = set_no[set_of(jobs[n])]
                    if br == "c":
                        v = soft[:, n % 4, 0:CW].rearrange("p (h c) -> p h c", h=HG)[:, :, 0:N_C]
                        nc.scalar.activation(v, v, ACT.Exp).then_inc(s_ex, 1)
                    else:
                        w = P * (i + 1 - first_block(jobs[n]))
                        if s >= 4 and h % HG == 0:
                            act.wait_ge(s_oe, s - 3)
                        nc.scalar.activation(soft[:, n % 4, 0:w], soft[:, n % 4, 0:w], ACT.Exp, scale=-1.0,
                                             bias=nmax[:, n % 4, 0:1],
                                             accum_out=rsum[:, s % 4, h % HG:h % HG + 1]).then_inc(s_ex, 1)
                elif what == "wout":
                    half, pair = divmod(n, KT // 2)
                    act.wait_ge(s_wo[half], 16)
                    if n == N_PIECES - 2:
                        act.wait_ge(s_qk, len(jobs))
                    nc.scalar.activation(wout_hi[half][pair].bitcast(F32R), wout_raw[half][:, 2 * pair:2 * pair + 2, :],
                                         ACT.Copy).then_inc(s_ohi, 1)
                elif what == "q":
                    act.wait_ge(s_qt, n + 1)
                    if n >= 2:
                        act.wait_ge(s_qk, first_job[n - 1])
                    g = G_QA if stages[n][0] else G_QB
                    nc.scalar.activation(q_st[:, n % 2, 0, :, :].rearrange("p h t -> p (h t)").bitcast(F32R),
                                         ps[:, 4 + turn_of[what, n] % 2, :], ACT.Copy,
                                         scale=gain[:, g:g + 1]).then_inc(s_qhi, 1)
                elif what == "t" and not chunk_dve[n]:
                    act.wait_ge(s_t, n + 1)
                    if n >= 3:
                        act.wait_ge(s_pv, n - 2)
                    nc.scalar.activation(probT[:, n % 3, :], ps[:, 4 + turn_of[what, n] % 2, :], ACT.Copy).then_inc(s_pta, 1)
            for t in range(NT):
                for half in range(2):
                    act.wait_ge(s_yt, 2 * t + half + 1)
                    if t >= 2:
                        act.wait_ge(s_op, t - 1)
                    nc.scalar.activation(yT[:, t % 2, 0, 4 * half:4 * half + 4, :].bitcast(F32R),
                                         ps[:, 4 + 2 * (t % 2) + half, :].rearrange("p (k t) -> p k t", k=4),
                                         ACT.Copy).then_inc(s_yta, 1)

        @block.vector
        def _(dve):
            chain = [0]

            def link(ins):
                chain[0] += 1
                ins.then_inc(s_dv, 1)
                dve.wait_ge(s_dv, chain[0])

            for n, (m, at, cn) in enumerate(line_parts):
                dve.wait_ge(s_line, n + 1)
                nc.vector.tensor_copy(lines[0:m, at:at + cn], ps[0:m, n, 0:cn]).then_inc(s_linesb, 1)
            for half in range(2):
                for t in range(4 * half, 4 * half + 4):
                    dve.wait_ge(s_rx, t // 2 + 1)
                    nc.vector.tensor_scalar(x_in[:, t, :], x_in[:, t, :], ssx[:, t:t + 1], None, ALU.mult).then_inc(s_h, 1)
                for k in range(KT):
                    dve.wait_ge(s_hact, half * KT + k + 1)
                    nc.vector.scalar_tensor_tensor(
                        out=hT_lo[:, 4 * half:4 * half + 4, k, :].bitcast(F32R),
                        in0=ps[:, k, :].rearrange("p (t c) -> p t c", t=4), scalar=gx[:, k:k + 1],
                        in1=hT_hi[:, k, half * BANK:(half + 1) * BANK].rearrange("p (t c) -> p t c", t=4),
                        op0=ALU.mult, op1=ALU.subtract).then_inc(s_hdve, 1)
            dve.wait_ge(s_pre, N_EARLY)
            nc.vector.tensor_tensor(gates[:, :, :], gates[:, :, :],
                                    bgate[:, :].unsqueeze(1).to_broadcast([P, NT, 3 * NH]), ALU.add).then_inc(s_gate, 1)
            dve.wait_ge(s_lined, 32)
            for n, (i, h) in enumerate(sjobs):
                o = SEL_OFF[i - T_SEL]
                w = P * (i + 1)
                y = score[:, o:o + w]
                dve.wait_ge(s_relu, n + 1)
                if h == 0:
                    nc.vector.tensor_scalar(y, relu[:, n % 2, 0:w], widx[:, i, h:h + 1], None, ALU.mult).then_inc(s_acc, 1)
                else:
                    dve.wait_ge(s_acc, n)
                    nc.vector.scalar_tensor_tensor(out=y, in0=relu[:, n % 2, 0:w], scalar=widx[:, i, h:h + 1], in1=y,
                                                   op0=ALU.mult, op1=ALU.add).then_inc(s_acc, 1)
            dve.wait_ge(s_acc, len(sjobs))
            nc.vector.memset(cur[:, :], 0).then_inc(s_flip, 1)
            dve.wait_ge(s_mask, N_SEL)

            def count(op, at, out, start=None):
                for n in range(N_SEL):
                    w = SEL_W[n]
                    if n >= 2:
                        dve.wait_ge(s_dv, chain[0] - 1)
                    chain[0] += 1
                    nc.vector.tensor_scalar(mark[n % 2][:, 0:w], score[:, SEL_OFF[n]:SEL_OFF[n] + w],
                                            0.0 if at is None else at[:, n:n + 1],
                                            None if start is None else start[:, n:n + 1],
                                            op, ALU.add, accum_out=out[:, n:n + 1]).then_inc(s_dv, 1)
                dve.wait_ge(s_dv, chain[0])

            count(ALU.is_ge, None, cnt)
            link(nc.vector.tensor_scalar(ispos[:, :], cnt[:, :], float(TOPK), None, ALU.is_ge))
            link(nc.vector.tensor_scalar(sgn[:, :], ispos[:, :], 2.0, -1.0, ALU.mult, ALU.add))
            link(nc.vector.tensor_scalar(kth[:, :], ispos[:, :], -1.0, 1.0, ALU.mult, ALU.add))
            link(nc.vector.tensor_tensor(kth[:, :], kth[:, :], rows[:, :], ALU.mult))
            link(nc.vector.tensor_scalar(kth[:, :], kth[:, :], float(TOPK), None, ALU.add))
            link(nc.vector.tensor_scalar(nkth[:, :], kth[:, :], -1.0, None, ALU.mult))
            for n in range(N_SEL):
                y = score[:, SEL_OFF[n]:SEL_OFF[n + 1]]
                last = nc.vector.tensor_scalar(y, y, sgn[:, n:n + 1], None, ALU.mult)
                if n < N_SEL - 1:
                    link(last)
            last.then_inc(s_flip, 1)
            dve.wait_ge(s_mask, 2 * N_SEL)

            high = selmask
            link(nc.vector.tensor_copy(high[:, :], score[:, :].bitcast(BF16).rearrange("p (c two) -> p c two", two=2)[:, :, 1]))
            steps = N_SEL + 3

            def search(first, count, values):
                base = chain[0]
                with dve.Fori(0, count) as bit:
                    dve.wait_ge(s_dv, steps * bit + base)
                    nc.vector.tensor_tensor(cand[:, :], cur[:, :],
                                            bitsi[:, bass.ds(bit + first, 1)].to_broadcast([P, N_SEL]),
                                            ALU.bitwise_or).then_inc(s_dv, 1)
                    dve.wait_ge(s_dv, steps * bit + base + 1)
                    for n in range(N_SEL):
                        w = SEL_W[n]
                        if n >= 2:
                            dve.wait_ge(s_dv, steps * bit + base + n)
                        nc.vector.tensor_scalar(mark[n % 2][:, 0:w], values[:, SEL_OFF[n]:SEL_OFF[n] + w],
                                                cand[:, n:n + 1].bitcast(F32), nkth[:, n:n + 1], ALU.is_ge, ALU.add,
                                                accum_out=cnt[:, n:n + 1]).then_inc(s_dv, 1)
                    dve.wait_ge(s_dv, steps * bit + base + N_SEL + 1)
                    nc.vector.tensor_scalar(keep[:, :], cnt[:, :], 0.0, bits[:, bass.ds(bit + first, 1)], ALU.is_ge,
                                            ALU.mult).then_inc(s_dv, 1)
                    dve.wait_ge(s_dv, steps * bit + base + N_SEL + 2)
                    nc.vector.tensor_tensor(cur[:, :], cur[:, :], keep[:, :], ALU.bitwise_or).then_inc(s_dv, 1)
                chain[0] += steps * count
                dve.wait_ge(s_dv, chain[0])

            search(0, N_BITS - 16, high)
            search(N_BITS - 16, 16, score)

            mag = cur[:, :].bitcast(F32)
            count(ALU.is_ge, mag, cnt)
            count(ALU.is_gt, mag, cnt2)
            link(nc.vector.tensor_tensor(cnt2[:, :], kth[:, :], cnt2[:, :], ALU.subtract))
            link(nc.vector.tensor_tensor(cnt[:, :], cnt[:, :], kth[:, :], ALU.subtract))
            link(nc.vector.tensor_scalar(cnt[:, :], cnt[:, :], 1.0, None, ALU.add))
            link(nc.vector.tensor_tensor(cnt2[:, :], cnt2[:, :], cnt[:, :], ALU.subtract))
            link(nc.vector.tensor_tensor(cnt2[:, :], cnt2[:, :], ispos[:, :], ALU.mult))
            link(nc.vector.tensor_tensor(need[:, :], cnt2[:, :], cnt[:, :], ALU.add))
            link(nc.vector.tensor_tensor(thr[:, :], mag, sgn[:, :], ALU.mult))
            for n in range(N_SEL):
                w = SEL_W[n]
                y = score[:, SEL_OFF[n]:SEL_OFF[n] + w]
                link(nc.vector.tensor_scalar(tie[:, 0:w], y, mag[:, n:n + 1], None, ALU.is_equal))
                link(nc.vector.tensor_tensor_scan(ties_to[:, 0:w], tie[:, 0:w], tie[:, 0:w], 0.0, ALU.add, ALU.max))
                link(nc.vector.scalar_tensor_tensor(out=tie[:, 0:w], in0=ties_to[:, 0:w], scalar=need[:, n:n + 1],
                                                    in1=tie[:, 0:w], op0=ALU.is_gt, op1=ALU.is_ge))
                link(nc.vector.tensor_scalar(unsel[:, 0:w], y, sgn[:, n:n + 1], thr[:, n:n + 1], ALU.mult, ALU.is_le))
                link(nc.vector.scalar_tensor_tensor(out=selmask[:, SEL_OFF[n]:SEL_OFF[n] + w], in0=unsel[:, 0:w],
                                                    scalar=NEG, in1=tie[:, 0:w], op0=ALU.mult, op1=ALU.mult))
            nc.vector.tensor_copy(need[:, :], cnt[:, :]).then_inc(s_sel, 1)

            for b in range(4):
                link(nc.vector.memset(soft[:, b, 0:CW], 0.0))
            dve.wait_ge(s_gate, 2)
            link(nc.vector.tensor_scalar(gates[:, 0, :].rearrange("p (h b) -> p h b", b=3)[:, :, 0],
                                         gates[:, 0, :].rearrange("p (h b) -> p h b", b=3)[:, :, 0],
                                         seen[:, 0:1], None, ALU.mult))

            def finish(s, k):
                br, i, g = sets[s]
                r = rinv[:, s % 2, :]
                if br == "a":
                    link(nc.vector.reciprocal(r, rsum[:, s % 4, :]))
                else:
                    gate = gates[:, i, :].rearrange("p (h b) -> p h b", b=3)[:, g * HG:(g + 1) * HG, "csw".index(br)]
                    link(nc.vector.reciprocal(r, rsum[:, s % 4, :]))
                    link(nc.vector.tensor_tensor(r, r, gate, ALU.mult))
                if br == "c":
                    dst, o_ps = o_acc, ps[:, 6 + s % 2, 0:CW].rearrange("p (h d) -> p h d", h=HG)
                    if s:
                        dve.wait_ge(s_fin, added[s - 1])
                else:
                    dst = head_o[s % 2]
                    o_ps = ps[:, 6 + s % 2, :].rearrange("p (h g d) -> p h g d", h=HG, g=NG)[:, :, g, :]
                    if s >= 2 and added[s - 2]:
                        dve.wait_ge(s_fin, added[s - 2])
                dve.wait_ge(s_pv, k + 1)
                nc.vector.tensor_tensor(dst.rearrange("p (h d) -> p h d", h=HG), o_ps,
                                        r.unsqueeze(2).to_broadcast([P, HG, HD]), ALU.mult).then_inc(s_oe, 1)

            for what, n in events:
                if what == "qk":
                    br, i, h = jobs[n]
                    if n >= 3 and jobs[n - 3][0] == "c":
                        m = n - 3
                        dve.wait_ge(s_ex, m + 1)
                        lg = soft[:, m % 4, 0:CW].rearrange("p (h c) -> p h c", h=HG)[:, :, 0:N_C]
                        link(nc.vector.tensor_reduce(rsum[:, set_no[set_of(jobs[m])] % 4, 0:HG], lg, AX.X, ALU.add))
                    dve.wait_ge(s_qk, n + 1)
                    if n >= 4:
                        dve.wait_ge(s_t, last_chunk[n - 4] + 1)
                    if n == 0:
                        dve.wait_ge(s_cstrip, 16 * (P // CMP_STRIDE))
                    if n == 1:
                        dve.wait_ge(s_bstrip0, 16 * (P // REP))
                    if h == HG and br == "s":
                        for m, (c0, c1) in enumerate(B_PIECES):
                            if c1 == L - i * P:
                                dve.wait_ge(s_bstrip[m], 16 * (P // REP))
                    if br == "a" and i == 0 and h % HG == 0:
                        dve.wait_ge(s_astrip[h // HG], 16 * (P // REP))
                    slot = ps[:, 2 * (n % 2):2 * (n % 2) + 2, :].rearrange("p b c -> p (b c)")
                    if br == "c":
                        c0 = (P // CMP_STRIDE) * (NT - 1 - i)
                        lg = soft[:, n % 4, 0:CW].rearrange("p (h c) -> p h c", h=HG)[:, :, 0:N_C]
                        link(nc.vector.tensor_tensor(lg, slot[:, 0:CW].rearrange("p (h c) -> p h c", h=HG)[:, :, 0:N_C],
                                                     strip_c[:, h:h + HG, c0:c0 + N_C], ALU.add))
                        link(nc.vector.tensor_reduce(nmax[:, n % 4, 0:HG], lg, AX.X, ALU.max, negate=True))
                        nc.vector.tensor_tensor(lg, lg, nmax[:, n % 4, 0:HG].unsqueeze(2).to_broadcast([P, HG, N_C]),
                                                ALU.add).then_inc(s_lg, 1)
                    else:
                        w = P * (i + 1 - first_block(jobs[n]))
                        nc.vector.tensor_tensor_reduce(out=soft[:, n % 4, 0:w], in0=slot[:, 0:w],
                                                       in1=strip[:, GROUP_AT[h // HG], h % HG, L - w:L], scale=-1.0, scalar=3e38, op0=ALU.add,
                                                       op1=ALU.min, accum_out=nmax[:, n % 4, 0:1]).then_inc(s_lg, 1)
                elif what == "t":
                    k = n
                    if chunk_dve[k]:
                        dve.wait_ge(s_t, k + 1)
                        if k >= 3:
                            dve.wait_ge(s_pv, k - 2)
                        nc.vector.tensor_copy(probT[:, k % 3, :], ps[:, 4 + turn_of[what, k] % 2, :]).then_inc(s_ptd, 1)
                elif what == "q":
                    dve.wait_ge(s_qhi, n + 1)
                    g = G_QA if stages[n][0] else G_QB
                    nc.vector.scalar_tensor_tensor(
                        out=q_st[:, n % 2, 1, :, :].rearrange("p h t -> p (h t)").bitcast(F32R),
                        in0=ps[:, 4 + turn_of[what, n] % 2, :], scalar=gain[:, g:g + 1],
                        in1=q_st[:, n % 2, 0, :, :].rearrange("p h t -> p (h t)"), op0=ALU.mult,
                        op1=ALU.subtract).then_inc(s_qlo, 1)
                elif what == "pv":
                    for s in ended[n]:
                        finish(s, n)
            def add_x(t):
                dve.wait_ge(s_op, t + 1)
                dve.wait_ge(s_xr[t % 2], 16 * (t // 2 + 1))
                nc.vector.tensor_tensor(x_res[t % 2], ps[:, 2 * (t % 2):2 * (t % 2) + 2, :].rearrange("p b c -> p (b c)"),
                                        x_res[t % 2], ALU.add).then_inc(s_oadd, 1)

            for t in range(NT):
                for half in range(2):
                    dve.wait_ge(s_yta, 2 * t + half + 1)
                    k = slice(4 * half, 4 * half + 4)
                    nc.vector.tensor_tensor(yT[:, t % 2, 1, k, :].bitcast(F32R),
                                            ps[:, 4 + 2 * (t % 2) + half, :].rearrange("p (k t) -> p k t", k=4),
                                            yT[:, t % 2, 0, k, :], ALU.subtract).then_inc(s_ytd, 1)
                if t:
                    add_x(t - 1)
            add_x(NT - 1)

        @block.tensor
        def _(pe):
            mm = nc.tensor.matmul
            pe.wait_ge(s_first, 16 * N_FIRST)
            pe.wait_ge(s_ncst, 1)
            for n, (m, at, cn) in enumerate(line_parts):
                lhs = rel[:, :] if m == 2 * NH else rel[:, NH:2 * NH]
                mm(ps[0:m, n, 0:cn], lhs, oh[:, at:at + cn], start=True, stop=True).then_inc(s_line, 1)
            pe.wait_ge(s_linesb, N_LINE)
            def h_transpose(half):
                pe.wait_ge(s_h, 4 * (half + 1))
                for k in range(KT):
                    if half and k == 0:
                        pe.wait_ge(s_pre, 1)
                    elif half:
                        pe.wait_ge(s_hdve, k + 1)
                    for t in range(4):
                        last = nc.tensor.transpose(ps[:, k, t * P:(t + 1) * P], x_in[:, half * 4 + t, k * P:(k + 1) * P],
                                                   eye[:, :])
                    last.then_inc(s_ht, 1)

            def unit(u):
                kind, a, half = units[u]
                if u >= 4:
                    pe.wait_ge(s_pre, u - 3)
                if kind == "up":
                    if a == 0:
                        pe.wait_ge(s_tre, 2)
                    mm(ps[:, u % 4, 0:2 * P], ckvT[:, a * P:(a + 1) * P], wup[:, :], start=True, stop=True).then_inc(s_pr, 1)
                    return
                ch = chunk_of(units[u])
                if u == first_unit[ch]:
                    pe.wait_ge(s_whi, split_no[ch] + 1)
                for n, (wp, hp) in enumerate(((1, 1), (1, 0), (0, 1))):
                    if n == 1 and u == 0:
                        pe.wait_ge(s_hdve, KT)
                    if n == 2 and u == first_unit[ch]:
                        pe.wait_ge(s_wlo, SPLIT_PIECES * (split_no[ch] + 1))
                    for k in range(KT):
                        begin, end = n == 0 and k == 0, n == 2 and k == KT - 1
                        if kind in ("qiT", "kiT", "kcT"):
                            w = wbuf[:, ch % 2, wp, k, (a % 2) * P:(a % 2 + 1) * P]
                            t0 = T_SEL if kind == "qiT" and half == 0 else 4 * half
                            if hp:
                                h = hT_hi[:, k, t0 * P:(half + 1) * BANK]
                            else:
                                h = hT_lo[:, t0:4 * half + 4, k, :]
                            last = mm(ps[:, u % 4, (t0 - 4 * half) * P:], w.bitcast(F32R), h.bitcast(F32R), start=begin, stop=end)
                        else:
                            c0, cn = (SMALL_AT, SMALL_W) if kind == "small" else (0, CW)
                            h = hT_hi[:, k, a * P:(a + 1) * P] if hp else hT_lo[:, a, k, :]
                            w = wbuf[:, ch % 2, wp, k, c0:c0 + cn]
                            last = mm(ps[:, u % 4, 0:cn], h.bitcast(F32R), w.bitcast(F32R), start=begin, stop=end)
                last.then_inc(s_pr, 1)

            def score_dots(n):
                i, h = sjobs[n]
                if n == 0:
                    pe.wait_ge(s_pre, unit_no[("small", 0, 0)])
                if n >= 2:
                    pe.wait_ge(s_relu, n - 1)
                r = slice(HD * (h % 2), HD * (h % 2) + HD)
                w = P * (i + 1)
                for b in range(0, w, BANK):
                    cn = min(BANK, w - b)
                    last = mm(ps[:, 4 + 2 * (n % 2) + b // BANK, 0:cn],
                              qiT[r, h // 2, (i - T_SEL) * P:(i - T_SEL + 1) * P], kiT[r, b:b + cn], start=True, stop=True)
                last.then_inc(s_sc, 1)

            def tr(m):
                kind, t = trs[m]
                if m >= 4:
                    pe.wait_ge(s_tre, m - 3)
                if m == 0:
                    pe.wait_ge(s_relu, len(sjobs))
                if m == trs_before_cmp:
                    pe.wait_ge(s_cme, 4)
                if kind == "ckvT":
                    pe.wait_ge(s_nrm, 4 * (t + 1))
                    for n in range(4):
                        last = nc.tensor.transpose(ps[:, 4 + m % 4, n * P:(n + 1) * P], ckv[:, 4 * t + n, :], eye[:, :])
                else:
                    n = norm_no[(kind, t)]
                    pe.wait_ge(s_nrm, n + 1)
                    if kind == "kc":
                        for g in range(NG):
                            last = nc.tensor.transpose(ps[:, 4 + m % 4, g * P:g * P + HD], kc64[:, g * P:(g + 1) * P],
                                                       eye[0:HD, 0:HD])
                    else:
                        for b in range(2):
                            last = nc.tensor.transpose(ps[:, 4 + m % 4, b * P:(b + 1) * P], nat[:, n % 3, b * P:(b + 1) * P],
                                                       eye[:, :])
                last.then_inc(s_tr, 1)

            def compress():
                pe.wait_ge(s_w[CH_W1 % 2], chunk_arrived(CH_W1))
                pe.wait_ge(s_pre, unit_no[("kcT", 1, 1)] + 1)
                pe.wait_ge(s_tre, trs_before_cmp)
                for v in range(2):
                    for j in range(JJ):
                        mm(ps[0:HD, 6 + v, 256:257], w1[:, v, j, :], posT[:, v, j:j + 1], start=(j == 0),
                           stop=(j == JJ - 1))
                    for j in range(JJ):
                        t0 = 2 * j
                        last = mm(ps[0:HD, 6 + v, 0:2 * N_C], w1[:, v, j, :],
                                  kcT_raw[:, v, :, t0:t0 + CMP_STRIDE * (N_C - 1) + 1:CMP_STRIDE],
                                  start=(j == 0), stop=(j == JJ - 1))
                last.then_inc(s_cmp, 1)

            def compress_out():
                pe.wait_ge(s_cme, 3)
                for v in range(2):
                    for g in range(NG):
                        for at in (0, HD)[0:1 + v]:
                            last = mm(ps[at:at + N_C, 6, (v * NG + g) * HD:(v * NG + g + 1) * HD],
                                      hid[:, v * NG + g, 0:N_C], w2[:, v, :], start=True, stop=True)
                last.then_inc(s_cmp, 1)

            h_transpose(0)
            pe.wait_ge(s_hact, KT)
            pe.wait_ge(s_hdve, 1)
            unit(0)
            h_transpose(1)
            pe.wait_ge(s_hdve, KT + 2)
            unit(1)
            pe.wait_ge(s_hdve, 2 * KT)
            for what, n in stage_order[2:]:
                if what == "unit":
                    unit(n)
                elif what == "tr":
                    tr(n)
                elif what == "score":
                    score_dots(n)
                elif what == "compress":
                    compress()
                elif what == "compress_out":
                    compress_out()

            pe.wait_ge(s_pre, len(units))
            pe.wait_ge(s_tre, len(trs))
            pe.wait_ge(s_low, KEY_TRS)
            v_of = {"s": vs, "w": vw, "a": va}
            for what, n in events:
                if what == "qk":
                    br, i, h = jobs[n]
                    if n >= 2:
                        pe.wait_ge(s_lg, n - 1)
                    if n == FIRST_A:
                        pe.wait_ge(s_sel, 1)
                    if n == first_windowed:
                        pe.wait_ge(s_masks, 4)
                    b0 = 2 * (n % 2)
                    m = stage_of[n]
                    if n == first_job[m]:
                        pe.wait_ge(s_qlo, m + 1)
                    if br == "c":
                        for q in range(HG):
                            for part in range(2):
                                last = mm(ps[:, b0, q * HD:(q + 1) * HD], q_st[:, m % 2, part, q, :].bitcast(F32R),
                                          kcT[:, h // HG, :].bitcast(F32R), start=(part == 0), stop=(part == 1))
                        last.then_inc(s_qk, 1)
                        continue
                    kT = {"a": kaT, "s": ksT, "w": kwT}[br]
                    k0 = first_block(jobs[n]) * P
                    w = (i + 1) * P - k0
                    for b in range(0, w, BANK):
                        cn = min(BANK, w - b)
                        dst = ps[:, b0 + b // BANK, 0:cn]
                        masked = br == "a" and i >= T_SEL or br == "w" and i >= WB and b == 0
                        for part in range(2):
                            last = mm(dst, q_st[:, m % 2, part, h % HG, :].bitcast(F32R),
                                      kT[:, h // HG, k0 + b:k0 + b + cn].bitcast(F32R), start=(part == 0),
                                      stop=(part == 1 and not masked))
                        if br == "a" and i >= T_SEL:
                            o = SEL_OFF[i - T_SEL] + b
                            last = mm(dst, eyeb[:, :], selmask[:, o:o + cn], start=False, stop=True)
                        elif br == "w" and i >= WB and b == 0:
                            last = mm(dst[:, 0:P], eyeb[:, :], winb[:, :], start=False, stop=True)
                    last.then_inc(s_qk, 1)
                elif what == "t":
                    pe.wait_ge(s_ex, chunks[n][-1][0] + 1)
                    turn_wait(pe, (what, n))
                    for q, (jn, h, j) in enumerate(chunks[n]):
                        dst = ps[:, 4 + turn_of[what, n] % 2, q * P:(q + 1) * P]
                        c0 = h * P if jobs[jn][0] == "c" else (j - first_block(jobs[jn])) * P
                        last = nc.tensor.transpose(dst, soft[:, jn % 4, c0:c0 + P], eye[:, :])
                    last.then_inc(s_t, 1)
                elif what == "q":
                    pe.wait_ge(s_dup, n + 1)
                    turn_wait(pe, (what, n))
                    for q in range(HG):
                        last = nc.tensor.transpose(ps[:, 4 + turn_of[what, n] % 2, q * P:(q + 1) * P],
                                                   q_dup[:, q, :, :].rearrange("p two d -> p (two d)"), eye[:, :])
                    last.then_inc(s_qt, 1)
                elif what == "pv":
                    pt_wait(pe, n)
                    for q, (jn, h, j) in enumerate(chunks[n]):
                        br, i, _ = jobs[jn]
                        s = set_no[set_of(jobs[jn])]
                        first = j == first_block(jobs[jn])
                        if first and h % HG == 0 and s >= 2:
                            pe.wait_ge(s_oe, s - 1)
                        cols = slice(q * P, (q + 1) * P)
                        if br == "c":
                            last = mm(ps[:, 6 + s % 2, h * P:(h + 1) * P], probT[:, n % 3, cols],
                                      vc[:, jobs[jn][2] // HG, :, :].rearrange("p two d -> p (two d)"), start=True, stop=True)
                        else:
                            hc = slice((h % HG) * P, (h % HG + 1) * P)
                            last = mm(ps[:, 6 + s % 2, hc], probT[:, n % 3, cols], v_of[br][:, j, :],
                                      start=first, stop=(j == i))
                    last.then_inc(s_pv, 1)

            def y_transpose(t):
                pe.wait_ge(s_fin, added[set_no["a", t, NG - 1]])
                if t == 1:
                    pe.wait_ge(s_oe, len(sets))
                for half in range(2):
                    for k in range(4):
                        c0 = (4 * half + k) * P
                        last = nc.tensor.transpose(ps[:, 4 + 2 * (t % 2) + half, k * P:(k + 1) * P], z[:, t, c0:c0 + P],
                                                   eye[:, :])
                    last.then_inc(s_yt, 1)

            y_transpose(0)
            for t in range(NT):
                if t + 1 < NT:
                    y_transpose(t + 1)
                pe.wait_ge(s_ytd, 2 * t + 2)
                if t >= 2:
                    pe.wait_ge(s_oadd, t - 1)
                for half in range(2):
                    if t == 0:
                        pe.wait_ge(s_olo, N_PIECES // 2 * (half + 1))
                    for n, (wp, yp) in enumerate(((1, 0), (1, 1), (0, 0))):
                        for k in range(KT):
                            w = wout_hi[half][k // 2][:, k % 2, :] if wp else wout_lo[half][:, k, :]
                            last = mm(ps[:, 2 * (t % 2) + half, :], yT[:, t % 2, yp, k, :].bitcast(F32R), w.bitcast(F32R),
                                      start=(n == 0 and k == 0), stop=(n == 2 and k == KT - 1))
                last.then_inc(s_op, 1)


_INS = ["x", "rel_bias", "norm_g", "w_in", "b_gate_b", "kv_norm_a", "w_kv_up_a", "q_norm_a", "k_norm_a", "q_norm_b",
        "k_norm_cmp", "k_norm_slc", "k_norm_win", "cmp_pos_k", "cmp_pos_v", "w_cmp_k1", "w_cmp_k2", "w_cmp_v1",
        "w_cmp_v2", "w_out"]


def kernel(**inputs):
    import concourse.bacc as bacc
    from concourse.bass_utils import run_bass_kernel_spmd

    nc = bacc.Bacc("TRN2", target_bir_lowering=False, num_devices=1)
    arrays = {name: np.ascontiguousarray(inputs[name]) for name in _INS} | shape_constants()
    aps = {name: nc.dram_tensor(f"in_{name}", a.shape, mybir.dt.from_np(a.dtype), kind="ExternalInput").ap()
           for name, a in arrays.items()}
    out = nc.dram_tensor("out", (1, L, D), F32, kind="ExternalOutput").ap()
    hybrid_layer(nc, out=out, **aps)
    r = run_bass_kernel_spmd(nc, [{f"in_{name}": a for name, a in arrays.items()}], core_ids=[0])
    return r.results[0]["out"]
```
